# Optimizing a Trainium2 kernel written in Bass

```python
import jax, jax.numpy as jnp
from jax import lax
import numpy as np

D_MODEL = 1024
BATCH = 1
SEQ = 512
DEPTH = 2

CHUNK = 64
Q_BLOCK = 128
N_MIXERS = 2
N_MLA_LAYERS = (DEPTH + 1) // 2
N_GDN_LAYERS = DEPTH // 2
MLA_HEADS = D_MODEL // 128
MLA_NOPE = 128
MLA_ROPE = 64
MLA_V = 128
MLA_Q_LORA = 3 * D_MODEL // 8
MLA_KV_LORA = D_MODEL // 4
ROPE_THETA = 10000.0
GDN_HEADS = D_MODEL // 128
GDN_DK = 128
GDN_DV = 128
GDN_CONV = 4
D_FF = 4 * D_MODEL
NORM_EPS = 1e-6
MAX_POS_OFFSET = 65536

kernel_name = 'hybrid_mla_gdn_sandwich_adaln'

def rms_norm(x, g, eps=NORM_EPS):
    xf = x.astype(jnp.float32)
    y = xf * lax.rsqrt(jnp.mean(xf * xf, axis=-1, keepdims=True) + eps)
    return (y * g.astype(jnp.float32)).astype(x.dtype)

def l2_norm(x, eps=1e-6):
    xf = x.astype(jnp.float32)
    return xf * lax.rsqrt(jnp.sum(xf * xf, axis=-1, keepdims=True) + eps)

def rope_tables(positions):
    half = MLA_ROPE // 2
    inv_freq = ROPE_THETA ** (-jnp.arange(half, dtype=jnp.float32) / half)
    ang = positions.astype(jnp.float32)[..., None] * inv_freq
    return jnp.cos(ang), jnp.sin(ang)

def apply_rope(x, cos, sin):
    xf = x.astype(jnp.float32)
    x1, x2 = jnp.split(xf, 2, axis=-1)
    return jnp.concatenate([x1 * cos - x2 * sin, x2 * cos + x1 * sin], axis=-1).astype(x.dtype)

def mla_mixer(h, cos, sin, w_in, q_norm_g, kv_norm_g, w_uq, w_ukv, w_o):
    B, S, _ = h.shape
    H = MLA_HEADS
    proj = h @ w_in
    c_q, c_kv, k_rope = jnp.split(proj, [MLA_Q_LORA, MLA_Q_LORA + MLA_KV_LORA], axis=-1)
    q = (rms_norm(c_q, q_norm_g) @ w_uq).reshape(B, S, H, MLA_NOPE + MLA_ROPE)
    q_nope, q_rope = jnp.split(q, [MLA_NOPE], axis=-1)
    q_rope = apply_rope(q_rope, cos[:, :, None, :], sin[:, :, None, :])
    kv = (rms_norm(c_kv, kv_norm_g) @ w_ukv).reshape(B, S, H, MLA_NOPE + MLA_V)
    k_nope, v = jnp.split(kv, [MLA_NOPE], axis=-1)
    k_rope = apply_rope(k_rope, cos, sin)
    scale = (MLA_NOPE + MLA_ROPE) ** -0.5
    nb = S // Q_BLOCK
    qn_blocks = q_nope.reshape(B, nb, Q_BLOCK, H, MLA_NOPE).transpose(1, 0, 2, 3, 4)
    qr_blocks = q_rope.reshape(B, nb, Q_BLOCK, H, MLA_ROPE).transpose(1, 0, 2, 3, 4)
    key_chunk = jnp.arange(S) // CHUNK
    neg = jnp.finfo(jnp.float32).min

    def attend(args):
        qn, qr, blk = args
        s = (jnp.einsum('bqhd,bkhd->bhqk', qn, k_nope)
             + jnp.einsum('bqhr,bkr->bhqk', qr, k_rope)).astype(jnp.float32) * scale
        q_chunk = (blk * Q_BLOCK + jnp.arange(Q_BLOCK)) // CHUNK
        mask = key_chunk[None, :] <= q_chunk[:, None]
        p = jax.nn.softmax(jnp.where(mask, s, neg), axis=-1).astype(v.dtype)
        return jnp.einsum('bhqk,bkhd->bqhd', p, v)

    o = lax.map(attend, (qn_blocks, qr_blocks, jnp.arange(nb)))
    o = o.transpose(1, 0, 2, 3, 4).reshape(B, S, H * MLA_V)
    return o @ w_o

def causal_depthwise_conv(x, w):
    K, C = w.shape
    return lax.conv_general_dilated(x, w[:, None, :].astype(x.dtype), window_strides=(1,),
                                    padding=[(K - 1, 0)],
                                    dimension_numbers=('NWC', 'WIO', 'NWC'),
                                    feature_group_count=C)

def gated_delta_rule_chunked(q, k, v, g, beta):
    B, S, H, Dk = q.shape
    Dv = v.shape[-1]
    N = S // CHUNK

    def chunks(t):
        return t.reshape(B, N, CHUNK, H, -1).transpose(1, 0, 3, 2, 4)

    q, k, v = chunks(q), chunks(k), chunks(v)
    beta = beta.reshape(B, N, CHUNK, H).transpose(1, 0, 3, 2)
    g = jnp.cumsum(g.reshape(B, N, CHUNK, H).transpose(1, 0, 3, 2), axis=-1)
    incl = jnp.tril(jnp.ones((CHUNK, CHUNK), dtype=bool))
    strict = jnp.tril(jnp.ones((CHUNK, CHUNK), dtype=bool), k=-1)
    decay = jnp.exp(jnp.where(incl, g[..., :, None] - g[..., None, :], -jnp.inf))
    kb = k * beta[..., None]
    L = jnp.where(strict, jnp.einsum('nbhcd,nbhjd->nbhcj', kb, k) * decay, 0.0)
    A = L + jnp.eye(CHUNK, dtype=L.dtype)
    rhs = jnp.concatenate([v * beta[..., None], kb * jnp.exp(g)[..., None]], axis=-1)
    sol = lax.linalg.triangular_solve(A, rhs, left_side=True, lower=True, unit_diagonal=True)
    u, w = jnp.split(sol, [Dv], axis=-1)
    a_qk = jnp.einsum('nbhcd,nbhjd->nbhcj', q, k) * decay
    q_dec = q * jnp.exp(g)[..., None]
    g_last = g[..., -1]
    k_dec = k * jnp.exp(g_last[..., None] - g)[..., None]

    def step(state, inp):
        u_n, w_n, qd_n, aqk_n, kd_n, gl_n = inp
        v_new = u_n - jnp.einsum('bhcd,bhde->bhce', w_n, state)
        o_n = jnp.einsum('bhcd,bhde->bhce', qd_n, state) + jnp.einsum('bhcj,bhje->bhce', aqk_n, v_new)
        state = state * jnp.exp(gl_n)[..., None, None] + jnp.einsum('bhcd,bhce->bhde', kd_n, v_new)
        return state, o_n

    s0 = jnp.zeros((B, H, Dk, Dv), jnp.float32)
    _, o = lax.scan(step, s0, (u, w, q_dec, a_qk, k_dec, g_last))
    return o.transpose(1, 0, 3, 2, 4).reshape(B, S, H, Dv)

def gdn_mixer(h, w_in, conv_w, a_log, dt_bias, out_norm_g, w_o):
    B, S, _ = h.shape
    H = GDN_HEADS
    f32 = jnp.float32
    qkv_w = H * (2 * GDN_DK + GDN_DV)
    proj = h @ w_in
    qkv, b_raw, a_raw, z = jnp.split(proj, [qkv_w, qkv_w + H, qkv_w + 2 * H], axis=-1)
    qkv = jax.nn.silu(causal_depthwise_conv(qkv, conv_w))
    q, k, v = jnp.split(qkv, [H * GDN_DK, 2 * H * GDN_DK], axis=-1)
    q = l2_norm(q.reshape(B, S, H, GDN_DK)) * (GDN_DK ** -0.5)
    k = l2_norm(k.reshape(B, S, H, GDN_DK))
    v = v.reshape(B, S, H, GDN_DV).astype(f32)
    beta = jax.nn.sigmoid(b_raw.astype(f32))
    g = -jnp.exp(a_log.astype(f32)) * jax.nn.softplus(a_raw.astype(f32) + dt_bias.astype(f32))
    o = gated_delta_rule_chunked(q, k, v, g, beta)
    o = rms_norm(o, out_norm_g) * jax.nn.silu(z.astype(f32)).reshape(B, S, H, GDN_DV)
    return o.reshape(B, S, H * GDN_DV).astype(h.dtype) @ w_o

def setup_inputs(seed: int = 0) -> dict:
    key = jax.random.key(seed)
    ks = jax.random.split(key, 24)
    f32 = jnp.float32

    def dense(k, shape, fan_in, scale=1.0):
        return jax.random.normal(k, shape, f32) * (scale * fan_in ** -0.5)

    def gain(k, shape):
        return 1.0 + 0.05 * jax.random.normal(k, shape, f32)

    x = jax.random.normal(ks[0], (BATCH, SEQ, D_MODEL), f32)
    c = jax.random.normal(ks[1], (BATCH, D_MODEL), f32)
    offset = jax.random.randint(ks[2], (BATCH, 1), 0, MAX_POS_OFFSET, dtype=jnp.int32)
    positions = offset + jnp.arange(SEQ, dtype=jnp.int32)[None, :]
    ada_w = dense(ks[3], (DEPTH, D_MODEL, 6 * D_MODEL), D_MODEL, 0.5)
    ada_b = 0.02 * jax.random.normal(ks[4], (DEPTH, 6 * D_MODEL), f32)
    sandwich_g = gain(ks[5], (DEPTH, 4, D_MODEL))
    mla_w_in = dense(ks[6], (N_MLA_LAYERS, D_MODEL, MLA_Q_LORA + MLA_KV_LORA + MLA_ROPE), D_MODEL)
    mla_q_norm_g = gain(ks[7], (N_MLA_LAYERS, MLA_Q_LORA))
    mla_kv_norm_g = gain(ks[8], (N_MLA_LAYERS, MLA_KV_LORA))
    mla_w_uq = dense(ks[9], (N_MLA_LAYERS, MLA_Q_LORA, MLA_HEADS * (MLA_NOPE + MLA_ROPE)), MLA_Q_LORA)
    mla_w_ukv = dense(ks[10], (N_MLA_LAYERS, MLA_KV_LORA, MLA_HEADS * (MLA_NOPE + MLA_V)), MLA_KV_LORA)
    mla_w_o = dense(ks[11], (N_MLA_LAYERS, MLA_HEADS * MLA_V, D_MODEL), MLA_HEADS * MLA_V)
    qkv_w = GDN_HEADS * (2 * GDN_DK + GDN_DV)
    gdn_in_width = qkv_w + 2 * GDN_HEADS + GDN_HEADS * GDN_DV
    col_scale = jnp.ones((gdn_in_width,), f32).at[qkv_w + GDN_HEADS:qkv_w + 2 * GDN_HEADS].set(0.1)
    gdn_w_in = dense(ks[12], (N_GDN_LAYERS, D_MODEL, gdn_in_width), D_MODEL) * col_scale
    gdn_conv_w = dense(ks[13], (N_GDN_LAYERS, GDN_CONV, qkv_w), GDN_CONV)
    gdn_a_log = jnp.log(jax.random.uniform(ks[14], (N_GDN_LAYERS, GDN_HEADS), f32, 1.0, 16.0))
    dt = jnp.exp(jax.random.uniform(ks[15], (N_GDN_LAYERS, GDN_HEADS), f32,
                                    float(np.log(1e-3)), float(np.log(1e-1))))
    gdn_dt_bias = dt + jnp.log(-jnp.expm1(-dt))
    gdn_out_norm_g = gain(ks[16], (N_GDN_LAYERS, GDN_DV))
    gdn_w_o = dense(ks[17], (N_GDN_LAYERS, GDN_HEADS * GDN_DV, D_MODEL), GDN_HEADS * GDN_DV)
    ffn_w1 = dense(ks[18], (DEPTH, D_MODEL, D_FF), D_MODEL)
    ffn_w2 = dense(ks[19], (DEPTH, D_FF, D_MODEL), D_FF)
    return {'x': x, 'c': c, 'positions': positions, 'ada_w': ada_w, 'ada_b': ada_b,
            'sandwich_g': sandwich_g, 'mla_w_in': mla_w_in, 'mla_q_norm_g': mla_q_norm_g,
            'mla_kv_norm_g': mla_kv_norm_g, 'mla_w_uq': mla_w_uq, 'mla_w_ukv': mla_w_ukv,
            'mla_w_o': mla_w_o, 'gdn_w_in': gdn_w_in, 'gdn_conv_w': gdn_conv_w,
            'gdn_a_log': gdn_a_log, 'gdn_dt_bias': gdn_dt_bias, 'gdn_out_norm_g': gdn_out_norm_g,
            'gdn_w_o': gdn_w_o, 'ffn_w1': ffn_w1, 'ffn_w2': ffn_w2}

def reference(x, c, positions, ada_w, ada_b, sandwich_g, mla_w_in, mla_q_norm_g, mla_kv_norm_g,
              mla_w_uq, mla_w_ukv, mla_w_o, gdn_w_in, gdn_conv_w, gdn_a_log, gdn_dt_bias,
              gdn_out_norm_g, gdn_w_o, ffn_w1, ffn_w2):
    cos, sin = rope_tables(positions)
    c_act = jax.nn.silu(c)
    for i in range(DEPTH):
        mod = c_act @ ada_w[i] + ada_b[i]
        sh_m, sc_m, gt_m, sh_f, sc_f, gt_f = [m[:, None, :] for m in jnp.split(mod, 6, axis=-1)]
        h = rms_norm(x, sandwich_g[i, 0]) * (1 + sc_m) + sh_m
        j = i // N_MIXERS
        if i % N_MIXERS == 0:
            y = mla_mixer(h, cos, sin, mla_w_in[j], mla_q_norm_g[j], mla_kv_norm_g[j],
                          mla_w_uq[j], mla_w_ukv[j], mla_w_o[j])
        else:
            y = gdn_mixer(h, gdn_w_in[j], gdn_conv_w[j], gdn_a_log[j], gdn_dt_bias[j],
                          gdn_out_norm_g[j], gdn_w_o[j])
        x = x + gt_m * rms_norm(y, sandwich_g[i, 1])
        h = rms_norm(x, sandwich_g[i, 2]) * (1 + sc_f) + sh_f
        y = jnp.square(jax.nn.relu(h @ ffn_w1[i])) @ ffn_w2[i]
        x = x + gt_f * rms_norm(y, sandwich_g[i, 3])
    return x


_drawn_inputs = setup_inputs


def setup_inputs(seed=0):
    import zlib

    import numpy as np

    out = dict(_drawn_inputs(seed))
    spreads = {}
    factors = {'mla_q_norm_g': 8.0, 'mla_kv_norm_g': 3.482, 'gdn_out_norm_g': 3.971}
    for name, (base, spread) in spreads.items():
        noise = np.random.default_rng([zlib.crc32(name.encode()), seed]).standard_normal(out[name].shape)
        drawn = base * np.exp(spread * noise) if base else spread * noise
        out[name] = __import__('jax').numpy.asarray(drawn.astype(out[name].dtype))
    for name, factor in factors.items():
        out[name] = (out[name] * factor).astype(out[name].dtype)
    return out
```

```python
from contextlib import ExitStack

import numpy as np

import concourse.bass as bass
from concourse import mybir

F32 = mybir.dt.float32
F32R = mybir.dt.float32r
I32 = mybir.dt.int32
ALU = mybir.AluOpType
ACT = mybir.ActivationFunctionType
AX = mybir.AxisListType

P = 128
D = 1024
SEQ = 512
KD = D // P
TT = SEQ // P
HEADS = 8
CHUNK = 64
Q_LORA = 384
KV_LORA = 256
ROPE = 64
NOPE = 128
KQ = Q_LORA // P
KKV = KV_LORA // P
FF = 4096
CONV = 4
EPS = 1e-6
ROPE_THETA = 10000.0
QKV_W = 3 * D
LEVELS = 6
ATT_SCALE = float((NOPE + ROPE) ** -0.5)
MASKED = -1e30

V_ADAB, V_C, V_QN, V_KVN, V_ON = 0, 96, 104, 107, 109
N_V1 = 110
V_SW = N_V1
V_CONV = V_SW + 64
N_VEC = V_CONV + 96

C_ID, C_TRI, C_SAME, C_LEVEL = 0, P, 2 * P, 3 * P
C_HALF = C_LEVEL + LEVELS * P
C_FREQ, C_SIGN, C_EARLY, C_LATE = C_HALF + 2, C_HALF + 3, C_HALF + 4, C_HALF + 4 + P
N_CONST = C_LATE + P


def constants():
    out = np.zeros((P, N_CONST), np.float32)
    j, c = np.arange(P)[:, None], np.arange(P)[None, :]
    same = j // CHUNK == c // CHUNK
    out[:, C_ID:C_ID + P] = j == c
    out[:, C_TRI:C_TRI + P] = same & (j <= c)
    out[:, C_SAME:C_SAME + P] = same
    for l in range(LEVELS):
        m = 1 << l
        out[:, C_LEVEL + l * P:C_LEVEL + (l + 1) * P] = (j // (2 * m) == c // (2 * m)) & (j // m < c // m)
    out[:, C_HALF] = np.arange(P) < CHUNK
    out[:, C_HALF + 1] = np.arange(P) >= CHUNK
    half = ROPE // 2
    freq = ROPE_THETA ** (-np.arange(half) / half)
    out[:, C_FREQ] = freq[np.arange(P) % half]
    out[:, C_SIGN] = np.where(np.arange(P) % ROPE < half, -1.0, 1.0)
    out[0, C_EARLY:C_EARLY + P] = np.arange(P) < CHUNK
    out[0, C_LATE:C_LATE + P] = MASKED * (np.arange(P) >= CHUNK)
    return out


def chunk_plan():
    size = [2048] * 3 + [1152] * 4 + [2048] * 2 + [2048] * 4 + [2048] * 32 + [2048] * 20 + [2048] * 32
    tiles = [2] * 3 + [3] * 4 + [8] * 2 + [2] * 4 + [2] * 32 + [2] * 20 + [2] * 32
    parts = [1] * 2 + [3] + [4] * 4 + [1] * (len(size) - 7)
    return size, tiles, parts


def build(nc, a, out):
    size, tiles, parts = chunk_plan()
    tiles_to = [sum(tiles[:n]) for n in range(len(tiles) + 1)]
    N_IN, N_UQ, N_UKV, N_WO, N_FFN0 = 0, 3, 7, 9, 13
    N_GDN, N_GWO, N_FFN1, N_END = 45, 61, 65, 97

    root = ExitStack()
    with root:
        sems = {}

        def sem(name):
            if name not in sems:
                sems[name] = root.enter_context(nc.semaphore(name))
            return sems[name]

        def sb(stack, name, shape, dt=F32, side="left"):
            return stack.enter_context(nc.sbuf_tensor(name, shape, dt, side=side))

        bank = [root.enter_context(nc.psum_tensor(f"bank{i}", [P, 512], F32)) for i in range(8)]
        sum_bank, mod_bank = bank[6], bank[7]

        x = sb(root, "x", [P, KD, SEQ])
        y = sb(root, "y", [P, KD, SEQ])
        w_raw = [sb(root, f"w_raw{i}", [P, 2048]) for i in range(2)]
        w_hi = [sb(root, f"w_hi{i}", [P, 2048], F32R) for i in range(2)]
        w_lo = [sb(root, f"w_lo{i}", [P, 2048], F32R) for i in range(2)]
        const = sb(root, "const", [P, N_CONST])
        vec = sb(root, "vec", [P, N_VEC])
        ones = sb(root, "ones", [P, P])
        coef = sb(root, "coef", [P, 2, 6 * KD])
        sq = [sb(root, f"sq{i}", [P, SEQ]) for i in range(2)]
        root_ms = sb(root, "root_ms", [P, SEQ])
        inv_ms = sb(root, "inv_ms", [P, SEQ])
        bias_t = sb(root, "bias_t", [P, 2])
        ident = const[:, C_ID:C_ID + P]

        w_loaded = [sem("w_loaded0"), sem("w_loaded1")]
        w_hi_ready, w_lo_ready, tile_done = sem("w_hi_ready"), sem("w_lo_ready"), sem("tile_done")

        def load_weights(sp, n, src, g=0):
            if n >= 2:
                sp.wait_ge(w_lo_ready, n - 1 + 8 * g)
            at = 0
            for part in src if isinstance(src, list) else [src]:
                k, cols = part.shape[1:]
                dst = w_raw[n % 2][:, 0:size[n]].rearrange("p (k n) -> p k n", k=k)[:, :, at:at + cols]
                sp.dma_start(dst, part).then_inc(w_loaded[n % 2], 16)
                at += cols

        def round_weights(act, n, g=0):
            act.wait_ge(w_loaded[n % 2], 16 * sum(parts[n % 2:n + 1:2]) + 64 * g)
            if n >= 2:
                act.wait_ge(tile_done, tiles_to[n - 1] + 16 * g)
            act.activation(w_hi[n % 2][:, 0:size[n]], w_raw[n % 2][:, 0:size[n]], ACT.Copy).then_inc(w_hi_ready, 1)

        def rest_weights(dve, n, g=0):
            dve.wait_ge(w_hi_ready, n + 1 + 8 * g)
            dve.tensor_tensor(w_lo[n % 2][:, 0:size[n]], w_raw[n % 2][:, 0:size[n]],
                              w_hi[n % 2][:, 0:size[n]].bitcast(F32), ALU.subtract).then_inc(w_lo_ready, 1)

        def product(pe, ps, s_hi, s_lo, m_hi, m_lo, first, last):
            pe.matmul(ps, s_lo, m_hi, start=first, stop=False)
            pe.matmul(ps, s_hi, m_lo, start=False, stop=False)
            return pe.matmul(ps, s_hi, m_hi, start=False, stop=last)

        def w_views(n, k):
            return (w_hi[n % 2][:, 0:size[n]].rearrange("p (k n) -> p k n", k=k),
                    w_lo[n % 2][:, 0:size[n]].rearrange("p (k n) -> p k n", k=k))

        def rows(w, k):
            return w.rearrange("(k p) n -> p k n", p=P)

        def src_of(n):
            if n == N_UQ - 1:
                w, at = rows(a["mla_w_in"][0], KD), 256 * n
                return [w[:, :, at:at + P]] + [w[:, :, at + P:at + P + ROPE]] * 2
            if n < N_UQ:
                return rows(a["mla_w_in"][0], KD)[:, :, 256 * n:min(256 * n + 256, Q_LORA + KV_LORA + ROPE)]
            if n < N_UKV:
                w, at = rows(a["mla_w_uq"][0], KQ), 2 * (NOPE + ROPE) * (n - N_UQ)
                heads = (at, at + NOPE + ROPE)
                return [w[:, :, c:c + NOPE] for c in heads] + [w[:, :, c + NOPE:c + NOPE + ROPE] for c in heads]
            if n < N_WO:
                return rows(a["mla_w_ukv"][0], KKV)[:, :, 1024 * (n - N_UKV):1024 * (n - N_UKV + 1)]
            if n < N_FFN0:
                return rows(a["mla_w_o"][0], KD)[:, :, 256 * (n - N_WO):256 * (n - N_WO + 1)]
            if n < N_GDN:
                return ffn_src(0, (n - N_FFN0) % 8, (n - N_FFN0) // 8)
            if n < N_GWO:
                pair, kind = (n - N_GDN) // 4, (n - N_GDN) % 4
                at = 256 * pair + (D * kind if kind < 3 else QKV_W + 2 * HEADS)
                return rows(a["gdn_w_in"][0], KD)[:, :, at:at + 256]
            if n < N_FFN1:
                return rows(a["gdn_w_o"][0], KD)[:, :, 256 * (n - N_GWO):256 * (n - N_GWO + 1)]
            return ffn_src(1, (n - N_FFN1) % 8, (n - N_FFN1) // 8)

        def ffn_src(l, j, g):
            if j < 4:
                return rows(a["ffn_w1"][l], KD)[:, :, bass.ds(1024 * g + 256 * j, 256)]
            return a["ffn_w2"][l][bass.ds(1024 * g, 1024), :].rearrange("(k p) n -> p k n", p=P)[
                :, :, 256 * (j - 4):256 * (j - 3)]

        ada_stack = root.enter_context(ExitStack())
        ada_raw = [sb(ada_stack, f"ada_raw{i}", [P, KD, 256]) for i in range(2)]
        ada_acc = [sb(ada_stack, f"ada_acc{i}", [P, 256]) for i in range(2)]
        c_act = sb(ada_stack, "c_act", [P, KD])
        ada_loaded = [sem("ada_loaded0"), sem("ada_loaded1")]
        ada_step, ada_reduced, ada_done = sem("ada_step"), sem("ada_reduced"), sem("ada_done")

        def load_ada(sp, m, g=0):
            if m >= 2:
                sp.wait_ge(ada_step, KD * (m - 1) + KD * 6 * g)
            src = a["ada_w"][m // 24].rearrange("(k p) n -> p k n", p=P)[:, :, bass.ds(256 * (m % 24) + 1536 * g, 256)]
            sp.dma_start(ada_raw[m % 2][:], src).then_inc(ada_loaded[m % 2], 16)

        def ada_multiply(dve, m, g=0):
            dve.wait_ge(ada_loaded[m % 2], 16 * (m // 2 + 1) + 48 * g)
            if m >= 2:
                dve.wait_ge(ada_reduced, m - 1 + 6 * g)
            acc = ada_acc[m % 2][:]
            dve.tensor_scalar(acc, ada_raw[m % 2][:, 0], c_act[:, 0:1], None, ALU.mult).then_inc(ada_step, 1)
            for k in range(1, KD):
                dve.wait_ge(ada_step, KD * m + k + KD * 6 * g)
                dve.scalar_tensor_tensor(acc, ada_raw[m % 2][:, k], c_act[:, k:k + 1], acc,
                                         ALU.mult, ALU.add).then_inc(ada_step, 1)

        def ada_reduce(pe, m, g=0):
            pe.wait_ge(ada_step, KD * (m + 1) + KD * 6 * g)
            if m >= 1:
                pe.wait_ge(ada_done, m + 6 * g)
            for i in range(2):
                last = pe.matmul(mod_bank[:, i:i + 1], ada_acc[m % 2][:, P * i:P * i + P], ones[:, 0:1],
                                 start=True, stop=True)
            last.then_inc(ada_reduced, 1)

        def ada_finish(dve, m, g=0):
            dve.wait_ge(ada_reduced, m + 1 + 6 * g)
            at = 2 * (m % 24) + 12 * g
            dve.tensor_tensor(coef[:, m // 24, bass.ds(at, 2)], mod_bank[:, 0:2],
                              vec[:, bass.ds(V_ADAB + 48 * (m // 24) + at, 2)], ALU.add).then_inc(ada_done, 1)

        def gain(l, s):
            return vec[:, V_SW + 8 * (4 * l + s):V_SW + 8 * (4 * l + s) + 8]

        def section(l, s):
            return coef[:, l, 8 * s:8 * s + 8]

        mla_tables = root.enter_context(ExitStack())
        low_stack = ExitStack()
        cos_t = sb(mla_tables, "cos_t", [P, SEQ], side="right")
        sin_t = sb(mla_tables, "sin_t", [P, SEQ], side="right")
        with ExitStack() as st:
            v1 = sb(st, "v1", [N_V1, P])
            v2 = sb(st, "v2", [64, P])
            v3 = sb(st, "v3", [96, P])
            pos_i = sb(st, "pos_i", [P, SEQ], I32)
            ang = sb(st, "ang", [P, SEQ])
            turns = sb(st, "turns", [P, SEQ])
            wrap = sb(st, "wrap", [P, SEQ])
            x_tok = y[:].rearrange("p k t -> p (k t)").rearrange("p (t d) -> p t d", t=TT)
            const_in, vec_in, x_in, pos_in = sem("const_in"), sem("vec_in"), sem("x_in"), sem("pos_in")
            v_turned, x_turned, x_copied, vec_copied = sem("v_turned"), sem("x_turned"), sem("x_copied"), sem("vec_copied")
            ones_set, angle_step, sin_done = sem("ones_set"), sem("angle_step"), sem("sin_done")
            with nc.Block() as block:
                @block.sync
                def _(sp):
                    sp.dma_start(const[:], a["const"]).then_inc(const_in, 16)
                    for dst, src in ((v1[0:96, :], a["ada_b"].rearrange("l (k p) -> (l k) p", p=P)),
                                     (v1[96:104, :], a["c"].rearrange("b (k p) -> (b k) p", p=P)),
                                     (v1[104:107, :], a["mla_q_norm_g"].rearrange("b (k p) -> (b k) p", p=P)),
                                     (v1[107:109, :], a["mla_kv_norm_g"].rearrange("b (k p) -> (b k) p", p=P)),
                                     (v1[109:110, :], a["gdn_out_norm_g"]),
                                     (v2[:], a["sandwich_g"].rearrange("l s (k p) -> (l s k) p", p=P)),
                                     (v3[:], a["gdn_conv_w"].rearrange("b j (k p) -> (b j k) p", p=P))):
                        sp.dma_start(dst, src).then_inc(vec_in, 16)
                    sp.dma_start(x_tok, a["x"][0].rearrange("(t p) d -> p t d", p=P)).then_inc(x_in, 16)
                    sp.dma_start(pos_i[:], a["positions"].to_broadcast([P, SEQ])).then_inc(pos_in, 16)
                    load_ada(sp, 0)
                    load_ada(sp, 1)
                    load_weights(sp, 0, src_of(0))
                    load_weights(sp, 1, src_of(1))

                @block.gpsimd
                def _(pool):
                    pool.memset(ones[:], 1.0).then_inc(ones_set, 1)

                @block.tensor
                def _(pe):
                    pe.wait_ge(const_in, 16)
                    pe.wait_ge(vec_in, 7 * 16)
                    for v, n, at in ((v1, N_V1, 0), (v2, 64, V_SW), (v3, 96, V_CONV)):
                        last = pe.transpose(bank[5][:, at:at + n], v[:], ident[0:n, 0:n])
                    last.then_inc(v_turned, 1)
                    pe.wait_ge(x_in, 16)
                    for k in range(KD):
                        if k >= 4:
                            pe.wait_ge(x_copied, k - 3)
                        for t in range(TT):
                            last = pe.transpose(bank[k % 4][:, P * t:P * t + P], x_tok[:, t, P * k:P * k + P], ident)
                        last.then_inc(x_turned, 1)

                @block.scalar
                def _(act):
                    act.wait_ge(v_turned, 1)
                    act.activation(vec[:], bank[5][:, 0:N_VEC], ACT.Copy).then_inc(vec_copied, 1)
                    act.wait_ge(vec_copied, 1)
                    act.activation(c_act[:], vec[:, V_C:V_C + KD], ACT.Silu)
                    for k in range(KD):
                        act.wait_ge(x_turned, k + 1)
                        act.activation(x[:, k], bank[k % 4][:], ACT.Copy).then_inc(x_copied, 1)
                    act.wait_ge(angle_step, 12)
                    act.activation(sin_t[:], ang[:], ACT.Sin, scale=const[:, C_SIGN:C_SIGN + 1]).then_inc(sin_done, 1)
                    act.wait_ge(angle_step, 16)
                    act.activation(cos_t[:], wrap[:], ACT.Sin)

                @block.vector
                def _(dve):
                    def step(ins, n):
                        ins.then_inc(angle_step, 1)
                        dve.wait_ge(angle_step, n)
                    two_pi = 2 * np.pi
                    p1 = 6.28125
                    p2 = float(np.float32(int((two_pi - p1) * 2 ** 19) / 2 ** 19))
                    p3 = float(two_pi - p1 - p2)
                    limit = 3.1415925
                    dve.wait_ge(pos_in, 16)
                    dve.wait_ge(const_in, 16)
                    step(dve.tensor_copy(ang[:], pos_i[:]), 1)
                    step(dve.tensor_scalar(ang[:], ang[:], const[:, C_FREQ:C_FREQ + 1], None, ALU.mult), 2)
                    step(dve.tensor_scalar(turns[:], ang[:], 1 / two_pi, 12582912.0, ALU.mult, ALU.add), 3)
                    step(dve.tensor_scalar(turns[:], turns[:], -12582912.0, None, ALU.add), 4)
                    for n, part in ((5, p1), (6, p2)):
                        step(dve.scalar_tensor_tensor(ang[:], turns[:], -part, ang[:], ALU.mult, ALU.add), n)
                    step(dve.scalar_tensor_tensor(ang[:], turns[:], -p3, ang[:], ALU.mult, ALU.add), 7)
                    step(dve.tensor_scalar(wrap[:], ang[:], np.pi / 2, None, ALU.add), 8)
                    for n, r in ((9, ang), (13, wrap)):
                        step(dve.tensor_scalar(turns[:], r[:], 1 / two_pi, 12582912.0, ALU.mult, ALU.add), n)
                        step(dve.tensor_scalar(turns[:], turns[:], -12582912.0, None, ALU.add), n + 1)
                        step(dve.scalar_tensor_tensor(r[:], turns[:], -two_pi, r[:], ALU.mult, ALU.add), n + 2)
                        step(dve.tensor_scalar(r[:], r[:], limit, -limit, ALU.min, ALU.max), n + 3)

        def square_tiles(act, src, n, name, b=0):
            for k in range(n):
                if k >= 2:
                    act.wait_ge(sem(name + "_summed"), n * b + k - 1)
                act.activation(sq[k % 2][:], src[:, k], ACT.Square).then_inc(sem(name + "_squared"), 1)

        def sum_tiles(pe, n, name, b=0):
            for k in range(n):
                pe.wait_ge(sem(name + "_squared"), n * b + k + 1)
                pe.matmul(sum_bank[:], ones[:], sq[k % 2][:], start=k == 0, stop=k == n - 1).then_inc(sem(name + "_summed"), 1)

        def root_of_mean(act, n, name, scale, b=0):
            act.wait_ge(sem(name + "_summed"), n * (b + 1))
            act.activation(root_ms[:], sum_bank[:], ACT.Sqrt, bias=bias_t[:, 0:1], scale=scale).then_inc(sem(name + "_root"), 1)

        def inverse_of_root(dve, name, b=0):
            dve.wait_ge(sem(name + "_root"), b + 1)
            dve.reciprocal(inv_ms[:], root_ms[:]).then_inc(sem(name + "_inv"), 1)
            dve.wait_ge(sem(name + "_inv"), b + 1)

        xr_ready, hf_ready, h_hi_ready, h_lo_ready = sem("xr_ready"), sem("hf_ready"), sem("h_hi_ready"), sem("h_lo_ready")

        def scale_h(dve, b, hf, xr, h_hi, h_lo):
            for k in range(KD):
                if k >= 2:
                    dve.wait_ge(hf_ready, KD * b + k - 1)
                dve.tensor_tensor(xr[k % 2][:], x[:, k], inv_ms[:], ALU.mult).then_inc(xr_ready, 1)
                if k >= 1:
                    rest_h(dve, b, k - 1, hf, h_hi, h_lo)
            rest_h(dve, b, KD - 1, hf, h_hi, h_lo)

        def rest_h(dve, b, k, hf, h_hi, h_lo):
            dve.wait_ge(h_hi_ready, KD * b + k + 1)
            dve.tensor_tensor(h_lo[:, k], hf[k % 2][:], h_hi[:, k].bitcast(F32), ALU.subtract).then_inc(h_lo_ready, 1)

        def modulate_h(act, b, l, s, hf, xr, h_hi):
            fac, shift = section(l, s + 1), section(l, s)
            for k in range(KD):
                act.wait_ge(xr_ready, KD * b + k + 1)
                if k >= 2:
                    act.wait_ge(h_lo_ready, KD * b + k - 1)
                act.activation(hf[k % 2][:], xr[k % 2][:], ACT.Identity, bias=shift[:, k:k + 1],
                               scale=fac[:, k:k + 1]).then_inc(hf_ready, 1)
                act.wait_ge(hf_ready, KD * b + k + 1)
                act.activation(h_hi[:, k], hf[k % 2][:], ACT.Copy).then_inc(h_hi_ready, 1)

        yr_ready, x_new, factors_ready = sem("yr_ready"), sem("x_new"), sem("factors_ready")

        def boundary(b, gate, nxt, h_hi, h_lo):
            with ExitStack() as st, nc.Block() as block:
                hf = [sb(st, f"hf{i}_{b}", [P, SEQ]) for i in range(2)]
                xr = [sb(st, f"xr{i}_{b}", [P, SEQ]) for i in range(2)]
                l, s = gate
                g_fac = section(l, s)

                @block.tensor
                def _(pe):
                    sum_tiles(pe, KD, "edge_y", b)
                    if nxt:
                        pe.wait_ge(sem("edge_y_root"), b + 1)
                        sum_tiles(pe, KD, "edge_x", b)

                @block.scalar
                def _(act):
                    square_tiles(act, y, KD, "edge_y", b)
                    root_of_mean(act, KD, "edge_y", 1 / D, b)
                    if nxt:
                        for k in range(KD):
                            act.wait_ge(x_new, KD * b + k + 1)
                            if k >= 2:
                                act.wait_ge(sem("edge_x_summed"), KD * b + k - 1)
                            act.activation(sq[k % 2][:], x[:, k], ACT.Square).then_inc(sem("edge_x_squared"), 1)
                        root_of_mean(act, KD, "edge_x", 1 / D, b)
                        modulate_h(act, b + 1, *nxt, hf, xr, h_hi)

                @block.vector
                def _(dve):
                    dve.tensor_tensor(g_fac, g_fac, gain(l, 1 if s == 2 else 3), ALU.mult).then_inc(factors_ready, 1)
                    if nxt:
                        nl, ns = nxt
                        dve.scalar_tensor_tensor(section(nl, ns + 1), section(nl, ns + 1), 1.0,
                                                 gain(nl, 0 if ns == 0 else 2), ALU.add, ALU.mult).then_inc(factors_ready, 1)
                    dve.wait_ge(factors_ready, 1 + 2 * b + (2 if nxt else 1))
                    inverse_of_root(dve, "edge_y", b)
                    for k in range(KD):
                        if k >= 2:
                            dve.wait_ge(x_new, KD * b + k - 1)
                        dve.tensor_tensor(xr[k % 2][:], y[:, k], inv_ms[:], ALU.mult).then_inc(yr_ready, 1)
                        dve.wait_ge(yr_ready, KD * b + k + 1)
                        dve.scalar_tensor_tensor(x[:, k], xr[k % 2][:], g_fac[:, k:k + 1], x[:, k],
                                                 ALU.mult, ALU.add).then_inc(x_new, 1)
                    dve.wait_ge(x_new, KD * (b + 1))
                    if nxt:
                        inverse_of_root(dve, "edge_x", b)
                        scale_h(dve, b + 1, hf, xr, h_hi, h_lo)

        mla_keep = ExitStack()
        v_tok = sb(mla_keep, "v_tok", [P, TT, HEADS * P])
        k_rope = sb(mla_keep, "k_rope", [P, SEQ])
        low_hi = sb(low_stack, "low_hi", [P, KQ + KKV, SEQ], F32R, side="right")
        low_lo = sb(low_stack, "low_lo", [P, KQ + KKV, SEQ], F32R, side="right")
        rope_t = [sb(low_stack, f"rope_t{i}", [P, SEQ], side="right") for i in range(2)]
        h_stack = ExitStack()
        h_hi = sb(h_stack, "h_hi_mla", [P, KD, SEQ], F32R)
        h_lo = sb(h_stack, "h_lo_mla", [P, KD, SEQ], F32R)
        with ExitStack() as st, nc.Block() as block:
            hf = [y[:, i] for i in range(2)]
            xr = [y[:, 2 + i] for i in range(2)]

            @block.sync
            def _(sp):
                for m in range(8):
                    load_ada(sp, m + 2)

            @block.tensor
            def _(pe):
                sum_tiles(pe, KD, "first_x")
                for m in range(8):
                    ada_reduce(pe, m)

            @block.scalar
            def _(act):
                act.wait_ge(sem("eps_set"), 2)
                square_tiles(act, x, KD, "first_x")
                root_of_mean(act, KD, "first_x", 1 / D)
                round_weights(act, 0)
                act.wait_ge(factors_ready, 1)
                modulate_h(act, 0, 0, 0, hf, xr, h_hi)

            @block.vector
            def _(dve):
                dve.memset(bias_t[:, 0:1], EPS).then_inc(sem("eps_set"), 1)
                dve.memset(bias_t[:, 1:2], P * EPS).then_inc(sem("eps_set"), 1)
                inverse_of_root(dve, "first_x")
                for m in range(8):
                    ada_multiply(dve, m)
                    if m >= 1:
                        ada_finish(dve, m - 1)
                ada_finish(dve, 7)
                rest_weights(dve, 0)
                dve.wait_ge(ada_done, 8)
                dve.scalar_tensor_tensor(section(0, 1), section(0, 1), 1.0, gain(0, 0), ALU.add,
                                         ALU.mult).then_inc(factors_ready, 1)
                scale_h(dve, 0, hf, xr, h_hi, h_lo)

        low_f = ExitStack()
        low = sb(low_f, "low", [P, KQ + KKV, SEQ])
        low_copied, krope_step = sem("low_copied"), sem("krope_step")

        def rope_dve(dve, ps, dst, base, first_wait, done):
            t0, t1 = rope_t[0][:], rope_t[1][:]
            for b in range(4):
                lo, hi = 32 * b, 32 * (b ^ 1)
                dve.tensor_copy(t1[lo:lo + 32, :], ps[hi:hi + 32, :]).then_inc(done, 1)
            dve.tensor_tensor(t0, ps, cos_t[:], ALU.mult).then_inc(done, 1)
            dve.wait_ge(done, base + 5)
            dve.tensor_tensor(t1, t1, sin_t[:], ALU.mult).then_inc(done, 1)
            dve.wait_ge(done, base + 6)
            dve.tensor_tensor(dst, t0, t1, ALU.add).then_inc(done, 1)
            dve.wait_ge(done, base + 7)

        with nc.Block() as block:
            @block.sync
            def _(sp):
                for n in range(N_IN, N_UQ):
                    load_weights(sp, n + 2, src_of(n + 2))
                    load_ada(sp, n + 10)

            @block.tensor
            def _(pe):
                for n in range(N_IN, N_UQ):
                    pe.wait_ge(w_lo_ready, n + 1)
                    hi, lo = w_views(n, KD)
                    for i in range(2):
                        t = 2 * n + i
                        cols = [v[:, :, P * i:P * i + P] for v in (hi, lo)]
                        if t >= 4:
                            pe.wait_ge(low_copied, t - 3)
                        for k in range(KD):
                            last = product(pe, bank[t % 4][:], cols[0][:, k], cols[1][:, k], h_hi[:, k], h_lo[:, k],
                                           k == 0, k == KD - 1)
                        last.then_inc(tile_done, 1)
                    ada_reduce(pe, n + 8)
                for name, n in (("cq", KQ), ("ckv", KKV)):
                    if name == "ckv":
                        pe.wait_ge(sem("cq_root"), 1)
                    sum_tiles(pe, n, name)

            @block.scalar
            def _(act):
                for n in range(N_IN, N_UQ):
                    round_weights(act, n + 1)
                    for t in range(2 * n, min(2 * n + 2, KQ + KKV)):
                        act.wait_ge(tile_done, t + 1)
                        act.activation(low[:, t], bank[t % 4][:], ACT.Copy).then_inc(low_copied, 1)
                act.wait_ge(low_copied, KQ + KKV)
                square_tiles(act, low[:, 0:KQ], KQ, "cq")
                root_of_mean(act, KQ, "cq", 1 / Q_LORA)
                for k in range(KKV):
                    act.wait_ge(sem("cq_summed"), KQ)
                    act.activation(sq[k % 2][:], low[:, KQ + k], ACT.Square).then_inc(sem("ckv_squared"), 1)
                act.wait_ge(sem("cq_inv"), 1)
                root_of_mean(act, KKV, "ckv", 1 / KV_LORA)
                for k in range(KQ + KKV):
                    act.wait_ge(sem("low_scaled"), k + 1)
                    act.activation(low_hi[:, k], low[:, k], ACT.Copy).then_inc(sem("low_hi_ready"), 1)

            @block.vector
            def _(dve):
                for n in range(N_IN, N_UQ):
                    rest_weights(dve, n + 1)
                    ada_multiply(dve, n + 8)
                    ada_finish(dve, n + 8)
                dve.wait_ge(tile_done, 6)
                rope_dve(dve, bank[1][:], k_rope[:], 0, None, krope_step)
                for name, at, n in (("cq", 0, KQ), ("ckv", KQ, KKV)):
                    if at:
                        dve.wait_ge(sem("low_scaled"), at)
                    inverse_of_root(dve, name)
                    for k in range(at, at + n):
                        g = vec[:, V_QN + k:V_QN + k + 1]
                        dve.scalar_tensor_tensor(low[:, k], low[:, k], g, inv_ms[:], ALU.mult,
                                                 ALU.mult).then_inc(sem("low_scaled"), 1)
                for k in range(KQ + KKV):
                    dve.wait_ge(sem("low_hi_ready"), k + 1)
                    dve.tensor_tensor(low_lo[:, k], low[:, k], low_hi[:, k].bitcast(F32), ALU.subtract)
        low_f.close()
        h_stack.close()

        q_stack = ExitStack()
        q_nope = sb(q_stack, "q_nope", [P, HEADS, SEQ])
        q_rope = sb(q_stack, "q_rope", [P, HEADS // 2, SEQ])
        k_nope = y
        up_copied, qrope_step = sem("up_copied"), sem("qrope_step")
        UP0 = 6
        with nc.Block() as block:
            def copies_before(n, i):
                return 2 * (n - N_UQ) + i if n < N_UKV else 8 + 8 * (n - N_UKV) + i

            def up_bank(n, i):
                return bank[4 + (n - N_UQ) % 2] if n < N_UKV and i == 2 else bank[copies_before(n, i) % 4]

            @block.sync
            def _(sp):
                for n in range(N_UQ, N_WO):
                    load_weights(sp, n + 2, src_of(n + 2))
                    load_ada(sp, n + 10)

            @block.tensor
            def _(pe):
                for n in range(N_UQ, N_WO):
                    pe.wait_ge(w_lo_ready, n + 1)
                    if n < N_UKV:
                        hi, lo = w_views(n, KQ)
                        for i in range(3):
                            if i < 2:
                                if copies_before(n, i) >= 4:
                                    pe.wait_ge(up_copied, copies_before(n, i) - 3)
                            else:
                                if n - N_UQ >= 2:
                                    pe.wait_ge(qrope_step, 7 * (n - N_UQ - 1))
                            cols = [v[:, :, P * i:P * i + P] for v in (hi, lo)]
                            for k in range(KQ):
                                last = product(pe, up_bank(n, i)[:], cols[0][:, k], cols[1][:, k], low_hi[:, k],
                                               low_lo[:, k], k == 0, k == KQ - 1)
                            last.then_inc(tile_done, 1)
                    else:
                        hi, lo = (v.rearrange("p k (h c) -> p k h c", h=4) for v in w_views(n, KKV))
                        for i in range(8):
                            pe.wait_ge(up_copied, copies_before(n, i) - 3)
                            for k in range(KKV):
                                ps = up_bank(n, i)[:]
                                kv = KQ + k
                                if i < 4:
                                    last = product(pe, ps, hi[:, k, i, 0:NOPE], lo[:, k, i, 0:NOPE], low_hi[:, kv],
                                                   low_lo[:, kv], k == 0, k == KKV - 1)
                                else:
                                    tok = slice(P * (i - 4), P * (i - 3))
                                    last = product(pe, ps, low_hi[:, kv, tok], low_lo[:, kv, tok], hi[:, k, :, NOPE:],
                                                   lo[:, k, :, NOPE:], k == 0, k == KKV - 1)
                            last.then_inc(tile_done, 1)
                    ada_reduce(pe, n + 8)

            @block.scalar
            def _(act):
                for n in range(N_UQ, N_WO):
                    round_weights(act, n + 1)
                    for i in range(2 if n < N_UKV else 8):
                        act.wait_ge(tile_done, tiles_to[n] + i + 1)
                        if n < N_UKV:
                            dst = q_nope[:, 2 * (n - N_UQ) + i]
                        elif i < 4:
                            dst = k_nope[:, 4 * (n - N_UKV) + i]
                        else:
                            dst = v_tok[:, i - 4, 512 * (n - N_UKV):512 * (n - N_UKV + 1)]
                        act.activation(dst, up_bank(n, i)[:], ACT.Copy).then_inc(up_copied, 1)

            @block.vector
            def _(dve):
                for n in range(N_UQ, N_WO):
                    rest_weights(dve, n + 1)
                    ada_multiply(dve, n + 8)
                    if n < N_UKV:
                        dve.wait_ge(tile_done, tiles_to[n] + 3)
                        rope_dve(dve, up_bank(n, 2)[:], q_rope[:, n - N_UQ], 7 * (n - N_UQ), None, qrope_step)
                    ada_finish(dve, n + 8)
        low_stack.close()
        mla_tables.close()

        o_stack = ExitStack()
        o_hi = sb(o_stack, "o_hi_mla", [P, HEADS, SEQ], F32R, side="right")
        o_lo = sb(o_stack, "o_lo_mla", [P, HEADS, SEQ], F32R, side="right")
        with ExitStack() as st, nc.Block() as block:
            prob = [sb(st, f"prob{i}", [P, SEQ]) for i in range(2)]
            prob_t = [sb(st, f"prob_t{i}", [P, TT, SEQ]) for i in range(1)]
            stat = [sb(st, f"stat{i}", [P, 4]) for i in range(2)]
            scores_ready, peak, bias_ready, exp_done = sem("scores_ready"), sem("peak"), sem("bias_ready"), sem("exp_done")
            inv_ready, prob_ready, turned, turned_copied = sem("inv_ready"), sem("prob_ready"), sem("turned"), sem("turned_copied")
            o_ready, o_rounded, o_rest = sem("o_ready"), sem("o_rounded"), sem("o_rest")
            items = [(h, b) for h in range(HEADS) for b in range(TT)]

            @block.tensor
            def _(pe):
                def scores(i):
                    h, b = items[i]
                    if i >= 2:
                        pe.wait_ge(exp_done, i - 1)
                    ps, keys, qs = bank[i % 2][:, 0:P * (b + 1)], slice(0, P * (b + 1)), slice(P * b, P * b + P)
                    r = 64 * (h % 2)
                    pe.matmul(ps, q_nope[:, h, qs], k_nope[:, h, keys], start=True, stop=False)
                    pe.matmul(ps, q_rope[r:r + 64, h // 2, qs], k_rope[r:r + 64, keys], start=False, stop=True)
                    pe.matmul(bank[i % 2][:, P * b:P * b + P], const[0:1, C_EARLY:C_EARLY + P],
                              const[0:1, C_LATE:C_LATE + P], start=False, stop=True,
                              skip_group_check=True).then_inc(scores_ready, 1)

                def turn(i):
                    h, b = items[i]
                    pe.wait_ge(prob_ready, i + 1)
                    if i >= 2:
                        pe.wait_ge(turned_copied, i - 1)
                    for j in range(b + 1):
                        last = pe.transpose(bank[2 + i % 2][:, P * j:P * j + P], prob[i % 2][:, P * j:P * j + P], ident)
                    last.then_inc(turned, 1)

                def values(h):
                    pe.wait_ge(turned_copied, TT * (h + 1))
                    if h >= 2:
                        pe.wait_ge(o_rest, h - 1)
                    for j in range(TT):
                        last = pe.matmul(bank[4 + h % 2][:, P * j:SEQ], v_tok[:, j, P * h:P * h + P],
                                         prob_t[0][:, j, P * j:SEQ], start=j == 0, stop=j == TT - 1,
                                         skip_group_check=True)
                    last.then_inc(o_ready, 1)

                scores(0)
                for i in range(len(items)):
                    if i + 1 < len(items):
                        scores(i + 1)
                    turn(i)
                    if i % TT == TT - 1:
                        values(i // TT)

            def finish_row(dve, i):
                h, b = items[i]
                s = stat[i % 2]
                dve.wait_ge(exp_done, i + 1)
                dve.reciprocal(s[:, 3:4], s[:, 2:3]).then_inc(inv_ready, 1)
                dve.wait_ge(inv_ready, i + 1)
                dve.tensor_scalar(prob[i % 2][:, 0:P * (b + 1)], prob[i % 2][:, 0:P * (b + 1)], s[:, 3:4], None,
                                  ALU.mult).then_inc(prob_ready, 1)
                dve.wait_ge(turned, i + 1)
                if b == 0 and h >= 1:
                    dve.wait_ge(o_ready, h)
                dve.tensor_copy(prob_t[0][:, 0:b + 1, P * b:P * b + P],
                                bank[2 + i % 2][:, 0:P * (b + 1)].rearrange("p (j q) -> p j q", q=P)).then_inc(turned_copied, 1)

            def rest_of_head(dve, h):
                dve.wait_ge(o_rounded, h + 1)
                dve.tensor_tensor(o_lo[:, h], bank[4 + h % 2][:], o_hi[:, h].bitcast(F32), ALU.subtract).then_inc(o_rest, 1)

            @block.vector
            def _(dve):
                for i, (h, b) in enumerate(items):
                    s = stat[i % 2]
                    dve.wait_ge(scores_ready, i + 1)
                    dve.reduce_max(s[:, 0:1], bank[i % 2][:, 0:P * (b + 1)], AX.X).then_inc(peak, 1)
                    dve.wait_ge(peak, i + 1)
                    dve.tensor_scalar(s[:, 1:2], s[:, 0:1], -ATT_SCALE, None, ALU.mult).then_inc(bias_ready, 1)
                    if i >= 1:
                        finish_row(dve, i - 1)
                    if i > TT and i % TT == 2:
                        rest_of_head(dve, h - 1)
                finish_row(dve, len(items) - 1)
                rest_of_head(dve, HEADS - 1)

            @block.scalar
            def _(act):
                def round_head(h):
                    act.wait_ge(o_ready, h + 1)
                    act.activation(o_hi[:, h], bank[4 + h % 2][:], ACT.Copy).then_inc(o_rounded, 1)

                for i, (h, b) in enumerate(items):
                    s = stat[i % 2]
                    act.wait_ge(bias_ready, i + 1)
                    if i >= 2:
                        act.wait_ge(turned, i - 1)
                    act.activation(prob[i % 2][:, 0:P * (b + 1)], bank[i % 2][:, 0:P * (b + 1)], ACT.Exp,
                                   bias=s[:, 1:2], scale=ATT_SCALE, accum_out=s[:, 2:3]).then_inc(exp_done, 1)
                    if i % TT == 1 and i > TT:
                        round_head(h - 1)
                round_head(HEADS - 1)
        q_stack.close()
        mla_keep.close()

        def out_projection(name, n0, s_hi, s_lo, ada_at):
            copied = sem(name + "_copied")
            with nc.Block() as block:
                @block.sync
                def _(sp):
                    for n in range(n0, n0 + 4):
                        load_weights(sp, n + 2, src_of(n + 2))
                        for m in ada_at[n - n0]:
                            if m + 2 < 48:
                                load_ada(sp, m + 2)

                @block.tensor
                def _(pe):
                    for n in range(n0, n0 + 4):
                        pe.wait_ge(w_lo_ready, n + 1)
                        hi, lo = w_views(n, KD)
                        for i in range(2):
                            t = 2 * (n - n0) + i
                            if t >= 4:
                                pe.wait_ge(copied, t - 3)
                            for k in range(KD):
                                last = product(pe, bank[t % 4][:], hi[:, k, P * i:P * i + P], lo[:, k, P * i:P * i + P],
                                               s_hi[:, k], s_lo[:, k], k == 0, k == KD - 1)
                            last.then_inc(tile_done, 1)
                        for m in ada_at[n - n0]:
                            ada_reduce(pe, m)

                @block.scalar
                def _(act):
                    for n in range(n0, n0 + 4):
                        round_weights(act, n + 1)
                        for i in range(2):
                            t = 2 * (n - n0) + i
                            act.wait_ge(tile_done, tiles_to[n0] + t + 1)
                            act.activation(y[:, t], bank[t % 4][:], ACT.Copy).then_inc(copied, 1)

                @block.vector
                def _(dve):
                    for n in range(n0, n0 + 4):
                        rest_weights(dve, n + 1)
                        for m in ada_at[n - n0]:
                            ada_multiply(dve, m)
                            ada_finish(dve, m)

        out_projection("mla_o", N_WO, o_hi, o_lo, [[17, 18], [19, 20], [21, 22], [23]])
        o_stack.close()

        def mlp(name, l, n0, f_hi, f_lo, with_ada, ends):
            u_stack = ExitStack()
            u_hi = sb(u_stack, name + "_u_hi", [P, 8, SEQ], F32R, side="right")
            u_lo = sb(u_stack, name + "_u_lo", [P, 8, SEQ], F32R, side="right")
            relu = [sb(u_stack, f"{name}_relu{i}", [P, SEQ], side="right") for i in range(2)]
            usq = [sb(u_stack, f"{name}_usq{i}", [P, SEQ], side="right") for i in range(2)]
            relu_done, u_rounded, u_squared = sem("relu_done"), sem("u_rounded"), sem("u_squared")
            u_rest, y_added = sem("u_rest"), sem("y_added")
            u0, y0 = 32 * l, 34 * l
            t0 = tiles_to[n0]

            def groups(eng, body):
                with eng.Fori(0, 3) as g:
                    body(g, False)
                body(3, True)

            with nc.Block() as block:
                @block.sync
                def _(sp):
                    def body(g, final):
                        for j in range(8):
                            if not final:
                                jj = (j + 2) % 8
                                load_weights(sp, n0 + j + 2, ffn_src(l, jj, g + (j + 2) // 8), g)
                            elif n0 + 24 + j + 2 < N_END:
                                load_weights(sp, n0 + 24 + j + 2, src_of(n0 + 24 + j + 2))
                            if with_ada and j < 6 and not (final and j >= 4):
                                load_ada(sp, 24 + j + 2, g)
                    groups(sp, body)

                @block.tensor
                def _(pe):
                    def body(g, final):
                        for j in range(8):
                            n = n0 + j
                            pe.wait_ge(w_lo_ready, n + 1 + 8 * g)
                            hi, lo = w_views(n, KD)
                            for i in range(2):
                                t = 2 * j + i
                                if j < 4:
                                    if t >= 4:
                                        pe.wait_ge(relu_done, u0 + t - 3 + 8 * g)
                                    ps, m_hi, m_lo = bank[t % 4][:], f_hi, f_lo
                                else:
                                    pe.wait_ge(y_added, y0 + t - 7 + 8 * g)
                                    ps, m_hi, m_lo = bank[4 + t % 2][:], u_hi, u_lo
                                for k in range(KD):
                                    if t == 8:
                                        pe.wait_ge(u_rest, u0 + k + 1 + 8 * g)
                                    last = product(pe, ps, hi[:, k, P * i:P * i + P], lo[:, k, P * i:P * i + P],
                                                   m_hi[:, k], m_lo[:, k], k == 0, k == KD - 1)
                                last.then_inc(tile_done, 1)
                            if with_ada and j < 6:
                                ada_reduce(pe, 24 + j, g)
                    groups(pe, body)

                @block.scalar
                def _(act):
                    def body(g, final):
                        for j in range(8):
                            if not final or n0 + 24 + j + 1 < N_END:
                                round_weights(act, n0 + j + 1, g)
                            for i in range(2 if j < 4 else 0):
                                t = 2 * j + i
                                act.wait_ge(tile_done, t0 + t + 1 + 16 * g)
                                if t >= 2:
                                    act.wait_ge(u_rest, u0 + t - 1 + 8 * g)
                                act.activation(relu[t % 2][:], bank[t % 4][:], ACT.Relu).then_inc(relu_done, 1)
                                act.wait_ge(relu_done, u0 + t + 1 + 8 * g)
                                act.activation(u_hi[:, t], relu[t % 2][:], ACT.Square).then_inc(u_rounded, 1)
                    groups(act, body)

                @block.vector
                def _(dve):
                    for i in range(2):
                        dve.memset(y[:, 4 * i:4 * i + 4], 0.0).then_inc(y_added, 1)

                    def body(g, final):
                        for j in range(8):
                            if not final or n0 + 24 + j + 1 < N_END:
                                rest_weights(dve, n0 + j + 1, g)
                            if with_ada and j < 6:
                                ada_multiply(dve, 24 + j, g)
                            if j < 4:
                                for i in range(2):
                                    t = 2 * j + i
                                    dve.wait_ge(relu_done, u0 + t + 1 + 8 * g)
                                    dve.tensor_tensor(usq[t % 2][:], relu[t % 2][:], relu[t % 2][:],
                                                      ALU.mult).then_inc(u_squared, 1)
                                    dve.wait_ge(u_squared, u0 + t + 1 + 8 * g)
                                    dve.wait_ge(u_rounded, u0 + t + 1 + 8 * g)
                                    dve.tensor_tensor(u_lo[:, t], usq[t % 2][:], u_hi[:, t].bitcast(F32),
                                                      ALU.subtract).then_inc(u_rest, 1)
                            else:
                                for i in range(2):
                                    t = 2 * j + i
                                    dve.wait_ge(tile_done, t0 + t + 1 + 16 * g)
                                    dve.wait_ge(y_added, y0 + t - 6 + 8 * g)
                                    dve.tensor_tensor(y[:, t - 8], y[:, t - 8], bank[4 + t % 2][:],
                                                      ALU.add).then_inc(y_added, 1)
                            if with_ada and j < 6:
                                ada_finish(dve, 24 + j, g)
                    groups(dve, body)
            u_stack.close()

        def gdn(h_hi, h_lo):
            st = ExitStack()
            gp = [sb(st, f"gdn_small{i}", [P, TT, HEADS]) for i in range(8)]
            t_, abs_, e_, u_, ln_, g_, beta, g_cum = gp
            beta_eg = sb(st, "beta_eg", [P, TT, HEADS])
            to_end = sb(st, "to_end", [P, TT, HEADS])
            end_decay = sb(st, "end_decay", [P, 2, TT, HEADS])
            ba = sb(st, "ba", [P, TT, 2 * HEADS])
            w_ba = sb(st, "w_ba", [P, KD, 2 * HEADS])
            w_ba_hi = sb(st, "w_ba_hi", [P, KD, 2 * HEADS], F32R)
            w_ba_lo = sb(st, "w_ba_lo", [P, KD, 2 * HEADS], F32R)
            head_in = sb(st, "head_in", [P, 2, HEADS])
            state = sb(st, "state", [P, 2, P])
            v_new = sb(st, "v_new", [P, 2, P])

            def per_token(v):
                return v.rearrange("p t h -> p (t h)")

            with nc.Block() as block:
                gate_in, gate_step, gate_act, gate_pe = sem("gate_in"), sem("gate_step"), sem("gate_act"), sem("gate_pe")

                @block.sync
                def _(sp):
                    sp.dma_start(w_ba[:], rows(a["gdn_w_in"][0], KD)[:, :, QKV_W:QKV_W + 2 * HEADS]).then_inc(gate_in, 16)
                    for i, name in enumerate(("gdn_a_log", "gdn_dt_bias")):
                        sp.dma_start(head_in[:, i], a[name].to_broadcast([P, HEADS])).then_inc(gate_in, 16)

                @block.scalar
                def _(act):
                    act.wait_ge(gate_in, 48)
                    act.activation(w_ba_hi[:], w_ba[:], ACT.Copy).then_inc(gate_act, 1)
                    act.wait_ge(gate_pe, 1)
                    act.activation(ba[:], bank[4][:, 0:TT * 2 * HEADS], ACT.Copy).then_inc(gate_act, 1)
                    act.wait_ge(gate_step, 4)
                    act.activation(e_[:], abs_[:], ACT.Exp, scale=-1.0).then_inc(gate_act, 1)
                    act.activation(head_in[:, 0], head_in[:, 0], ACT.Exp).then_inc(gate_act, 1)
                    act.wait_ge(gate_step, 5)
                    act.activation(ln_[:], u_[:], ACT.Ln).then_inc(gate_act, 1)
                    act.activation(beta[:], ba[:, :, 0:HEADS], ACT.Sigmoid).then_inc(gate_act, 1)
                    act.wait_ge(gate_step, 15)
                    act.activation(per_token(beta_eg[:]), per_token(g_cum[:]), ACT.Exp).then_inc(gate_act, 1)
                    act.activation(to_end[:], to_end[:], ACT.Exp).then_inc(gate_act, 1)
                    act.activation(end_decay[:].rearrange("p i t h -> p (i t h)"), bank[5][:, 0:64],
                                   ACT.Exp).then_inc(gate_act, 1)

                @block.vector
                def _(dve):
                    def step(ins, n):
                        ins.then_inc(gate_step, 1)
                        dve.wait_ge(gate_step, n)
                    dve.wait_ge(gate_act, 1)
                    step(dve.tensor_tensor(w_ba_lo[:], w_ba[:], w_ba_hi[:].bitcast(F32), ALU.subtract), 1)
                    dve.wait_ge(gate_act, 2)
                    bias = head_in[:, 1:2].to_broadcast([P, TT, HEADS])
                    step(dve.tensor_tensor(t_[:], ba[:, :, HEADS:], bias, ALU.add), 2)
                    step(dve.scalar_tensor_tensor(abs_[:], t_[:], -1.0, t_[:], ALU.mult, ALU.max), 3)
                    step(dve.tensor_scalar(t_[:], t_[:], 0.0, None, ALU.max), 4)
                    dve.wait_ge(gate_act, 3)
                    step(dve.tensor_scalar(u_[:], e_[:], 1.0, None, ALU.add), 5)
                    step(dve.scalar_tensor_tensor(e_[:], u_[:], -1.0, e_[:], ALU.add, ALU.subtract), 6)
                    dve.wait_ge(gate_act, 5)
                    step(dve.reciprocal(u_[:], u_[:]), 7)
                    step(dve.tensor_tensor(e_[:], e_[:], u_[:], ALU.mult), 8)
                    step(dve.tensor_tensor(ln_[:], ln_[:], e_[:], ALU.subtract), 9)
                    step(dve.tensor_tensor(t_[:], t_[:], ln_[:], ALU.add), 10)
                    step(dve.tensor_scalar(t_[:], t_[:], -1.0, None, ALU.mult), 11)
                    step(dve.tensor_tensor(g_[:], t_[:], head_in[:, 0:1].to_broadcast([P, TT, HEADS]), ALU.mult), 12)
                    dve.wait_ge(gate_pe, 2)
                    step(dve.tensor_copy(per_token(g_cum[:]), bank[4][:, 0:32]), 13)
                    step(dve.tensor_copy(per_token(to_end[:]), bank[4][:, 32:64]), 14)
                    step(dve.tensor_tensor(to_end[:], to_end[:], g_cum[:], ALU.subtract), 15)
                    dve.wait_ge(gate_act, 7)
                    dve.tensor_tensor(beta_eg[:], beta_eg[:], beta[:], ALU.mult)

                @block.tensor
                def _(pe):
                    pe.wait_ge(gate_step, 1)
                    for t in range(TT):
                        for k in range(KD):
                            tok = slice(P * t, P * t + P)
                            last = product(pe, bank[4][:, 16 * t:16 * t + 16], h_hi[:, k, tok], h_lo[:, k, tok],
                                           w_ba_hi[:, k], w_ba_lo[:, k], k == 0, k == KD - 1)
                    last.then_inc(gate_pe, 1)
                    pe.wait_ge(gate_step, 12)
                    gf = per_token(g_[:])
                    pe.matmul(bank[4][:, 0:32], const[:, C_TRI:C_TRI + P], gf, start=True, stop=True)
                    pe.matmul(bank[4][:, 32:64], const[:, C_SAME:C_SAME + P], gf, start=True, stop=True)
                    for i in range(2):
                        last = pe.matmul(bank[5][:, 32 * i:32 * i + 32],
                                         const[:, C_HALF + i:C_HALF + i + 1].to_broadcast([P, P]), gf,
                                         start=True, stop=True)
                    last.then_inc(gate_pe, 1)

            for pair in range(HEADS // 2):
                gdn_pair(st, pair, h_hi, h_lo, g_, g_cum, beta, beta_eg, to_end, end_decay, state, v_new)
            st.close()

        def gdn_pair(outer, pair, h_hi, h_lo, g_, g_cum, beta, beta_eg, to_end, end_decay, state, v_new):
            q_t, k_t, v_t, z_t = (y[:, 2 * i:2 * i + 2] for i in range(4))
            n0 = N_GDN + 4 * pair
            t0 = tiles_to[n0]
            heads = (2 * pair, 2 * pair + 1)

            pre_copied, z_done, conv_step, conv_silu = sem("pre_copied"), sem("z_done"), sem("conv_step"), sem("conv_silu")
            hn_squared, hn_summed, hn_root, hn_inv, hn_done = (sem("hn_" + v) for v in ("squared", "summed", "root", "inv", "done"))
            with ExitStack() as st, nc.Block() as block:
                pre = [sb(st, f"pre{i}_{pair}", [P, CONV - 1 + SEQ]) for i in range(2)]
                conv = [sb(st, f"conv{i}_{pair}", [P, SEQ]) for i in range(2)]
                norm = [sb(st, f"norm{i}_{pair}", [P, SEQ]) for i in range(2)]
                dst = [v[:, i] for v in (q_t, k_t, v_t) for i in range(2)]

                @block.sync
                def _(sp):
                    for n in range(n0, n0 + 4):
                        load_weights(sp, n + 2, src_of(n + 2))

                @block.tensor
                def _(pe):
                    for n in range(n0, n0 + 4):
                        pe.wait_ge(w_lo_ready, n + 1)
                        hi, lo = w_views(n, KD)
                        for i in range(2):
                            t = 2 * (n - n0) + i
                            if t >= 4:
                                pe.wait_ge(pre_copied, 6 * pair + t - 3)
                            for k in range(KD):
                                last = product(pe, bank[t % 4][:], hi[:, k, P * i:P * i + P], lo[:, k, P * i:P * i + P],
                                               h_hi[:, k], h_lo[:, k], k == 0, k == KD - 1)
                            last.then_inc(tile_done, 1)
                    for t in range(4):
                        pe.wait_ge(hn_squared, 4 * pair + t + 1)
                        pe.matmul(bank[4 + t][:], ones[:], sq[t % 2][:], start=True, stop=True).then_inc(hn_summed, 1)

                @block.scalar
                def _(act):
                    def silu(t):
                        act.wait_ge(conv_step, 2 + 26 * pair + 4 * t + 4)
                        act.activation(dst[t], conv[t % 2][:], ACT.Silu).then_inc(conv_silu, 1)

                    for n in range(n0, n0 + 4):
                        round_weights(act, n + 1)
                        for i in range(2):
                            t = 2 * (n - n0) + i
                            act.wait_ge(tile_done, t0 + t + 1)
                            if t < 6:
                                act.wait_ge(conv_step, 2 + 26 * pair + (4 * (t - 1) if t >= 2 else 0))
                                act.activation(pre[t % 2][:, CONV - 1:], bank[t % 4][:], ACT.Copy).then_inc(pre_copied, 1)
                                if t >= 1:
                                    silu(t - 1)
                            else:
                                if t == 6:
                                    silu(5)
                                act.activation(z_t[:, i], bank[t % 4][:], ACT.Silu).then_inc(z_done, 1)
                    for t in range(4):
                        if t >= 2:
                            act.wait_ge(hn_summed, 4 * pair + t - 1)
                        act.wait_ge(conv_silu, 6 * pair + 6)
                        act.activation(sq[t % 2][:], dst[t], ACT.Square).then_inc(hn_squared, 1)
                    for t in range(4):
                        act.wait_ge(hn_summed, 4 * pair + t + 1)
                        if t >= 2:
                            act.wait_ge(hn_done, 4 * pair + t - 1)
                        act.activation(norm[t % 2][:], bank[4 + t][:], ACT.Sqrt, bias=bias_t[:, 1:2] if t < 2 else bias_t[:, 0:1],
                                       scale=float(P) if t < 2 else 1.0).then_inc(hn_root, 1)

                @block.vector
                def _(dve):
                    base = 26 * pair + 2
                    for i in range(2):
                        dve.memset(pre[i][:, 0:CONV - 1], 0.0).then_inc(conv_step, 1)
                    for n in range(n0, n0 + 4):
                        rest_weights(dve, n + 1)
                        for i in range(2 if n < n0 + 3 else 0):
                            t = 2 * (n - n0) + i
                            dve.wait_ge(pre_copied, 6 * pair + t + 1)
                            if t >= 2:
                                dve.wait_ge(conv_silu, 6 * pair + t - 1)
                            for j in range(CONV):
                                at = V_CONV + 24 * j + 8 * (n - n0) + heads[i]
                                tap, w = pre[t % 2][:, j:j + SEQ], vec[:, at:at + 1]
                                if j == 0:
                                    dve.tensor_scalar(conv[t % 2][:], tap, w, None, ALU.mult).then_inc(conv_step, 1)
                                else:
                                    dve.wait_ge(conv_step, base + 4 * t + j)
                                    dve.scalar_tensor_tensor(conv[t % 2][:], tap, w, conv[t % 2][:], ALU.mult,
                                                             ALU.add).then_inc(conv_step, 1)
                    for t in range(4):
                        dve.wait_ge(hn_root, 4 * pair + t + 1)
                        dve.reciprocal(norm[t % 2][:], norm[t % 2][:]).then_inc(hn_inv, 1)
                        dve.wait_ge(hn_inv, 4 * pair + t + 1)
                        dve.tensor_tensor(dst[t], dst[t], norm[t % 2][:], ALU.mult).then_inc(hn_done, 1)

            core = ExitStack()
            names = ("kbg", "k_end", "v_beta", "decay", "a_qk", "l_t", "q_dec", "inv", "inv_t", "prod")
            kbg, k_end, v_beta, decay, a_qk, l_t, q_dec, inv, inv_t, prod = (
                sb(core, f"{v}_{pair}", [P, 2, TT, P]) for v in names)
            w_t, u_tok, l_off = kbg, v_beta, decay

            def flat(v):
                return v.rearrange("p t c -> p (t c)")

            def over_tiles(v):
                return v.unsqueeze(1).to_broadcast([P, TT, P])

            def token_scalar(v, h):
                return v[:, :, h:h + 1].to_broadcast([P, TT, P])

            def tiles4(v):
                return v.rearrange("p (t c) -> p t c", t=TT)

            names = ("gram", "turned_kv", "kv_used", "diff", "grow_exp", "decay_exp", "core_dve", "off", "w_ready",
                     "w_copied", "step_ready", "stepped", "uw_ready", "uw_copied")
            (gram, turned_kv, kv_used, diff, grow_exp, decay_exp, core_dve, off, w_ready, w_copied, step_ready,
             stepped, uw_ready, uw_copied) = (sem("core_" + v) for v in names)
            with nc.Block() as block:
                @block.tensor
                def _(pe):
                    for i, h in enumerate(heads):
                        for t in range(TT):
                            tok, dst = slice(P * t, P * t + P), slice(P * t, P * t + P)
                            pe.matmul(bank[4 + i][:, dst], g_[:, t, h:h + 1].to_broadcast([P, P]),
                                      const[:, C_TRI:C_TRI + P], start=True, stop=True)
                            pe.matmul(bank[i][:, dst], k_t[:, i, tok], k_t[:, i, tok], start=True, stop=True)
                            pe.matmul(bank[2 + i][:, dst], k_t[:, i, tok], q_t[:, i, tok], start=True, stop=True)
                            last = pe.matmul(bank[6 + i][:, dst], beta[:, t, h:h + 1].to_broadcast([P, P]), ident,
                                             start=True, stop=True)
                        last.then_inc(gram, 1)
                    for j, src in enumerate((k_t, v_t)):
                        for i in range(2):
                            if j == 0:
                                pe.wait_ge(core_dve, 8 * pair + 4 * i + 3)
                            else:
                                pe.wait_ge(kv_used, 6 * pair + 2 * i + 2)
                            for t in range(TT):
                                last = pe.transpose(bank[6 + i][:, P * t:P * t + P], src[:, i, P * t:P * t + P], ident)
                            last.then_inc(turned_kv, 1)
                    for l in range(LEVELS):
                        for i in range(2):
                            pe.wait_ge(off, 12 * pair + 2 * l + i + 1)
                            if l:
                                pe.wait_ge(stepped, 22 * pair + 4 * (l - 1) + 2 * i + 2)
                            for t in range(TT):
                                last = pe.matmul(bank[i][:, P * t:P * t + P], l_off[:, i, t], inv[:, i, t] if l else ident,
                                                 start=True, stop=True)
                            last.then_inc(w_ready, 1)
                        for i in range(2 if l else 0):
                            pe.wait_ge(w_copied, 10 * pair + 2 * (l - 1) + i + 1)
                            for t in range(TT):
                                cols = slice(P * t, P * t + P)
                                if l < LEVELS - 1:
                                    pe.matmul(bank[2 + i][:, cols], inv_t[:, i, t], prod[:, i, t], start=True, stop=True)
                                last = pe.matmul(bank[4 + i][:, cols], prod[:, i, t], inv_t[:, i, t], start=True, stop=True)
                            last.then_inc(step_ready, 1)
                    for i in range(2):
                        pe.wait_ge(stepped, 22 * pair + 20 + i + 1)
                        pe.wait_ge(kv_used, 6 * pair + 4 + i + 1)
                        for t in range(TT):
                            cols = slice(P * t, P * t + P)
                            pe.matmul(bank[i][:, cols], inv_t[:, i, t], v_beta[:, i, t], start=True, stop=True)
                            last = pe.matmul(bank[2 + i][:, cols], kbg[:, i, t], inv_t[:, i, t], start=True, stop=True)
                        last.then_inc(uw_ready, 1)

                @block.gpsimd
                def _(pool):
                    for l in range(LEVELS):
                        for i in range(2):
                            if l:
                                pool.wait_ge(w_ready, 12 * pair + 2 * (l - 1) + i + 1)
                                if l == 1:
                                    pool.wait_ge(stepped, 22 * pair + 2 * i + 2)
                            else:
                                pool.wait_ge(core_dve, 8 * pair + 4 * i + 4)
                            mask = const[:, C_LEVEL + P * l:C_LEVEL + P * l + P]
                            pool.tensor_tensor(l_off[:, i], l_t[:, i], over_tiles(mask), ALU.mult).then_inc(off, 1)

                @block.scalar
                def _(act):
                    for i in range(2):
                        act.wait_ge(diff, 8 * pair + 4 * i + 4)
                        act.activation(flat(decay[:, i]), flat(decay[:, i]), ACT.Exp).then_inc(decay_exp, 1)
                        act.activation(flat(q_dec[:, i]), bank[4 + i][:], ACT.Exp).then_inc(grow_exp, 1)
                    for l in range(1, LEVELS):
                        for i in range(2):
                            act.wait_ge(w_ready, 12 * pair + 2 * l + i + 1)
                            act.activation(flat(prod[:, i]), bank[i][:], ACT.Copy).then_inc(w_copied, 1)
                    for i in range(2):
                        act.wait_ge(uw_ready, 2 * pair + i + 1)
                        act.activation(flat(u_tok[:, i]), bank[i][:], ACT.Copy).then_inc(uw_copied, 1)
                        act.activation(flat(w_t[:, i]), bank[2 + i][:], ACT.Copy).then_inc(uw_copied, 1)

                @block.vector
                def _(dve):
                    for i, h in enumerate(heads):
                        dve.wait_ge(gram, 2 * pair + i + 1)
                        for t in range(TT):
                            dve.tensor_scalar(decay[:, i, t], bank[4 + i][:, P * t:P * t + P], g_cum[:, t, h:h + 1], 0.0,
                                              ALU.subtract, ALU.min).then_inc(diff, 1)
                    for i in range(2):
                        at = 8 * pair + 4 * i
                        dve.wait_ge(decay_exp, 2 * pair + i + 1)
                        dve.tensor_tensor(decay[:, i], decay[:, i], over_tiles(const[:, C_TRI:C_TRI + P]),
                                          ALU.mult).then_inc(core_dve, 1)
                        dve.wait_ge(core_dve, at + 1)
                        dve.tensor_tensor(flat(l_t[:, i]), flat(decay[:, i]), bank[i][:], ALU.mult).then_inc(core_dve, 1)
                        dve.wait_ge(core_dve, at + 2)
                        dve.tensor_tensor(flat(l_t[:, i]), flat(l_t[:, i]), bank[6 + i][:], ALU.mult).then_inc(core_dve, 1)
                        dve.tensor_tensor(flat(a_qk[:, i]), flat(decay[:, i]), bank[2 + i][:], ALU.mult).then_inc(core_dve, 1)
                    for i, h in enumerate(heads):
                        dve.wait_ge(turned_kv, 4 * pair + i + 1)
                        for dst, f in ((kbg, beta_eg), (k_end, to_end)):
                            dve.tensor_tensor(dst[:, i], tiles4(bank[6 + i][:]), token_scalar(f, h), ALU.mult).then_inc(kv_used, 1)
                    for i in range(2):
                        dve.wait_ge(grow_exp, 2 * pair + i + 1)
                        dve.tensor_tensor(flat(q_dec[:, i]), flat(q_dec[:, i]), q_t[:, i], ALU.mult)
                    for i, h in enumerate(heads):
                        dve.wait_ge(turned_kv, 4 * pair + 2 + i + 1)
                        dve.tensor_tensor(v_beta[:, i], tiles4(bank[6 + i][:]), token_scalar(beta, h), ALU.mult).then_inc(kv_used, 1)
                    for l in range(LEVELS):
                        for i in range(2):
                            if l == 0:
                                dve.wait_ge(w_ready, 12 * pair + i + 1)
                                dve.tensor_tensor(inv[:, i], over_tiles(ident), tiles4(bank[i][:]), ALU.subtract).then_inc(stepped, 1)
                                dve.tensor_tensor(inv_t[:, i], over_tiles(ident), l_off[:, i], ALU.subtract).then_inc(stepped, 1)
                            else:
                                dve.wait_ge(step_ready, 10 * pair + 2 * (l - 1) + i + 1)
                                if l < LEVELS - 1:
                                    dve.tensor_tensor(flat(inv[:, i]), flat(inv[:, i]), bank[2 + i][:], ALU.subtract).then_inc(stepped, 1)
                                dve.tensor_tensor(flat(inv_t[:, i]), flat(inv_t[:, i]), bank[4 + i][:], ALU.subtract).then_inc(stepped, 1)

            scan_ws, scan_new, scan_kv, scan_state = (sem("scan_" + v) for v in ("ws", "new", "kv", "state"))
            on_squared, on_summed, on_root, on_step, on_hi, on_out = (sem("on_" + v) for v in ("squared", "summed", "root", "step", "hi", "out"))
            N_CH = SEQ // CHUNK
            o_n, o_f = (inv, inv_t)
            with nc.Block() as block:
                @block.tensor
                def _(pe):
                    for n in range(N_CH):
                        t, r = n // 2, CHUNK * (n % 2)
                        cols = slice(CHUNK * n, CHUNK * n + CHUNK)
                        for i in range(2):
                            pe.wait_ge(scan_state, (2 * N_CH + 1) * pair + (2 * n + i if n else 1))
                            pe.matmul(bank[i][r:r + CHUNK, 0:P], flat(w_t[:, i])[:, cols], state[:, i], start=True,
                                      stop=True).then_inc(scan_ws, 1)
                            pe.matmul(bank[4 + i][:, cols], state[:, i], flat(q_dec[:, i])[:, cols], start=True, stop=False)
                        for i in range(2):
                            pe.wait_ge(scan_new, 2 * (N_CH * pair + n) + i + 1)
                            vn = v_new[r:r + CHUNK, i]
                            pe.matmul(bank[4 + i][:, cols], vn, a_qk[r:r + CHUNK, i, t, r:r + CHUNK], start=False, stop=True)
                            pe.matmul(bank[2 + i][:, 0:P], k_end[r:r + CHUNK, i, t], vn, start=True,
                                      stop=True).then_inc(scan_kv, 1)
                    for i in range(2):
                        pe.wait_ge(on_squared, 2 * pair + i + 1)
                        pe.matmul(bank[6 + i][:], ones[:], sq[i][:], start=True, stop=True).then_inc(on_summed, 1)

                @block.vector
                def _(dve):
                    dve.memset(state[:], 0.0).then_inc(scan_state, 1)
                    for n in range(N_CH):
                        t, r = n // 2, CHUNK * (n % 2)
                        for i in range(2):
                            dve.wait_ge(scan_ws, 2 * (N_CH * pair + n) + i + 1)
                            dve.tensor_tensor(v_new[r:r + CHUNK, i], u_tok[r:r + CHUNK, i, t], bank[i][r:r + CHUNK, 0:P],
                                              ALU.subtract).then_inc(scan_new, 1)
                        for i, h in enumerate(heads):
                            dve.wait_ge(scan_kv, 2 * (N_CH * pair + n) + i + 1)
                            dve.scalar_tensor_tensor(state[:, i], state[:, i], end_decay[:, n % 2, t, h:h + 1],
                                                     bank[2 + i][:, 0:P], ALU.mult, ALU.add).then_inc(scan_state, 1)
                    for i in range(2):
                        at = 6 * pair + 3 * i
                        dve.wait_ge(on_root, 2 * pair + i + 1)
                        dve.reciprocal(sq[i][:], sq[i][:]).then_inc(on_step, 1)
                        dve.wait_ge(on_step, at + 1)
                        dve.tensor_tensor(flat(o_n[:, i]), bank[4 + i][:], sq[i][:], ALU.mult).then_inc(on_step, 1)
                        dve.wait_ge(on_step, at + 2)
                        dve.scalar_tensor_tensor(flat(o_f[:, i]), flat(o_n[:, i]), vec[:, V_ON:V_ON + 1], z_t[:, i],
                                                 ALU.mult, ALU.mult).then_inc(on_step, 1)
                    for i, h in enumerate(heads):
                        dve.wait_ge(on_hi, 2 * pair + i + 1)
                        dve.tensor_tensor(o_lo[:, h], flat(o_f[:, i]), o_hi[:, h].bitcast(F32), ALU.subtract)

                @block.scalar
                def _(act):
                    for i in range(2):
                        act.wait_ge(scan_kv, 2 * N_CH * (pair + 1) - 1 + i)
                        act.activation(sq[i][:], bank[4 + i][:], ACT.Square).then_inc(on_squared, 1)
                    for i in range(2):
                        act.wait_ge(on_summed, 2 * pair + i + 1)
                        act.activation(sq[i][:], bank[6 + i][:], ACT.Sqrt, bias=bias_t[:, 0:1], scale=1 / P).then_inc(on_root, 1)
                    for i, h in enumerate(heads):
                        act.wait_ge(on_step, 6 * pair + 3 * i + 3)
                        act.activation(o_hi[:, h], flat(o_f[:, i]), ACT.Copy).then_inc(on_hi, 1)
            core.close()

        def h_pair(name):
            st = ExitStack()
            return st, sb(st, "h_hi_" + name, [P, KD, SEQ], F32R), sb(st, "h_lo_" + name, [P, KD, SEQ], F32R)

        hs, h_hi, h_lo = h_pair("mlp0")
        boundary(0, (0, 2), (0, 3), h_hi, h_lo)
        mlp("mlp0", 0, N_FFN0, h_hi, h_lo, True, False)
        hs.close()
        ada_stack.close()

        hs, h_hi, h_lo = h_pair("gdn")
        boundary(1, (0, 5), (1, 0), h_hi, h_lo)
        gdn_o_stack = ExitStack()
        o_hi = sb(gdn_o_stack, "o_hi_gdn", [P, HEADS, SEQ], F32R, side="right")
        o_lo = sb(gdn_o_stack, "o_lo_gdn", [P, HEADS, SEQ], F32R, side="right")
        gdn(h_hi, h_lo)
        hs.close()
        out_projection("gdn_o", N_GWO, o_hi, o_lo, [[]] * 4)
        gdn_o_stack.close()
        hs, h_hi, h_lo = h_pair("mlp1")
        boundary(2, (1, 2), (1, 3), h_hi, h_lo)
        mlp("mlp1", 1, N_FFN1, h_hi, h_lo, False, True)
        hs.close()
        boundary(3, (1, 5), None, None, None)

        with nc.Block() as block:
            o_tok = sb(root, "o_tok", [P, TT, D], side="right")
            back, back_copied, stored = sem("back"), sem("back_copied"), sem("stored")

            @block.tensor
            def _(pe):
                for i in range(2 * TT):
                    if i >= 4:
                        pe.wait_ge(back_copied, i - 3)
                    for k in range(4):
                        last = pe.transpose(bank[i % 4][:, P * k:P * k + P],
                                            x[:, 4 * (i % 2) + k, P * (i // 2):P * (i // 2) + P], ident)
                    last.then_inc(back, 1)

            @block.vector
            def _(dve):
                for i in range(2 * TT):
                    dve.wait_ge(back, i + 1)
                    dve.tensor_copy(o_tok[:, i // 2, 512 * (i % 2):512 * (i % 2) + 512], bank[i % 4][:]).then_inc(back_copied, 1)

            @block.sync
            def _(sp):
                for t in range(TT):
                    sp.wait_ge(back_copied, 2 * t + 2)
                    sp.dma_start(out[0, P * t:P * t + P, :], o_tok[:, t]).then_inc(stored, 16)
                sp.wait_ge(stored, 16 * TT)


_INS = ['x', 'c', 'positions', 'ada_w', 'ada_b', 'sandwich_g', 'mla_w_in', 'mla_q_norm_g', 'mla_kv_norm_g',
        'mla_w_uq', 'mla_w_ukv', 'mla_w_o', 'gdn_w_in', 'gdn_conv_w', 'gdn_a_log', 'gdn_dt_bias',
        'gdn_out_norm_g', 'gdn_w_o', 'ffn_w1', 'ffn_w2']


def make(nc, inputs):
    arrays, aps = {}, {}
    for name in _INS + ["const"]:
        v = constants() if name == "const" else np.ascontiguousarray(inputs[name])
        arrays[f"in_{name}"] = v
        aps[name] = nc.dram_tensor(f"in_{name}", v.shape, mybir.dt.from_np(v.dtype), kind="ExternalInput").ap()
    out = nc.dram_tensor("out_x", (1, SEQ, D), F32, kind="ExternalOutput").ap()
    build(nc, aps, out)
    return arrays


def kernel(**inputs):
    import concourse.bacc as bacc
    from concourse.bass_utils import run_bass_kernel_spmd

    nc = bacc.Bacc("TRN2", target_bir_lowering=False, num_devices=1)
    arrays = make(nc, inputs)
    r = run_bass_kernel_spmd(nc, [arrays], core_ids=[0])
    return r.results[0]["out_x"]
```

```python
from contextlib import ExitStack

import numpy as np

import concourse.bass as bass
from concourse import mybir

F32 = mybir.dt.float32
F32R = mybir.dt.float32r
I32 = mybir.dt.int32
ALU = mybir.AluOpType
ACT = mybir.ActivationFunctionType
AX = mybir.AxisListType

P = 128
D = 1024
SEQ = 512
KD = D // P
TT = SEQ // P
HEADS = 8
CHUNK = 64
Q_LORA = 384
KV_LORA = 256
ROPE = 64
NOPE = 128
KQ = Q_LORA // P
KKV = KV_LORA // P
FF = 4096
CONV = 4
EPS = 1e-6
ROPE_THETA = 10000.0
QKV_W = 3 * D
LEVELS = 6
ATT_SCALE = float((NOPE + ROPE) ** -0.5)
MASKED = -1e30

V_ADAB, V_C, V_QN, V_KVN, V_ON = 0, 96, 104, 107, 109
N_V1 = 110
V_SW = N_V1
V_CONV = V_SW + 64
N_VEC = V_CONV + 96

C_ID, C_TRI, C_SAME, C_LEVEL = 0, P, 2 * P, 3 * P
C_HALF = C_LEVEL + LEVELS * P
C_FREQ, C_SIGN, C_EARLY, C_LATE = C_HALF + 2, C_HALF + 3, C_HALF + 4, C_HALF + 4 + P
N_CONST = C_LATE + P


def constants():
    out = np.zeros((P, N_CONST), np.float32)
    j, c = np.arange(P)[:, None], np.arange(P)[None, :]
    same = j // CHUNK == c // CHUNK
    out[:, C_ID:C_ID + P] = j == c
    out[:, C_TRI:C_TRI + P] = same & (j <= c)
    out[:, C_SAME:C_SAME + P] = same
    for l in range(LEVELS):
        m = 1 << l
        out[:, C_LEVEL + l * P:C_LEVEL + (l + 1) * P] = (j // (2 * m) == c // (2 * m)) & (j // m < c // m)
    out[:, C_HALF] = np.arange(P) < CHUNK
    out[:, C_HALF + 1] = np.arange(P) >= CHUNK
    half = ROPE // 2
    freq = ROPE_THETA ** (-np.arange(half) / half)
    out[:, C_FREQ] = freq[np.arange(P) % half]
    out[:, C_SIGN] = np.where(np.arange(P) % ROPE < half, -1.0, 1.0)
    out[0, C_EARLY:C_EARLY + P] = np.arange(P) < CHUNK
    out[0, C_LATE:C_LATE + P] = MASKED * (np.arange(P) >= CHUNK)
    return out


def chunk_plan():
    size = [2048] * 3 + [1152] * 4 + [2048] * 2 + [2048] * 4 + [2048] * 32 + [2048] * 20 + [2048] * 32
    tiles = [2] * 3 + [3] * 4 + [8] * 2 + [2] * 4 + [2] * 32 + [2] * 20 + [2] * 32
    parts = [1] * 2 + [3] + [4] * 4 + [1] * (len(size) - 7)
    return size, tiles, parts


def build(nc, a, out):
    size, tiles, parts = chunk_plan()
    tiles_to = [sum(tiles[:n]) for n in range(len(tiles) + 1)]
    N_IN, N_UQ, N_UKV, N_WO, N_FFN0 = 0, 3, 7, 9, 13
    N_GDN, N_GWO, N_FFN1, N_END = 45, 61, 65, 97

    root = ExitStack()
    with root:
        sems = {}

        def sem(name):
            if name not in sems:
                sems[name] = root.enter_context(nc.semaphore(name))
            return sems[name]

        def sb(stack, name, shape, dt=F32, side="left"):
            return stack.enter_context(nc.sbuf_tensor(name, shape, dt, side=side))

        bank = [root.enter_context(nc.psum_tensor(f"bank{i}", [P, 512], F32)) for i in range(8)]
        sum_bank, mod_bank = bank[6], bank[7]

        x = sb(root, "x", [P, KD, SEQ])
        y = sb(root, "y", [P, KD, SEQ])
        w_raw = [sb(root, f"w_raw{i}", [P, 2048]) for i in range(2)]
        w_hi = [sb(root, f"w_hi{i}", [P, 2048], F32R) for i in range(2)]
        w_lo = [sb(root, f"w_lo{i}", [P, 2048], F32R) for i in range(2)]
        const = sb(root, "const", [P, N_CONST])
        vec = sb(root, "vec", [P, N_VEC])
        ones = sb(root, "ones", [P, P])
        coef = sb(root, "coef", [P, 2, 6 * KD])
        sq = [sb(root, f"sq{i}", [P, SEQ]) for i in range(2)]
        rms_tok = sb(root, "rms_tok", [P, 2 * TT])
        bias_t = sb(root, "bias_t", [P, 2])
        ident = const[:, C_ID:C_ID + P]

        w_loaded = [sem("w_loaded0"), sem("w_loaded1")]
        w_hi_ready, w_lo_ready, tile_done = sem("w_hi_ready"), sem("w_lo_ready"), sem("tile_done")

        def load_weights(sp, n, src, g=0):
            if n >= 2:
                sp.wait_ge(w_lo_ready, n - 1 + 8 * g)
            at = 0
            for part in src if isinstance(src, list) else [src]:
                k, cols = part.shape[1:]
                dst = w_raw[n % 2][:, 0:size[n]].rearrange("p (k n) -> p k n", k=k)[:, :, at:at + cols]
                sp.dma_start(dst, part).then_inc(w_loaded[n % 2], 16)
                at += cols

        def round_weights(act, n, g=0):
            act.wait_ge(w_loaded[n % 2], 16 * sum(parts[n % 2:n + 1:2]) + 64 * g)
            if n >= 2:
                act.wait_ge(tile_done, tiles_to[n - 1] + 16 * g)
            act.activation(w_hi[n % 2][:, 0:size[n]], w_raw[n % 2][:, 0:size[n]], ACT.Copy).then_inc(w_hi_ready, 1)

        def rest_weights(dve, n, g=0):
            dve.wait_ge(w_hi_ready, n + 1 + 8 * g)
            dve.tensor_tensor(w_lo[n % 2][:, 0:size[n]], w_raw[n % 2][:, 0:size[n]],
                              w_hi[n % 2][:, 0:size[n]].bitcast(F32), ALU.subtract).then_inc(w_lo_ready, 1)

        def product(pe, ps, s_hi, s_lo, m_hi, m_lo, first, last):
            pe.matmul(ps, s_lo, m_hi, start=first, stop=False)
            pe.matmul(ps, s_hi, m_lo, start=False, stop=False)
            return pe.matmul(ps, s_hi, m_hi, start=False, stop=last)

        def w_views(n, k):
            return (w_hi[n % 2][:, 0:size[n]].rearrange("p (k n) -> p k n", k=k),
                    w_lo[n % 2][:, 0:size[n]].rearrange("p (k n) -> p k n", k=k))

        def rows(w, k):
            return w.rearrange("(k p) n -> p k n", p=P)

        def src_of(n):
            if n == N_UQ - 1:
                w, at = rows(a["mla_w_in"][0], KD), 256 * n
                return [w[:, :, at:at + P]] + [w[:, :, at + P:at + P + ROPE]] * 2
            if n < N_UQ:
                return rows(a["mla_w_in"][0], KD)[:, :, 256 * n:min(256 * n + 256, Q_LORA + KV_LORA + ROPE)]
            if n < N_UKV:
                w, at = rows(a["mla_w_uq"][0], KQ), 2 * (NOPE + ROPE) * (n - N_UQ)
                heads = (at, at + NOPE + ROPE)
                return [w[:, :, c:c + NOPE] for c in heads] + [w[:, :, c + NOPE:c + NOPE + ROPE] for c in heads]
            if n < N_WO:
                return rows(a["mla_w_ukv"][0], KKV)[:, :, 1024 * (n - N_UKV):1024 * (n - N_UKV + 1)]
            if n < N_FFN0:
                return rows(a["mla_w_o"][0], KD)[:, :, 256 * (n - N_WO):256 * (n - N_WO + 1)]
            if n < N_GDN:
                return ffn_src(0, (n - N_FFN0) % 8, (n - N_FFN0) // 8)
            if n < N_GWO:
                pair, kind = (n - N_GDN) // 4, (n - N_GDN) % 4
                at = 256 * pair + (D * kind if kind < 3 else QKV_W + 2 * HEADS)
                return rows(a["gdn_w_in"][0], KD)[:, :, at:at + 256]
            if n < N_FFN1:
                return rows(a["gdn_w_o"][0], KD)[:, :, 256 * (n - N_GWO):256 * (n - N_GWO + 1)]
            return ffn_src(1, (n - N_FFN1) % 8, (n - N_FFN1) // 8)

        def ffn_src(l, j, g):
            if j < 4:
                return rows(a["ffn_w1"][l], KD)[:, :, bass.ds(1024 * g + 256 * j, 256)]
            return a["ffn_w2"][l][bass.ds(1024 * g, 1024), :].rearrange("(k p) n -> p k n", p=P)[
                :, :, 256 * (j - 4):256 * (j - 3)]

        ada_stack = root.enter_context(ExitStack())
        ada_raw = [sb(ada_stack, f"ada_raw{i}", [P, KD, 256]) for i in range(2)]
        ada_acc = [sb(ada_stack, f"ada_acc{i}", [P, 256]) for i in range(2)]
        c_act = sb(ada_stack, "c_act", [P, KD])
        ada_loaded = [sem("ada_loaded0"), sem("ada_loaded1")]
        ada_step, ada_reduced, ada_done = sem("ada_step"), sem("ada_reduced"), sem("ada_done")

        def load_ada(sp, m, g=0):
            if m >= 2:
                sp.wait_ge(ada_step, KD * (m - 1) + KD * 6 * g)
            src = a["ada_w"][m // 24].rearrange("(k p) n -> p k n", p=P)[:, :, bass.ds(256 * (m % 24) + 1536 * g, 256)]
            sp.dma_start(ada_raw[m % 2][:], src).then_inc(ada_loaded[m % 2], 16)

        def ada_multiply(dve, m, g=0):
            dve.wait_ge(ada_loaded[m % 2], 16 * (m // 2 + 1) + 48 * g)
            if m >= 2:
                dve.wait_ge(ada_reduced, m - 1 + 6 * g)
            acc = ada_acc[m % 2][:]
            dve.tensor_scalar(acc, ada_raw[m % 2][:, 0], c_act[:, 0:1], None, ALU.mult).then_inc(ada_step, 1)
            for k in range(1, KD):
                dve.wait_ge(ada_step, KD * m + k + KD * 6 * g)
                dve.scalar_tensor_tensor(acc, ada_raw[m % 2][:, k], c_act[:, k:k + 1], acc,
                                         ALU.mult, ALU.add).then_inc(ada_step, 1)

        def ada_reduce(pe, m, g=0):
            pe.wait_ge(ada_step, KD * (m + 1) + KD * 6 * g)
            if m >= 1:
                pe.wait_ge(ada_done, m + 6 * g)
            for i in range(2):
                last = pe.matmul(mod_bank[:, i:i + 1], ada_acc[m % 2][:, P * i:P * i + P], ones[:, 0:1],
                                 start=True, stop=True)
            last.then_inc(ada_reduced, 1)

        def ada_finish(dve, m, g=0):
            dve.wait_ge(ada_reduced, m + 1 + 6 * g)
            at = 2 * (m % 24) + 12 * g
            dve.tensor_tensor(coef[:, m // 24, bass.ds(at, 2)], mod_bank[:, 0:2],
                              vec[:, bass.ds(V_ADAB + 48 * (m // 24) + at, 2)], ALU.add).then_inc(ada_done, 1)

        def gain(l, s):
            return vec[:, V_SW + 8 * (4 * l + s):V_SW + 8 * (4 * l + s) + 8]

        def section(l, s):
            return coef[:, l, 8 * s:8 * s + 8]

        mla_tables = root.enter_context(ExitStack())
        low_stack = ExitStack()
        cos_t = sb(mla_tables, "cos_t", [P, SEQ], side="right")
        sin_t = sb(mla_tables, "sin_t", [P, SEQ], side="right")
        with ExitStack() as st:
            v1 = sb(st, "v1", [N_V1, P])
            v2 = sb(st, "v2", [64, P])
            v3 = sb(st, "v3", [96, P])
            pos_i = sb(st, "pos_i", [P, SEQ], I32)
            ang = sb(st, "ang", [P, SEQ])
            turns = sb(st, "turns", [P, SEQ])
            wrap = sb(st, "wrap", [P, SEQ])
            x_tok = y[:].rearrange("p k t -> p (k t)").rearrange("p (t d) -> p t d", t=TT)
            const_in, vec_in, x_in, pos_in = sem("const_in"), sem("vec_in"), sem("x_in"), sem("pos_in")
            v_turned, x_turned, x_copied, vec_copied = sem("v_turned"), sem("x_turned"), sem("x_copied"), sem("vec_copied")
            ones_set, angle_step, sin_done = sem("ones_set"), sem("angle_step"), sem("sin_done")
            with nc.Block() as block:
                @block.sync
                def _(sp):
                    sp.dma_start(const[:], a["const"]).then_inc(const_in, 16)
                    for dst, src in ((v1[0:96, :], a["ada_b"].rearrange("l (k p) -> (l k) p", p=P)),
                                     (v1[96:104, :], a["c"].rearrange("b (k p) -> (b k) p", p=P)),
                                     (v1[104:107, :], a["mla_q_norm_g"].rearrange("b (k p) -> (b k) p", p=P)),
                                     (v1[107:109, :], a["mla_kv_norm_g"].rearrange("b (k p) -> (b k) p", p=P)),
                                     (v1[109:110, :], a["gdn_out_norm_g"]),
                                     (v2[:], a["sandwich_g"].rearrange("l s (k p) -> (l s k) p", p=P)),
                                     (v3[:], a["gdn_conv_w"].rearrange("b j (k p) -> (b j k) p", p=P))):
                        sp.dma_start(dst, src).then_inc(vec_in, 16)
                    sp.dma_start(x_tok, a["x"][0].rearrange("(t p) d -> p t d", p=P)).then_inc(x_in, 16)
                    sp.dma_start(pos_i[:], a["positions"].to_broadcast([P, SEQ])).then_inc(pos_in, 16)
                    load_ada(sp, 0)
                    load_ada(sp, 1)
                    load_weights(sp, 0, src_of(0))
                    load_weights(sp, 1, src_of(1))

                @block.gpsimd
                def _(pool):
                    pool.memset(ones[:], 1.0).then_inc(ones_set, 1)

                @block.tensor
                def _(pe):
                    pe.wait_ge(const_in, 16)
                    pe.wait_ge(vec_in, 7 * 16)
                    for v, n, at in ((v1, N_V1, 0), (v2, 64, V_SW), (v3, 96, V_CONV)):
                        last = pe.transpose(bank[5][:, at:at + n], v[:], ident[0:n, 0:n])
                    last.then_inc(v_turned, 1)
                    pe.wait_ge(x_in, 16)
                    for k in range(KD):
                        if k >= 4:
                            pe.wait_ge(x_copied, k - 3)
                        for t in range(TT):
                            last = pe.transpose(bank[k % 4][:, P * t:P * t + P], x_tok[:, t, P * k:P * k + P], ident)
                        last.then_inc(x_turned, 1)

                @block.scalar
                def _(act):
                    act.wait_ge(v_turned, 1)
                    act.activation(vec[:], bank[5][:, 0:N_VEC], ACT.Copy).then_inc(vec_copied, 1)
                    act.wait_ge(vec_copied, 1)
                    act.activation(c_act[:], vec[:, V_C:V_C + KD], ACT.Silu)
                    for k in range(KD):
                        act.wait_ge(x_turned, k + 1)
                        act.activation(x[:, k], bank[k % 4][:], ACT.Copy).then_inc(x_copied, 1)
                    act.wait_ge(angle_step, 12)
                    act.activation(sin_t[:], ang[:], ACT.Sin, scale=const[:, C_SIGN:C_SIGN + 1]).then_inc(sin_done, 1)
                    act.wait_ge(angle_step, 16)
                    act.activation(cos_t[:], wrap[:], ACT.Sin)

                @block.vector
                def _(dve):
                    def step(ins, n):
                        ins.then_inc(angle_step, 1)
                        dve.wait_ge(angle_step, n)
                    two_pi = 2 * np.pi
                    p1 = 6.28125
                    p2 = float(np.float32(int((two_pi - p1) * 2 ** 19) / 2 ** 19))
                    p3 = float(two_pi - p1 - p2)
                    limit = 3.1415925
                    dve.wait_ge(pos_in, 16)
                    dve.wait_ge(const_in, 16)
                    step(dve.tensor_copy(ang[:], pos_i[:]), 1)
                    step(dve.tensor_scalar(ang[:], ang[:], const[:, C_FREQ:C_FREQ + 1], None, ALU.mult), 2)
                    step(dve.tensor_scalar(turns[:], ang[:], 1 / two_pi, 12582912.0, ALU.mult, ALU.add), 3)
                    step(dve.tensor_scalar(turns[:], turns[:], -12582912.0, None, ALU.add), 4)
                    for n, part in ((5, p1), (6, p2)):
                        step(dve.scalar_tensor_tensor(ang[:], turns[:], -part, ang[:], ALU.mult, ALU.add), n)
                    step(dve.scalar_tensor_tensor(ang[:], turns[:], -p3, ang[:], ALU.mult, ALU.add), 7)
                    step(dve.tensor_scalar(wrap[:], ang[:], np.pi / 2, None, ALU.add), 8)
                    for n, r in ((9, ang), (13, wrap)):
                        step(dve.tensor_scalar(turns[:], r[:], 1 / two_pi, 12582912.0, ALU.mult, ALU.add), n)
                        step(dve.tensor_scalar(turns[:], turns[:], -12582912.0, None, ALU.add), n + 1)
                        step(dve.scalar_tensor_tensor(r[:], turns[:], -two_pi, r[:], ALU.mult, ALU.add), n + 2)
                        step(dve.tensor_scalar(r[:], r[:], limit, -limit, ALU.min, ALU.max), n + 3)

        def square_tiles(act, src, n, name, b=0):
            for k in range(n):
                if k >= 2:
                    act.wait_ge(sem(name + "_summed"), n * b + k - 1)
                act.activation(sq[k % 2][:], src[:, k], ACT.Square).then_inc(sem(name + "_squared"), 1)

        def sum_tiles(pe, n, name, b=0, ps=None):
            for k in range(n):
                sum_tile(pe, k, n, name, b, ps or sum_bank)

        def sum_tile(pe, k, n, name, b, ps):
            pe.wait_ge(sem(name + "_squared"), n * b + k + 1)
            for t in range(TT):
                last = pe.matmul(ps[:, t:t + 1], sq[k % 2][:, P * t:P * t + P], ones[:, 0:1],
                                 start=k == 0 and t == 0, stop=k == n - 1, skip_group_check=True)
            last.then_inc(sem(name + "_summed"), 1)

        def root_of_mean(act, n, name, scale, b=0, ps=None):
            ps = ps or sum_bank
            act.wait_ge(sem(name + "_summed"), n * (b + 1))
            act.activation(rms_tok[:, 0:TT], ps[:, 0:TT], ACT.Sqrt, bias=bias_t[:, 0:1], scale=scale).then_inc(sem(name + "_root"), 1)

        def inverse_of_root(dve, name, b=0):
            dve.wait_ge(sem(name + "_root"), b + 1)
            dve.reciprocal(rms_tok[:, TT:2 * TT], rms_tok[:, 0:TT]).then_inc(sem(name + "_inv"), 1)

        def spread(pe, name, b=0, ps=None):
            ps = ps or sum_bank
            pe.wait_ge(sem(name + "_inv"), b + 1)
            for t in range(TT):
                last = pe.matmul(ps[:, P * t:P * t + P], rms_tok[:, TT + t:TT + t + 1].to_broadcast([P, P]), ident,
                                 start=True, stop=True)
            last.then_inc(sem(name + "_spread"), 1)

        xr_ready, hf_ready, h_hi_ready, h_lo_ready = sem("xr_ready"), sem("hf_ready"), sem("h_hi_ready"), sem("h_lo_ready")

        def scale_h(dve, b, inv_rms, hf, xr, h_hi, h_lo):
            for k in range(KD):
                if k >= 2:
                    dve.wait_ge(hf_ready, KD * b + k - 1)
                dve.tensor_tensor(xr[k % 2][:], x[:, k], inv_rms[:], ALU.mult).then_inc(xr_ready, 1)
                if k >= 1:
                    rest_h(dve, b, k - 1, hf, h_hi, h_lo)
            rest_h(dve, b, KD - 1, hf, h_hi, h_lo)

        def rest_h(dve, b, k, hf, h_hi, h_lo):
            dve.wait_ge(h_hi_ready, KD * b + k + 1)
            dve.tensor_tensor(h_lo[:, k], hf[k % 2][:], h_hi[:, k].bitcast(F32), ALU.subtract).then_inc(h_lo_ready, 1)

        def modulate_h(act, b, l, s, hf, xr, h_hi):
            fac, shift = section(l, s + 1), section(l, s)
            for k in range(KD):
                act.wait_ge(xr_ready, KD * b + k + 1)
                if k >= 2:
                    act.wait_ge(h_lo_ready, KD * b + k - 1)
                act.activation(hf[k % 2][:], xr[k % 2][:], ACT.Identity, bias=shift[:, k:k + 1],
                               scale=fac[:, k:k + 1]).then_inc(hf_ready, 1)
                act.wait_ge(hf_ready, KD * b + k + 1)
                act.activation(h_hi[:, k], hf[k % 2][:], ACT.Copy).then_inc(h_hi_ready, 1)

        yr_ready, x_new, factors_ready = sem("yr_ready"), sem("x_new"), sem("factors_ready")

        ADDS = KD - 1

        def square_y(act, b, t, src):
            if t >= 2:
                act.wait_ge(sem("edge_y_added"), ADDS * b + t - 1)
            act.activation(sq[min(t, 1)][:], src, ACT.Square).then_inc(sem("edge_y_squared"), 1)

        def add_squares(pool, name, b, slots):
            for k in range(1, KD):
                pool.wait_ge(sem(name + "_squared"), KD * b + k + 1)
                if k >= 2:
                    pool.wait_ge(sem(name + "_added"), ADDS * b + k - 1)
                pool.tensor_tensor(sq[0][:], sq[0][:], slots[(k - 1) % len(slots)][:], ALU.add).then_inc(sem(name + "_added"), 1)

        def sum_added(pe, name, b, ps):
            pe.wait_ge(sem(name + "_added"), ADDS * (b + 1))
            for t in range(TT):
                last = pe.matmul(ps[:, t:t + 1], sq[0][:, P * t:P * t + P], ones[:, 0:1], start=True, stop=True)
            last.then_inc(sem(name + "_summed"), 1)

        def edge_pe(pe, b, nxt):
            sum_added(pe, "edge_y", b, sum_bank)
            spread(pe, "edge_y", b)
            if nxt:
                sum_added(pe, "edge_x", b, mod_bank)
                spread(pe, "edge_x", b, mod_bank)

        def edge_pool(pool, b, hf):
            add_squares(pool, "edge_x", b, (sq[1], hf[0]))

        def edge_act(act, b, nxt, hf, xr, h_hi, n_round=None):
            root_of_mean(act, 1, "edge_y", 1 / D, b)
            if nxt:
                round_weights(act, n_round)
                for k in range(KD):
                    act.wait_ge(x_new, KD * b + k + 1)
                    if k >= 3:
                        act.wait_ge(sem("edge_x_added"), ADDS * b + k - 2)
                    slot = sq[0] if k == 0 else (sq[1], hf[0])[(k - 1) % 2]
                    act.activation(slot[:], x[:, k], ACT.Square).then_inc(sem("edge_x_squared"), 1)
                root_of_mean(act, 1, "edge_x", 1 / D, b, mod_bank)
                modulate_h(act, b + 1, *nxt, hf, xr, h_hi)

        def edge_dve(dve, b, gate, nxt, hf, xr, h_hi, h_lo, n_round=None):
            l, s = gate
            g_fac = section(l, s)
            dve.tensor_tensor(g_fac, g_fac, gain(l, 1 if s == 2 else 3), ALU.mult).then_inc(factors_ready, 1)
            if nxt:
                nl, ns = nxt
                dve.scalar_tensor_tensor(section(nl, ns + 1), section(nl, ns + 1), 1.0,
                                         gain(nl, 0 if ns == 0 else 2), ALU.add, ALU.mult).then_inc(factors_ready, 1)
            dve.wait_ge(factors_ready, 1 + 2 * b + (2 if nxt else 1))
            inverse_of_root(dve, "edge_y", b)
            dve.wait_ge(sem("edge_y_spread"), b + 1)
            for k in range(KD + 1):
                if k < KD:
                    if k >= 2:
                        dve.wait_ge(x_new, KD * b + k - 1)
                    dve.scalar_tensor_tensor(xr[k % 2][:], y[:, k], g_fac[:, k:k + 1], sum_bank[:],
                                             ALU.mult, ALU.mult).then_inc(yr_ready, 1)
                if k:
                    dve.wait_ge(yr_ready, KD * b + k)
                    dve.tensor_tensor(x[:, k - 1], x[:, k - 1], xr[(k - 1) % 2][:], ALU.add).then_inc(x_new, 1)
            dve.wait_ge(x_new, KD * (b + 1))
            if nxt:
                rest_weights(dve, n_round)
                inverse_of_root(dve, "edge_x", b)
                dve.wait_ge(sem("edge_x_spread"), b + 1)
                scale_h(dve, b + 1, mod_bank, hf, xr, h_hi, h_lo)

        mla_keep = ExitStack()
        v_tok = sb(mla_keep, "v_tok", [P, TT, HEADS * P])
        k_rope = sb(mla_keep, "k_rope", [P, SEQ])
        low_hi = sb(low_stack, "low_hi", [P, KQ + KKV, SEQ], F32R, side="right")
        low_lo = sb(low_stack, "low_lo", [P, KQ + KKV, SEQ], F32R, side="right")
        rope_t = [sb(low_stack, f"rope_t{i}", [P, SEQ], side="right") for i in range(2)]
        h_stack = ExitStack()
        h_hi = sb(h_stack, "h_hi_mla", [P, KD, SEQ], F32R)
        h_lo = sb(h_stack, "h_lo_mla", [P, KD, SEQ], F32R)
        with ExitStack() as st, nc.Block() as block:
            hf = [y[:, i] for i in range(2)]
            xr = [y[:, 2 + i] for i in range(2)]

            @block.sync
            def _(sp):
                for m in range(8):
                    load_ada(sp, m + 2)

            @block.tensor
            def _(pe):
                sum_tiles(pe, KD, "first_x")
                spread(pe, "first_x")
                for m in range(8):
                    ada_reduce(pe, m)

            @block.scalar
            def _(act):
                act.wait_ge(sem("eps_set"), 2)
                square_tiles(act, x, KD, "first_x")
                root_of_mean(act, KD, "first_x", 1 / D)
                round_weights(act, 0)
                act.wait_ge(factors_ready, 1)
                modulate_h(act, 0, 0, 0, hf, xr, h_hi)

            @block.vector
            def _(dve):
                dve.memset(bias_t[:, 0:1], EPS).then_inc(sem("eps_set"), 1)
                dve.memset(bias_t[:, 1:2], P * EPS).then_inc(sem("eps_set"), 1)
                inverse_of_root(dve, "first_x")
                for m in range(8):
                    ada_multiply(dve, m)
                    if m >= 1:
                        ada_finish(dve, m - 1)
                ada_finish(dve, 7)
                rest_weights(dve, 0)
                dve.wait_ge(ada_done, 8)
                dve.scalar_tensor_tensor(section(0, 1), section(0, 1), 1.0, gain(0, 0), ALU.add,
                                         ALU.mult).then_inc(factors_ready, 1)
                dve.wait_ge(sem("first_x_spread"), 1)
                scale_h(dve, 0, sum_bank, hf, xr, h_hi, h_lo)

        low_f = ExitStack()
        low = sb(low_f, "low", [P, KQ + KKV, SEQ])
        low_copied, krope_step = sem("low_copied"), sem("krope_step")

        def rope_dve(dve, ps, dst, base, first_wait, done):
            t0, t1 = rope_t[0][:], rope_t[1][:]
            for b in range(4):
                lo, hi = 32 * b, 32 * (b ^ 1)
                dve.tensor_copy(t1[lo:lo + 32, :], ps[hi:hi + 32, :]).then_inc(done, 1)
            dve.tensor_tensor(t0, ps, cos_t[:], ALU.mult).then_inc(done, 1)
            dve.wait_ge(done, base + 5)
            dve.tensor_tensor(t1, t1, sin_t[:], ALU.mult).then_inc(done, 1)
            dve.wait_ge(done, base + 6)
            dve.tensor_tensor(dst, t0, t1, ALU.add).then_inc(done, 1)
            dve.wait_ge(done, base + 7)

        with nc.Block() as block:
            @block.sync
            def _(sp):
                for n in range(N_IN, N_UQ):
                    load_weights(sp, n + 2, src_of(n + 2))
                    load_ada(sp, n + 10)

            @block.tensor
            def _(pe):
                for n in range(N_IN, N_UQ):
                    pe.wait_ge(w_lo_ready, n + 1)
                    hi, lo = w_views(n, KD)
                    for i in range(2):
                        t = 2 * n + i
                        cols = [v[:, :, P * i:P * i + P] for v in (hi, lo)]
                        if t >= 4:
                            pe.wait_ge(low_copied, t - 3)
                        for k in range(KD):
                            last = product(pe, bank[t % 4][:], cols[0][:, k], cols[1][:, k], h_hi[:, k], h_lo[:, k],
                                           k == 0, k == KD - 1)
                        last.then_inc(tile_done, 1)
                    ada_reduce(pe, n + 8)
                sum_tiles(pe, KQ, "cq")
                spread(pe, "cq")
                sum_tiles(pe, KKV, "ckv", 0, bank[5])
                spread(pe, "ckv", 0, bank[5])

            @block.scalar
            def _(act):
                for n in range(N_IN, N_UQ):
                    round_weights(act, n + 1)
                    for t in range(2 * n, min(2 * n + 2, KQ + KKV)):
                        act.wait_ge(tile_done, t + 1)
                        act.activation(low[:, t], bank[t % 4][:], ACT.Copy).then_inc(low_copied, 1)
                act.wait_ge(low_copied, KQ + KKV)
                square_tiles(act, low[:, 0:KQ], KQ, "cq")
                root_of_mean(act, KQ, "cq", 1 / Q_LORA)
                for k in range(KKV):
                    act.wait_ge(sem("cq_summed"), KQ)
                    act.activation(sq[k % 2][:], low[:, KQ + k], ACT.Square).then_inc(sem("ckv_squared"), 1)
                act.wait_ge(sem("cq_inv"), 1)
                root_of_mean(act, KKV, "ckv", 1 / KV_LORA, 0, bank[5])
                for k in range(KQ + KKV):
                    act.wait_ge(sem("low_scaled"), k + 1)
                    act.activation(low_hi[:, k], low[:, k], ACT.Copy).then_inc(sem("low_hi_ready"), 1)

            @block.vector
            def _(dve):
                for n in range(N_IN, N_UQ):
                    rest_weights(dve, n + 1)
                    ada_multiply(dve, n + 8)
                    ada_finish(dve, n + 8)
                dve.wait_ge(tile_done, 6)
                rope_dve(dve, bank[1][:], k_rope[:], 0, None, krope_step)
                for name, at, n in (("cq", 0, KQ), ("ckv", KQ, KKV)):
                    if at:
                        dve.wait_ge(sem("cq_spread"), 1)
                    inverse_of_root(dve, name)
                    dve.wait_ge(sem(name + "_spread"), 1)
                    for k in range(at, at + n):
                        g = vec[:, V_QN + k:V_QN + k + 1]
                        inv_rms = sum_bank if name == "cq" else bank[5]
                        dve.scalar_tensor_tensor(low[:, k], low[:, k], g, inv_rms[:], ALU.mult,
                                                 ALU.mult).then_inc(sem("low_scaled"), 1)
                for k in range(KQ + KKV):
                    dve.wait_ge(sem("low_hi_ready"), k + 1)
                    dve.tensor_tensor(low_lo[:, k], low[:, k], low_hi[:, k].bitcast(F32), ALU.subtract)
        low_f.close()
        h_stack.close()

        q_stack = ExitStack()
        q_nope = sb(q_stack, "q_nope", [P, HEADS, SEQ])
        q_rope = sb(q_stack, "q_rope", [P, HEADS // 2, SEQ])
        k_nope = y
        up_copied, qrope_step = sem("up_copied"), sem("qrope_step")
        UP0 = 6
        with nc.Block() as block:
            def copies_before(n, i):
                return 2 * (n - N_UQ) + i if n < N_UKV else 8 + 8 * (n - N_UKV) + i

            def up_bank(n, i):
                return bank[4 + (n - N_UQ) % 2] if n < N_UKV and i == 2 else bank[copies_before(n, i) % 4]

            @block.sync
            def _(sp):
                for n in range(N_UQ, N_WO):
                    load_weights(sp, n + 2, src_of(n + 2))
                    load_ada(sp, n + 10)

            @block.tensor
            def _(pe):
                for n in range(N_UQ, N_WO):
                    pe.wait_ge(w_lo_ready, n + 1)
                    if n < N_UKV:
                        hi, lo = w_views(n, KQ)
                        for i in range(3):
                            if i < 2:
                                if copies_before(n, i) >= 4:
                                    pe.wait_ge(up_copied, copies_before(n, i) - 3)
                            else:
                                if n - N_UQ >= 2:
                                    pe.wait_ge(qrope_step, 7 * (n - N_UQ - 1))
                            cols = [v[:, :, P * i:P * i + P] for v in (hi, lo)]
                            for k in range(KQ):
                                last = product(pe, up_bank(n, i)[:], cols[0][:, k], cols[1][:, k], low_hi[:, k],
                                               low_lo[:, k], k == 0, k == KQ - 1)
                            last.then_inc(tile_done, 1)
                    else:
                        hi, lo = (v.rearrange("p k (h c) -> p k h c", h=4) for v in w_views(n, KKV))
                        for i in range(8):
                            pe.wait_ge(up_copied, copies_before(n, i) - 3)
                            for k in range(KKV):
                                ps = up_bank(n, i)[:]
                                kv = KQ + k
                                if i < 4:
                                    last = product(pe, ps, hi[:, k, i, 0:NOPE], lo[:, k, i, 0:NOPE], low_hi[:, kv],
                                                   low_lo[:, kv], k == 0, k == KKV - 1)
                                else:
                                    tok = slice(P * (i - 4), P * (i - 3))
                                    last = product(pe, ps, low_hi[:, kv, tok], low_lo[:, kv, tok], hi[:, k, :, NOPE:],
                                                   lo[:, k, :, NOPE:], k == 0, k == KKV - 1)
                            last.then_inc(tile_done, 1)
                    ada_reduce(pe, n + 8)

            @block.scalar
            def _(act):
                for n in range(N_UQ, N_WO):
                    round_weights(act, n + 1)
                    for i in range(2 if n < N_UKV else 8):
                        act.wait_ge(tile_done, tiles_to[n] + i + 1)
                        if n < N_UKV:
                            dst = q_nope[:, 2 * (n - N_UQ) + i]
                        elif i < 4:
                            dst = k_nope[:, 4 * (n - N_UKV) + i]
                        else:
                            dst = v_tok[:, i - 4, 512 * (n - N_UKV):512 * (n - N_UKV + 1)]
                        act.activation(dst, up_bank(n, i)[:], ACT.Copy).then_inc(up_copied, 1)

            @block.vector
            def _(dve):
                for n in range(N_UQ, N_WO):
                    rest_weights(dve, n + 1)
                    ada_multiply(dve, n + 8)
                    if n < N_UKV:
                        dve.wait_ge(tile_done, tiles_to[n] + 3)
                        rope_dve(dve, up_bank(n, 2)[:], q_rope[:, n - N_UQ], 7 * (n - N_UQ), None, qrope_step)
                    ada_finish(dve, n + 8)
        low_stack.close()
        mla_tables.close()

        o_stack = ExitStack()
        o_hi = sb(o_stack, "o_hi_mla", [P, HEADS, SEQ], F32R, side="right")
        o_lo = sb(o_stack, "o_lo_mla", [P, HEADS, SEQ], F32R, side="right")
        with ExitStack() as st, nc.Block() as block:
            prob = [sb(st, f"prob{i}", [P, SEQ]) for i in range(3)]
            prob_t = [sb(st, f"prob_t{i}", [P, SEQ]) for i in range(3)]
            stat = [sb(st, f"stat{i}", [P, 4]) for i in range(4)]
            scores_ready, peak, bias_ready, exp_done = sem("scores_ready"), sem("peak"), sem("bias_ready"), sem("exp_done")
            inv_ready, prob_ready, turned, turned_copied = sem("inv_ready"), sem("prob_ready"), sem("turned"), sem("turned_copied")
            valued, o_rounded, o_rest = sem("valued"), sem("o_rounded"), sem("o_rest")
            items = [(h, b) for h in range(HEADS) for b in range(TT)]
            N = len(items)
            score_bank = (bank[0], bank[1], bank[6])
            TURN_LAG, COPY_LAG, VALUE_LAG = 2, 3, 4

            @block.tensor
            def _(pe):
                def scores(i):
                    h, b = items[i]
                    if i >= 3:
                        pe.wait_ge(exp_done, i - 2)
                    into = score_bank[i % 3]
                    ps, keys, qs = into[:, 0:P * (b + 1)], slice(0, P * (b + 1)), slice(P * b, P * b + P)
                    r = ROPE * (h % 2)
                    pe.matmul(ps, q_nope[:, h, qs], k_nope[:, h, keys], start=True, stop=False)
                    pe.matmul(ps, q_rope[r:r + ROPE, h // 2, qs], k_rope[r:r + ROPE, keys], start=False, stop=True)
                    pe.matmul(into[:, P * b:P * b + P], const[0:1, C_EARLY:C_EARLY + P],
                              const[0:1, C_LATE:C_LATE + P], start=False, stop=True,
                              skip_group_check=True).then_inc(scores_ready, 1)

                def turn(i):
                    b = items[i][1]
                    pe.wait_ge(prob_ready, i + 1)
                    if i >= 2:
                        pe.wait_ge(turned_copied, i - 1)
                    for j in range(b + 1):
                        last = pe.transpose(bank[2 + i % 2][:, P * j:P * j + P], prob[i % 3][:, P * j:P * j + P], ident)
                    last.then_inc(turned, 1)

                def values(i):
                    h, b = items[i]
                    pe.wait_ge(turned_copied, i + 1)
                    if h >= 2 and b == 0:
                        pe.wait_ge(o_rest, h - 1)
                    for j in range(b + 1):
                        last = pe.matmul(bank[4 + h % 2][:, P * b:P * b + P], v_tok[:, j, P * h:P * h + P],
                                         prob_t[i % 3][:, P * j:P * j + P], start=j == 0, stop=j == b)
                    last.then_inc(valued, 1)

                for i in range(N + VALUE_LAG):
                    if i < N:
                        scores(i)
                    if TURN_LAG <= i < N + TURN_LAG:
                        turn(i - TURN_LAG)
                    if i >= VALUE_LAG:
                        values(i - VALUE_LAG)

            @block.vector
            def _(dve):
                def row_peak(i):
                    s, b = stat[i % 4], items[i][1]
                    dve.wait_ge(scores_ready, i + 1)
                    dve.reduce_max(s[:, 0:1], score_bank[i % 3][:, 0:P * (b + 1)], AX.X).then_inc(peak, 1)
                    dve.wait_ge(peak, i + 1)
                    dve.tensor_scalar(s[:, 1:2], s[:, 0:1], -ATT_SCALE, None, ALU.mult).then_inc(bias_ready, 1)

                def divide(i):
                    s, p = stat[i % 4], prob[i % 3][:, 0:P * (items[i][1] + 1)]
                    dve.wait_ge(exp_done, i + 1)
                    dve.reciprocal(s[:, 3:4], s[:, 2:3]).then_inc(inv_ready, 1)
                    dve.wait_ge(inv_ready, i + 1)
                    dve.tensor_scalar(p, p, s[:, 3:4], None, ALU.mult).then_inc(prob_ready, 1)

                def copy_turned(i):
                    cols = slice(0, P * (items[i][1] + 1))
                    dve.wait_ge(turned, i + 1)
                    if i >= 3:
                        dve.wait_ge(valued, i - 2)
                    dve.tensor_copy(prob_t[i % 3][:, cols], bank[2 + i % 2][:, cols]).then_inc(turned_copied, 1)

                def rest_of_head(h):
                    dve.wait_ge(o_rounded, h + 1)
                    dve.tensor_tensor(o_lo[:, h], bank[4 + h % 2][:], o_hi[:, h].bitcast(F32),
                                      ALU.subtract).then_inc(o_rest, 1)

                for i in range(N + COPY_LAG):
                    if i < N:
                        row_peak(i)
                    if 1 <= i <= N:
                        divide(i - 1)
                    if i >= COPY_LAG:
                        copy_turned(i - COPY_LAG)
                    if i >= 10 and i % TT == 2:
                        rest_of_head((i - 10) // TT)
                for h in range((N + COPY_LAG - 11) // TT + 1, HEADS):
                    rest_of_head(h)

            @block.scalar
            def _(act):
                def round_head(h):
                    act.wait_ge(valued, TT * (h + 1))
                    act.activation(o_hi[:, h], bank[4 + h % 2][:], ACT.Copy).then_inc(o_rounded, 1)

                for i in range(N):
                    s, b = stat[i % 4], items[i][1]
                    act.wait_ge(bias_ready, i + 1)
                    if i >= 3:
                        act.wait_ge(turned, i - 2)
                    act.activation(prob[i % 3][:, 0:P * (b + 1)], score_bank[i % 3][:, 0:P * (b + 1)], ACT.Exp,
                                   bias=s[:, 1:2], scale=ATT_SCALE, accum_out=s[:, 2:3]).then_inc(exp_done, 1)
                    if i >= 9 and i % TT == 1:
                        round_head((i - 9) // TT)
                for h in range((N - 10) // TT + 1, HEADS):
                    round_head(h)
        q_stack.close()
        mla_keep.close()

        def out_projection(name, n0, s_hi, s_lo, ada_at, edge):
            copied = sem(name + "_copied")
            with nc.Block() as block:
                @block.sync
                def _(sp):
                    for n in range(n0, n0 + 4):
                        load_weights(sp, n + 2, src_of(n + 2))
                        for m in ada_at[n - n0]:
                            if m + 2 < 48:
                                load_ada(sp, m + 2)

                @block.tensor
                def _(pe):
                    for n in range(n0, n0 + 4):
                        pe.wait_ge(w_lo_ready, n + 1)
                        hi, lo = w_views(n, KD)
                        for i in range(2):
                            t = 2 * (n - n0) + i
                            if t >= 4:
                                pe.wait_ge(copied, t - 3)
                            for k in range(KD):
                                last = product(pe, bank[t % 4][:], hi[:, k, P * i:P * i + P], lo[:, k, P * i:P * i + P],
                                               s_hi[:, k], s_lo[:, k], k == 0, k == KD - 1)
                            last.then_inc(tile_done, 1)
                        for m in ada_at[n - n0]:
                            ada_reduce(pe, m)

                @block.gpsimd
                def _(pool):
                    add_squares(pool, "edge_y", edge, (sq[1],))

                @block.scalar
                def _(act):
                    for n in range(n0, n0 + 4):
                        round_weights(act, n + 1)
                        for i in range(2):
                            t = 2 * (n - n0) + i
                            act.wait_ge(tile_done, tiles_to[n0] + t + 1)
                            square_y(act, edge, t, bank[t % 4][:])
                            act.activation(y[:, t], bank[t % 4][:], ACT.Copy).then_inc(copied, 1)

                @block.vector
                def _(dve):
                    for n in range(n0, n0 + 4):
                        rest_weights(dve, n + 1)
                        for m in ada_at[n - n0]:
                            ada_multiply(dve, m)
                            ada_finish(dve, m)

        out_projection("mla_o", N_WO, o_hi, o_lo, [[17, 18], [19, 20], [21, 22], [23]], 0)
        o_stack.close()

        def mlp(name, l, n0, f_hi, f_lo, with_ada):
            edge = 2 * l
            u_stack = ExitStack()
            u_hi = sb(u_stack, name + "_u_hi", [P, 8, SEQ], F32R, side="right")
            u_lo = sb(u_stack, name + "_u_lo", [P, 8, SEQ], F32R, side="right")
            relu = [sb(u_stack, f"{name}_relu{i}", [P, SEQ], side="right") for i in range(2)]
            usq = [sb(u_stack, f"{name}_usq{i}", [P, SEQ], side="right") for i in range(2)]
            relu_done, u_rounded, u_squared = sem("relu_done"), sem("u_rounded"), sem("u_squared")
            u_rest, y_added = sem("u_rest"), sem("y_added")
            u0, y0 = 32 * l, 34 * l
            t0 = tiles_to[n0]

            def groups(eng, body):
                with eng.Fori(0, 3) as g:
                    body(g, False)
                body(3, True)

            with nc.Block() as block:
                @block.sync
                def _(sp):
                    def body(g, final):
                        for j in range(8):
                            if not final:
                                jj = (j + 2) % 8
                                load_weights(sp, n0 + j + 2, ffn_src(l, jj, g + (j + 2) // 8), g)
                            elif n0 + 24 + j + 2 < N_END:
                                load_weights(sp, n0 + 24 + j + 2, src_of(n0 + 24 + j + 2))
                            if with_ada and j < 6 and not (final and j >= 4):
                                load_ada(sp, 24 + j + 2, g)
                    groups(sp, body)

                @block.tensor
                def _(pe):
                    edge_pe(pe, edge, True)

                    def body(g, final):
                        for j in range(8):
                            n = n0 + j
                            pe.wait_ge(w_lo_ready, n + 1 + 8 * g)
                            hi, lo = w_views(n, KD)
                            if j == 0:
                                for k in range(KD):
                                    pe.wait_ge(h_lo_ready, KD * (edge + 1) + k + 1)
                                    for i in range(2):
                                        last = product(pe, bank[i][:], hi[:, k, P * i:P * i + P],
                                                       lo[:, k, P * i:P * i + P], f_hi[:, k], f_lo[:, k],
                                                       k == 0, k == KD - 1)
                                        if k == KD - 1:
                                            last.then_inc(tile_done, 1)
                            for i in range(2 if j else 0):
                                t = 2 * j + i
                                if j < 4:
                                    if t >= 4:
                                        pe.wait_ge(relu_done, u0 + t - 3 + 8 * g)
                                    ps, m_hi, m_lo = bank[t % 4][:], f_hi, f_lo
                                else:
                                    pe.wait_ge(y_added, y0 + t - 7 + 8 * g)
                                    ps, m_hi, m_lo = bank[4 + t % 2][:], u_hi, u_lo
                                for k in range(KD):
                                    if t == 8:
                                        pe.wait_ge(u_rest, u0 + k + 1 + 8 * g)
                                    last = product(pe, ps, hi[:, k, P * i:P * i + P], lo[:, k, P * i:P * i + P],
                                                   m_hi[:, k], m_lo[:, k], k == 0, k == KD - 1)
                                last.then_inc(tile_done, 1)
                                if with_ada and j < 7 and i == 0:
                                    ada_reduce(pe, 24 + j - 1, g)
                    groups(pe, body)

                @block.gpsimd
                def _(pool):
                    edge_pool(pool, edge, usq)
                    for i in range(2):
                        pool.memset(y[:, 4 * i:4 * i + 4], 0.0).then_inc(y_added, 1)
                    add_squares(pool, "edge_y", edge + 1, (sq[1],))

                @block.scalar
                def _(act):
                    edge_act(act, edge, (l, 3), usq, relu, f_hi, n0 + 1)

                    def body(g, final):
                        for j in range(8):
                            for i in range(2 if j < 4 else 0):
                                t = 2 * j + i
                                act.wait_ge(tile_done, t0 + t + 1 + 16 * g)
                                if t >= 2:
                                    act.wait_ge(u_rest, u0 + t - 1 + 8 * g)
                                act.activation(relu[t % 2][:], bank[t % 4][:], ACT.Relu).then_inc(relu_done, 1)
                                act.wait_ge(relu_done, u0 + t + 1 + 8 * g)
                                act.activation(u_hi[:, t], relu[t % 2][:], ACT.Square).then_inc(u_rounded, 1)
                            for t in range(2 * j - 8, 2 * j - 6) if final and j >= 4 else ():
                                act.wait_ge(y_added, y0 + 2 + 24 + t + 1)
                                square_y(act, edge + 1, t, y[:, t])
                            if not final or (j < 7 and n0 + 24 + j + 2 < N_END):
                                round_weights(act, n0 + j + 2, g)
                    groups(act, body)

                @block.vector
                def _(dve):
                    edge_dve(dve, edge, (l, 2), (l, 3), usq, relu, f_hi, f_lo, n0 + 1)

                    def body(g, final):
                        for j in range(8):
                            if with_ada and j < 6:
                                ada_multiply(dve, 24 + j, g)
                            if j < 4:
                                for i in range(2):
                                    t = 2 * j + i
                                    dve.wait_ge(relu_done, u0 + t + 1 + 8 * g)
                                    dve.tensor_tensor(usq[t % 2][:], relu[t % 2][:], relu[t % 2][:],
                                                      ALU.mult).then_inc(u_squared, 1)
                                    dve.wait_ge(u_squared, u0 + t + 1 + 8 * g)
                                    dve.wait_ge(u_rounded, u0 + t + 1 + 8 * g)
                                    dve.tensor_tensor(u_lo[:, t], usq[t % 2][:], u_hi[:, t].bitcast(F32),
                                                      ALU.subtract).then_inc(u_rest, 1)
                                    if with_ada and j and i == 0:
                                        ada_finish(dve, 24 + j - 1, g)
                            else:
                                for i in range(2):
                                    t = 2 * j + i
                                    dve.wait_ge(tile_done, t0 + t + 1 + 16 * g)
                                    dve.wait_ge(y_added, y0 + t - 6 + 8 * g)
                                    dve.tensor_tensor(y[:, t - 8], y[:, t - 8], bank[4 + t % 2][:],
                                                      ALU.add).then_inc(y_added, 1)
                                    if with_ada and j < 7 and i == 0:
                                        ada_finish(dve, 24 + j - 1, g)
                            if not final or (j < 7 and n0 + 24 + j + 2 < N_END):
                                rest_weights(dve, n0 + j + 2, g)
                    groups(dve, body)
            u_stack.close()

        PAIRS = HEADS // 2
        pre_copied, z_done, conv_step, conv_silu = sem("pre_copied"), sem("z_done"), sem("conv_step"), sem("conv_silu")
        hn_squared, hn_summed, hn_root, hn_inv, hn_spread, hn_scaled = (
            sem("hn_" + v) for v in ("squared", "summed", "root", "inv", "spread", "scaled"))
        names = ("gram", "turned", "kv_used", "diff", "grow_exp", "decay_exp", "core_dve", "off", "w_ready",
                 "w_copied", "step_ready", "stepped", "uw_ready", "uw_copied")
        (gram, turned_kv, kv_used, diff, grow_exp, decay_exp, core_dve, off, w_ready, w_copied, step_ready,
         stepped, uw_ready, uw_copied) = (sem("core_" + v) for v in names)
        scan_ws, scan_new, scan_kv, scan_state = (sem("scan_" + v) for v in ("ws", "new", "kv", "state"))
        on_squared, on_summed, on_root, on_inv, on_spread, on_step, on_hi = (
            sem("on_" + v) for v in ("squared", "summed", "root", "inv", "spread", "step", "hi"))
        N_CH = SEQ // CHUNK
        FILL_FRONT = ((0, 4), (4, 8), (8, 12), (12, 16))
        FILL_W = ((16, 18), (18, 21), (24, 27), (30, 33), (36, 39), (42, 45))
        FILL_STEP = ((18, 18), (21, 24), (27, 30), (33, 36), (39, 42), (45, 48))

        def flat(v):
            return v.rearrange("p t c -> p (t c)")

        def over_tiles(v):
            return v.unsqueeze(1).to_broadcast([P, TT, P])

        def token_scalar(v, h):
            return v[:, :, h:h + 1].to_broadcast([P, TT, P])

        def tiles4(v):
            return v.rearrange("p (t c) -> p t c", t=TT)

        def first_chunk(q):
            return N_GDN + 4 * q

        def proj_bank(q, t):
            return bank[t % 4] if q == 0 else bank[7 - t % 2]

        def stat_bank(q, j):
            return bank[4 + j] if q == 0 else bank[j]

        def hn_sum_cols(q):
            return bank[4][:, 0:4 * TT] if q == 0 else bank[6][:, 0:4 * TT]

        def project(pe, q, steps, h_hi, h_lo):
            for s in steps:
                t, k = s // KD, s % KD
                if k == 0:
                    pe.wait_ge(w_lo_ready, first_chunk(q) + t // 2 + 1)
                    ahead = 4 if q == 0 else 2
                    if q and t == 7:
                        pe.wait_ge(hn_root, 2 * q + 2)
                    if t >= ahead:
                        pe.wait_ge(pre_copied, 6 * q + t - ahead + 1)
                    elif q and t == 1:
                        pe.wait_ge(core_dve, 8 * (q - 1) + 3)
                hi, lo = w_views(first_chunk(q) + t // 2, KD)
                cols = slice(P * (t % 2), P * (t % 2) + P)
                last = product(pe, proj_bank(q, t)[:], hi[:, k, cols], lo[:, k, cols], h_hi[:, k], h_lo[:, k],
                               k == 0, k == KD - 1)
                if k == KD - 1:
                    last.then_inc(tile_done, 1)

        def copy_pre(act, q, t, pre):
            act.wait_ge(tile_done, tiles_to[first_chunk(q)] + t + 1)
            act.wait_ge(conv_step, 2 + 24 * q + (4 * (t - 1) if t >= 2 else 0))
            act.activation(pre[t % 2][:, CONV - 1:], proj_bank(q, t)[:], ACT.Copy).then_inc(pre_copied, 1)

        def silu_conv(act, q, t, dst):
            act.wait_ge(conv_step, 2 + 24 * q + 4 * t + 4)
            act.activation(dst[t], dst[t], ACT.Silu).then_inc(conv_silu, 1)

        def silu_z(act, q, i, z_t):
            act.wait_ge(tile_done, tiles_to[first_chunk(q)] + 6 + i + 1)
            act.activation(z_t[:, i], proj_bank(q, 6 + i)[:], ACT.Silu).then_inc(z_done, 1)

        def convolve(dve, q, t, pre, dst):
            dve.wait_ge(pre_copied, 6 * q + t + 1)
            for j in range(CONV):
                at = V_CONV + 24 * j + 8 * (t // 2) + 2 * q + t % 2
                tap, w = pre[t % 2][:, j:j + SEQ], vec[:, at:at + 1]
                if j == 0:
                    dve.tensor_scalar(dst[t], tap, w, None, ALU.mult).then_inc(conv_step, 1)
                else:
                    dve.wait_ge(conv_step, 2 + 24 * q + 4 * t + j)
                    dve.scalar_tensor_tensor(dst[t], tap, w, dst[t], ALU.mult, ALU.add).then_inc(conv_step, 1)

        def square_head(act, q, j, dst):
            act.wait_ge(conv_silu, 6 * q + 6)
            if j >= 2:
                act.wait_ge(hn_summed, 4 * q + j - 1)
            act.activation(sq[j % 2][:], dst[j], ACT.Square).then_inc(hn_squared, 1)

        def sum_head(pe, q, j):
            pe.wait_ge(hn_squared, 4 * q + j + 1)
            for t in range(TT):
                last = pe.matmul(hn_sum_cols(q)[:, TT * j + t:TT * j + t + 1], sq[j % 2][:, P * t:P * t + P],
                                 ones[:, 0:1], start=True, stop=True)
            last.then_inc(hn_summed, 1)

        def root_heads(act, q, hn_tok):
            act.wait_ge(hn_summed, 4 * q + 4)
            sums = hn_sum_cols(q)
            act.activation(hn_tok[:, 0:2 * TT], sums[:, 0:2 * TT], ACT.Sqrt, bias=bias_t[:, 1:2],
                           scale=float(P)).then_inc(hn_root, 1)
            act.activation(hn_tok[:, 2 * TT:], sums[:, 2 * TT:], ACT.Sqrt, bias=bias_t[:, 0:1]).then_inc(hn_root, 1)

        def invert_heads(dve, q, hn_tok):
            dve.wait_ge(hn_root, 2 * q + 2)
            dve.reciprocal(hn_tok[:], hn_tok[:]).then_inc(hn_inv, 1)

        def spread_heads(pe, q, hn_tok):
            pe.wait_ge(hn_inv, q + 1)
            for j in range(4):
                for t in range(TT):
                    last = pe.matmul(stat_bank(q, j)[:, P * t:P * t + P],
                                     hn_tok[:, TT * j + t:TT * j + t + 1].to_broadcast([P, P]), ident,
                                     start=True, stop=True)
                last.then_inc(hn_spread, 1)

        def scale_heads(dve, q, dst):
            for j in range(4):
                dve.wait_ge(hn_spread, 4 * q + j + 1)
                dve.tensor_tensor(dst[j], dst[j], stat_bank(q, j)[:], ALU.mult)

        def gdn_pair(pair, h_hi, h_lo, g_, g_cum, beta, beta_eg, to_end, end_decay, state, v_new, sets, pre, hn_tok, core):
            q = pair + 1
            more = q < PAIRS
            n_next = first_chunk(q)
            mine = sets[pair % 2]
            q_t, k_t, v_t, z_t = (mine[:, 2 * i:2 * i + 2] for i in range(4))
            other = sets[q % 2]
            dst = [other[:, i] for i in range(6)]
            z_next = other[:, 6:8]
            heads = (2 * pair, 2 * pair + 1)
            kbg, k_end, v_beta, decay, a_qk, l_t, inv_t = core
            w_t, u_tok, l_off = kbg, v_beta, decay
            prod, inv = (v.rearrange("p i (t c) -> p i t c", t=TT) for v in (k_t, v_t))
            grow = inv_t

            with nc.Block() as block:
                @block.sync
                def _(sp):
                    for n in range(n_next, n_next + 3) if more else ():
                        load_weights(sp, n + 2, src_of(n + 2))

                @block.tensor
                def _(pe):
                    def rows_of(i, ps, col):
                        for t in range(TT):
                            last = pe.matmul(ps[:, P * t:P * t + P], col[:, t, heads[i]:heads[i] + 1].to_broadcast([P, P]),
                                             ident, start=True, stop=True)
                        return last

                    def turn(ps, src):
                        for t in range(TT):
                            last = pe.transpose(ps[:, P * t:P * t + P], src[:, P * t:P * t + P], ident)
                        last.then_inc(turned_kv, 1)

                    def fill(a, b):
                        if more:
                            project(pe, q, range(a, b), h_hi, h_lo)

                    for i, h in enumerate(heads):
                        for t in range(TT):
                            tok, cols = slice(P * t, P * t + P), slice(P * t, P * t + P)
                            pe.matmul(bank[4 + i][:, cols], g_[:, t, h:h + 1].to_broadcast([P, P]),
                                      const[:, C_TRI:C_TRI + P], start=True, stop=True)
                            pe.matmul(bank[i][:, cols], k_t[:, i, tok], k_t[:, i, tok], start=True, stop=True)
                            last = pe.matmul(bank[2 + i][:, cols], k_t[:, i, tok], q_t[:, i, tok], start=True, stop=True)
                        last.then_inc(gram, 1)
                        if i == 0:
                            rows_of(0, bank[6], beta).then_inc(gram, 1)
                    fill(*FILL_FRONT[0])
                    pe.wait_ge(diff, 8 * pair + 4)
                    pe.wait_ge(grow_exp, 2 * pair + 1)
                    rows_of(1, bank[4], beta).then_inc(gram, 1)
                    pe.wait_ge(diff, 8 * pair + 8)
                    pe.wait_ge(grow_exp, 2 * pair + 2)
                    turn(bank[5], k_t[:, 0])
                    fill(*FILL_FRONT[1])
                    pe.wait_ge(core_dve, 8 * pair + 4)
                    turn(bank[2], v_t[:, 0])
                    fill(*FILL_FRONT[2])
                    pe.wait_ge(core_dve, 8 * pair + 7)
                    turn(bank[4], k_t[:, 1])
                    pe.wait_ge(core_dve, 8 * pair + 8)
                    turn(bank[3], v_t[:, 1])
                    fill(*FILL_FRONT[3])
                    for l in range(LEVELS):
                        for i in range(2):
                            pe.wait_ge(off, 12 * pair + 2 * l + i + 1)
                            if l:
                                pe.wait_ge(stepped, 22 * pair + 4 * (l - 1) + 2 * i + 2)
                            for t in range(TT):
                                last = pe.matmul(bank[i][:, P * t:P * t + P], l_off[:, i, t], inv[:, i, t] if l else ident,
                                                 start=True, stop=True)
                            last.then_inc(w_ready, 1)
                        fill(*FILL_W[l])
                        for i in range(2 if l else 0):
                            pe.wait_ge(w_copied, 10 * pair + 2 * (l - 1) + i + 1)
                            for t in range(TT):
                                cols = slice(P * t, P * t + P)
                                if l < LEVELS - 1:
                                    pe.matmul(bank[2 + i][:, cols], inv_t[:, i, t], prod[:, i, t], start=True, stop=True)
                                last = pe.matmul(bank[4 + i][:, cols], prod[:, i, t], inv_t[:, i, t], start=True, stop=True)
                            last.then_inc(step_ready, 1)
                        fill(*FILL_STEP[l])
                    for i in range(2):
                        pe.wait_ge(stepped, 22 * pair + 20 + i + 1)
                        for t in range(TT):
                            cols = slice(P * t, P * t + P)
                            pe.matmul(bank[i][:, cols], inv_t[:, i, t], v_beta[:, i, t], start=True, stop=True)
                            last = pe.matmul(bank[2 + i][:, cols], kbg[:, i, t], inv_t[:, i, t], start=True, stop=True)
                        last.then_inc(uw_ready, 1)

                @block.gpsimd
                def _(pool):
                    for l in range(LEVELS):
                        for i in range(2):
                            if l:
                                pool.wait_ge(w_ready, 12 * pair + 2 * (l - 1) + i + 1)
                                if l == 1:
                                    pool.wait_ge(stepped, 22 * pair + 2 * i + 2)
                            else:
                                pool.wait_ge(core_dve, 8 * pair + 4 * i + 4)
                            mask = const[:, C_LEVEL + P * l:C_LEVEL + P * l + P]
                            pool.tensor_tensor(l_off[:, i], l_t[:, i], over_tiles(mask), ALU.mult).then_inc(off, 1)

                @block.scalar
                def _(act):
                    def copy_w(l):
                        for i in range(2):
                            act.wait_ge(w_ready, 12 * pair + 2 * l + i + 1)
                            act.activation(flat(prod[:, i]), bank[i][:], ACT.Copy).then_inc(w_copied, 1)

                    if more:
                        round_weights(act, n_next + 1)
                    for i in range(2):
                        act.wait_ge(diff, 8 * pair + 4 * i + 4)
                        act.activation(flat(decay[:, i]), flat(decay[:, i]), ACT.Exp).then_inc(decay_exp, 1)
                        act.activation(flat(grow[:, i]), bank[4 + i][:], ACT.Exp).then_inc(grow_exp, 1)
                    after = {0: (("pre", 0), ("pre", 1), ("round", 2)), 1: (("silu", 0), ("pre", 2)),
                             2: (("silu", 1), ("pre", 3)), 3: (("silu", 2), ("round", 3)),
                             4: (("silu", 3), ("pre", 4)), 5: (("silu", 4), ("pre", 5))}
                    for l in range(LEVELS):
                        if l:
                            copy_w(l)
                        for what, v in after[l] if more else ():
                            if what == "pre":
                                copy_pre(act, q, v, pre)
                            elif what == "silu":
                                silu_conv(act, q, v, dst)
                            else:
                                round_weights(act, n_next + v)
                    for i in range(2):
                        act.wait_ge(uw_ready, 2 * pair + i + 1)
                        act.activation(flat(u_tok[:, i]), bank[i][:], ACT.Copy).then_inc(uw_copied, 1)
                        act.activation(flat(w_t[:, i]), bank[2 + i][:], ACT.Copy).then_inc(uw_copied, 1)
                    if more:
                        silu_conv(act, q, 5, dst)

                @block.vector
                def _(dve):
                    for i, h in enumerate(heads):
                        dve.wait_ge(gram, 4 * pair + (1, 3)[i])
                        for t in range(TT):
                            dve.tensor_scalar(decay[:, i, t], bank[4 + i][:, P * t:P * t + P], g_cum[:, t, h:h + 1], 0.0,
                                              ALU.subtract, ALU.min).then_inc(diff, 1)
                    for i in range(2):
                        at = 8 * pair + 4 * i
                        dve.wait_ge(decay_exp, 2 * pair + i + 1)
                        dve.tensor_tensor(decay[:, i], decay[:, i], over_tiles(const[:, C_TRI:C_TRI + P]),
                                          ALU.mult).then_inc(core_dve, 1)
                        dve.wait_ge(core_dve, at + 1)
                        dve.tensor_tensor(flat(l_t[:, i]), flat(decay[:, i]), bank[i][:], ALU.mult).then_inc(core_dve, 1)
                        dve.wait_ge(core_dve, at + 2)
                        dve.wait_ge(gram, 4 * pair + (2, 4)[i])
                        beta_row = bank[(6, 4)[i]]
                        dve.tensor_tensor(flat(l_t[:, i]), flat(l_t[:, i]), beta_row[:], ALU.mult).then_inc(core_dve, 1)
                        dve.tensor_tensor(flat(a_qk[:, i]), flat(decay[:, i]), bank[2 + i][:], ALU.mult).then_inc(core_dve, 1)
                    for i, h in enumerate(heads):
                        dve.tensor_tensor(q_t[:, i], flat(grow[:, i]), q_t[:, i], ALU.mult).then_inc(kv_used, 1)
                        dve.wait_ge(turned_kv, 4 * pair + 2 * i + 1)
                        for dst_, f in ((kbg, beta_eg), (k_end, to_end)):
                            dve.tensor_tensor(dst_[:, i], tiles4(bank[5 - i][:]), token_scalar(f, h), ALU.mult).then_inc(kv_used, 1)
                        dve.wait_ge(turned_kv, 4 * pair + 2 * i + 2)
                        dve.tensor_tensor(v_beta[:, i], tiles4(bank[2 + i][:]), token_scalar(beta, h), ALU.mult).then_inc(kv_used, 1)
                    if more:
                        rest_weights(dve, n_next + 1)
                    dve.wait_ge(kv_used, 8 * pair + 8)
                    after = {0: (("conv", 0), ("rest", 2)), 1: (("conv", 1),), 2: (("conv", 2),), 3: (("conv", 3), ("rest", 3)),
                             4: (("conv", 4),), 5: (("conv", 5),)}
                    for l in range(LEVELS):
                        for i in range(2):
                            if l == 0:
                                dve.wait_ge(w_ready, 12 * pair + i + 1)
                                dve.tensor_tensor(inv[:, i], over_tiles(ident), tiles4(bank[i][:]), ALU.subtract).then_inc(stepped, 1)
                                dve.tensor_tensor(inv_t[:, i], over_tiles(ident), l_off[:, i], ALU.subtract).then_inc(stepped, 1)
                            else:
                                dve.wait_ge(step_ready, 10 * pair + 2 * (l - 1) + i + 1)
                                if l < LEVELS - 1:
                                    dve.tensor_tensor(flat(inv[:, i]), flat(inv[:, i]), bank[2 + i][:], ALU.subtract).then_inc(stepped, 1)
                                dve.tensor_tensor(flat(inv_t[:, i]), flat(inv_t[:, i]), bank[4 + i][:], ALU.subtract).then_inc(stepped, 1)
                        for what, v in after[l] if more else ():
                            if what == "conv":
                                convolve(dve, q, v, pre, dst)
                            else:
                                rest_weights(dve, n_next + v)

            o_n, o_f = (inv, inv_t)
            on_sums = bank[0][:, 0:2 * TT]
            with nc.Block() as block:
                @block.sync
                def _(sp):
                    if more:
                        load_weights(sp, n_next + 5, src_of(n_next + 5))

                @block.tensor
                def _(pe):
                    def fill(a, b):
                        if more:
                            project(pe, q, range(a, b), h_hi, h_lo)

                    for n in range(N_CH):
                        t, r = n // 2, CHUNK * (n % 2)
                        cols = slice(CHUNK * n, CHUNK * n + CHUNK)
                        for i in range(2):
                            pe.wait_ge(scan_state, (2 * N_CH + 1) * pair + (2 * n + i if n else 1))
                            pe.matmul(bank[i][r:r + CHUNK, 0:P], flat(w_t[:, i])[:, cols], state[:, i], start=True,
                                      stop=True).then_inc(scan_ws, 1)
                            pe.matmul(bank[4 + i][:, cols], state[:, i], q_t[:, i, cols], start=True, stop=False)
                        fill(48 + n, 49 + n)
                        for i in range(2):
                            pe.wait_ge(scan_new, 2 * (N_CH * pair + n) + i + 1)
                            vn = v_new[r:r + CHUNK, i]
                            pe.matmul(bank[4 + i][:, cols], vn, a_qk[r:r + CHUNK, i, t, r:r + CHUNK], start=False, stop=True)
                            pe.matmul(bank[2 + i][:, 0:P], k_end[r:r + CHUNK, i, t], vn, start=True,
                                      stop=True).then_inc(scan_kv, 1)
                        if more and n < 4:
                            sum_head(pe, q, n)
                    fill(56, 60)
                    for i in range(2):
                        pe.wait_ge(on_squared, 2 * pair + i + 1)
                        for t in range(TT):
                            last = pe.matmul(on_sums[:, TT * i + t:TT * i + t + 1], sq[i][:, P * t:P * t + P], ones[:, 0:1],
                                             start=True, stop=True)
                    last.then_inc(on_summed, 1)
                    fill(60, 64)
                    pe.wait_ge(on_inv, pair + 1)
                    if more:
                        pe.wait_ge(scan_state, (2 * N_CH + 1) * (pair + 1))
                        spread_heads(pe, q, hn_tok)
                        pe.wait_ge(z_done, 2 * q + 2)
                    for i in range(2):
                        for t in range(TT):
                            last = pe.matmul(bank[6 + i][:, P * t:P * t + P],
                                             rms_tok[:, TT * i + t:TT * i + t + 1].to_broadcast([P, P]), ident,
                                             start=True, stop=True)
                        last.then_inc(on_spread, 1)

                @block.vector
                def _(dve):
                    dve.memset(state[:], 0.0).then_inc(scan_state, 1)
                    for n in range(N_CH):
                        t, r = n // 2, CHUNK * (n % 2)
                        for i in range(2):
                            dve.wait_ge(scan_ws, 2 * (N_CH * pair + n) + i + 1)
                            dve.tensor_tensor(v_new[r:r + CHUNK, i], u_tok[r:r + CHUNK, i, t], bank[i][r:r + CHUNK, 0:P],
                                              ALU.subtract).then_inc(scan_new, 1)
                        for i, h in enumerate(heads):
                            dve.wait_ge(scan_kv, 2 * (N_CH * pair + n) + i + 1)
                            dve.scalar_tensor_tensor(state[:, i], state[:, i], end_decay[:, n % 2, t, h:h + 1],
                                                     bank[2 + i][:, 0:P], ALU.mult, ALU.add).then_inc(scan_state, 1)
                    if more:
                        invert_heads(dve, q, hn_tok)
                    for i in range(2):
                        dve.wait_ge(on_squared, 2 * pair + i + 1)
                        dve.scalar_tensor_tensor(flat(o_n[:, i]), bank[4 + i][:], vec[:, V_ON:V_ON + 1], z_t[:, i],
                                                 ALU.mult, ALU.mult).then_inc(on_step, 1)
                    dve.wait_ge(on_root, pair + 1)
                    dve.reciprocal(rms_tok[:], rms_tok[:]).then_inc(on_inv, 1)
                    if more:
                        rest_weights(dve, n_next + 4)
                        scale_heads(dve, q, dst)
                    dve.wait_ge(on_step, 4 * pair + 2)
                    for i in range(2):
                        dve.wait_ge(on_spread, 2 * pair + i + 1)
                        dve.tensor_tensor(flat(o_f[:, i]), flat(o_n[:, i]), bank[6 + i][:], ALU.mult).then_inc(on_step, 1)
                    for i, h in enumerate(heads):
                        dve.wait_ge(on_hi, 2 * pair + i + 1)
                        dve.tensor_tensor(o_lo[:, h], flat(o_f[:, i]), o_hi[:, h].bitcast(F32), ALU.subtract)

                @block.scalar
                def _(act):
                    if more:
                        for j in range(4):
                            square_head(act, q, j, dst)
                        root_heads(act, q, hn_tok)
                        round_weights(act, n_next + 4)
                        silu_z(act, q, 0, z_next)
                    for i in range(2):
                        act.wait_ge(scan_kv, 2 * N_CH * (pair + 1) - 1 + i)
                        act.activation(sq[i][:], bank[4 + i][:], ACT.Square).then_inc(on_squared, 1)
                    act.wait_ge(on_summed, pair + 1)
                    act.activation(rms_tok[:], on_sums, ACT.Sqrt, bias=bias_t[:, 0:1], scale=1 / P).then_inc(on_root, 1)
                    if more:
                        silu_z(act, q, 1, z_next)
                    for i, h in enumerate(heads):
                        act.wait_ge(on_step, 4 * pair + 3 + i)
                        act.activation(o_hi[:, h], flat(o_f[:, i]), ACT.Copy).then_inc(on_hi, 1)

        def gdn(h_hi, h_lo):
            st = ExitStack()
            g_, beta, g_cum = (sb(st, v, [P, TT, HEADS]) for v in ("g_", "beta", "g_cum"))
            beta_eg = sb(st, "beta_eg", [P, TT, HEADS])
            to_end = sb(st, "to_end", [P, TT, HEADS])
            end_decay = sb(st, "end_decay", [P, 2, TT, HEADS])
            state = sb(st, "state", [P, 2, P])
            v_new = sb(st, "v_new", [P, 2, P])
            hn_tok = sb(st, "hn_tok", [P, 4 * TT])
            sets = (y, sb(st, "qkvz_odd", [P, KD, SEQ]))
            pre = [sb(st, f"pre{i}", [P, CONV - 1 + SEQ]) for i in range(2)]
            temp = ExitStack()
            hf, xr = ([sb(temp, f"{v}{i}_gdn", [P, SEQ]) for i in range(2)] for v in ("hf", "xr"))
            t_, abs_, e_, u_, ln_ = (sb(temp, f"gate_temp{i}", [P, TT, HEADS]) for i in range(5))
            ba = sb(temp, "ba", [P, TT, 2 * HEADS])
            ba_f = sb(temp, "ba_f", [2 * HEADS, SEQ])
            w_ba = sb(temp, "w_ba", [P, KD, 2 * HEADS])
            w_ba_hi = sb(temp, "w_ba_hi", [P, KD, 2 * HEADS], F32R)
            w_ba_lo = sb(temp, "w_ba_lo", [P, KD, 2 * HEADS], F32R)
            head_in = sb(temp, "head_in", [P, 2, HEADS])

            def per_token(v):
                return v.rearrange("p t h -> p (t h)")

            dst, z_first, n0 = [y[:, i] for i in range(6)], y[:, 6:8], first_chunk(0)
            gate_in, gate_step, gate_act, gate_pe = sem("gate_in"), sem("gate_step"), sem("gate_act"), sem("gate_pe")
            with nc.Block() as block:
                @block.sync
                def _(sp):
                    sp.dma_start(w_ba[:], rows(a["gdn_w_in"][0], KD)[:, :, QKV_W:QKV_W + 2 * HEADS]).then_inc(gate_in, 16)
                    for i, name in enumerate(("gdn_a_log", "gdn_dt_bias")):
                        sp.dma_start(head_in[:, i], a[name].to_broadcast([P, HEADS])).then_inc(gate_in, 16)
                    for n in range(n0, n0 + 4):
                        load_weights(sp, n + 2, src_of(n + 2))

                @block.scalar
                def _(act):
                    act.wait_ge(gate_in, 48)
                    act.activation(w_ba_hi[:], w_ba[:], ACT.Copy).then_inc(gate_act, 1)
                    edge_act(act, 1, (1, 0), hf, xr, h_hi, n0 + 1)
                    act.wait_ge(gate_pe, 1)
                    act.activation(ba_f[:], bank[4][0:2 * HEADS, :], ACT.Copy).then_inc(gate_act, 1)
                    copy_pre(act, 0, 0, pre)
                    copy_pre(act, 0, 1, pre)
                    act.wait_ge(gate_pe, 2)
                    act.activation(ba[:], bank[5][:, 0:TT * 2 * HEADS], ACT.Copy).then_inc(gate_act, 1)
                    round_weights(act, n0 + 2)
                    silu_conv(act, 0, 0, dst)
                    copy_pre(act, 0, 2, pre)
                    act.wait_ge(gate_step, 4)
                    act.activation(e_[:], abs_[:], ACT.Exp, scale=-1.0).then_inc(gate_act, 1)
                    act.activation(head_in[:, 0], head_in[:, 0], ACT.Exp).then_inc(gate_act, 1)
                    silu_conv(act, 0, 1, dst)
                    copy_pre(act, 0, 3, pre)
                    act.wait_ge(gate_step, 5)
                    act.activation(ln_[:], u_[:], ACT.Ln).then_inc(gate_act, 1)
                    act.activation(beta[:], ba[:, :, 0:HEADS], ACT.Sigmoid).then_inc(gate_act, 1)
                    round_weights(act, n0 + 3)
                    silu_conv(act, 0, 2, dst)
                    copy_pre(act, 0, 4, pre)
                    silu_conv(act, 0, 3, dst)
                    copy_pre(act, 0, 5, pre)
                    silu_conv(act, 0, 4, dst)
                    round_weights(act, n0 + 4)
                    silu_z(act, 0, 0, z_first)
                    silu_conv(act, 0, 5, dst)
                    act.wait_ge(gate_step, 15)
                    act.activation(per_token(beta_eg[:]), per_token(g_cum[:]), ACT.Exp).then_inc(gate_act, 1)
                    act.activation(to_end[:], to_end[:], ACT.Exp).then_inc(gate_act, 1)
                    act.activation(end_decay[:].rearrange("p i t h -> p (i t h)"), bank[5][:, 0:64],
                                   ACT.Exp).then_inc(gate_act, 1)
                    for j in range(4):
                        square_head(act, 0, j, dst)
                    silu_z(act, 0, 1, z_first)
                    root_heads(act, 0, hn_tok)

                @block.vector
                def _(dve):
                    def step(ins, n):
                        ins.then_inc(gate_step, 1)
                        dve.wait_ge(gate_step, n)
                    for i in range(2):
                        dve.memset(pre[i][:, 0:CONV - 1], 0.0).then_inc(conv_step, 1)
                    dve.wait_ge(gate_act, 1)
                    step(dve.tensor_tensor(w_ba_lo[:], w_ba[:], w_ba_hi[:].bitcast(F32), ALU.subtract), 1)
                    edge_dve(dve, 1, (0, 5), (1, 0), hf, xr, h_hi, h_lo, n0 + 1)
                    convolve(dve, 0, 0, pre, dst)
                    dve.wait_ge(gate_act, 3)
                    bias = head_in[:, 1:2].to_broadcast([P, TT, HEADS])
                    step(dve.tensor_tensor(t_[:], ba[:, :, HEADS:], bias, ALU.add), 2)
                    step(dve.scalar_tensor_tensor(abs_[:], t_[:], -1.0, t_[:], ALU.mult, ALU.max), 3)
                    step(dve.tensor_scalar(t_[:], t_[:], 0.0, None, ALU.max), 4)
                    convolve(dve, 0, 1, pre, dst)
                    rest_weights(dve, n0 + 2)
                    dve.wait_ge(gate_act, 4)
                    step(dve.tensor_scalar(u_[:], e_[:], 1.0, None, ALU.add), 5)
                    step(dve.scalar_tensor_tensor(e_[:], u_[:], -1.0, e_[:], ALU.add, ALU.subtract), 6)
                    convolve(dve, 0, 2, pre, dst)
                    dve.wait_ge(gate_act, 6)
                    step(dve.reciprocal(u_[:], u_[:]), 7)
                    step(dve.tensor_tensor(e_[:], e_[:], u_[:], ALU.mult), 8)
                    step(dve.tensor_tensor(ln_[:], ln_[:], e_[:], ALU.subtract), 9)
                    step(dve.tensor_tensor(t_[:], t_[:], ln_[:], ALU.add), 10)
                    step(dve.tensor_scalar(t_[:], t_[:], -1.0, None, ALU.mult), 11)
                    step(dve.tensor_tensor(g_[:], t_[:], head_in[:, 0:1].to_broadcast([P, TT, HEADS]), ALU.mult), 12)
                    convolve(dve, 0, 3, pre, dst)
                    rest_weights(dve, n0 + 3)
                    convolve(dve, 0, 4, pre, dst)
                    convolve(dve, 0, 5, pre, dst)
                    dve.wait_ge(gate_pe, 3)
                    step(dve.tensor_copy(per_token(g_cum[:]), bank[4][:, 0:32]), 13)
                    step(dve.tensor_copy(per_token(to_end[:]), bank[4][:, 32:64]), 14)
                    step(dve.tensor_tensor(to_end[:], to_end[:], g_cum[:], ALU.subtract), 15)
                    dve.wait_ge(gate_act, 8)
                    dve.tensor_tensor(beta_eg[:], beta_eg[:], beta[:], ALU.mult)
                    rest_weights(dve, n0 + 4)
                    invert_heads(dve, 0, hn_tok)
                    scale_heads(dve, 0, dst)

                @block.gpsimd
                def _(pool):
                    edge_pool(pool, 1, hf)

                @block.tensor
                def _(pe):
                    edge_pe(pe, 1, True)
                    pe.wait_ge(gate_step, 1)
                    for k in range(KD):
                        pe.wait_ge(h_lo_ready, 2 * KD + k + 1)
                        last = product(pe, bank[4][0:2 * HEADS, :], w_ba_hi[:, k], w_ba_lo[:, k], h_hi[:, k],
                                       h_lo[:, k], k == 0, k == KD - 1)
                        if k == KD - 1:
                            last.then_inc(gate_pe, 1)
                        project(pe, 0, (k, KD + k), h_hi, h_lo)
                    project(pe, 0, range(2 * KD, 3 * KD), h_hi, h_lo)
                    pe.wait_ge(gate_act, 2)
                    for t in range(TT):
                        last = pe.transpose(bank[5][:, 16 * t:16 * t + 16], ba_f[0:2 * HEADS, P * t:P * t + P],
                                            ident[0:2 * HEADS, 0:2 * HEADS])
                    last.then_inc(gate_pe, 1)
                    project(pe, 0, range(3 * KD, 6 * KD), h_hi, h_lo)
                    pe.wait_ge(gate_step, 12)
                    gf = per_token(g_[:])
                    pe.matmul(bank[4][:, 0:32], const[:, C_TRI:C_TRI + P], gf, start=True, stop=True)
                    pe.matmul(bank[4][:, 32:64], const[:, C_SAME:C_SAME + P], gf, start=True, stop=True)
                    for i in range(2):
                        last = pe.matmul(bank[5][:, 32 * i:32 * i + 32],
                                         const[:, C_HALF + i:C_HALF + i + 1].to_broadcast([P, P]), gf,
                                         start=True, stop=True)
                    last.then_inc(gate_pe, 1)
                    project(pe, 0, range(6 * KD, 8 * KD), h_hi, h_lo)
                    pe.wait_ge(gate_step, 14)
                    for j in range(4):
                        sum_head(pe, 0, j)
                    pe.wait_ge(gate_act, 10)
                    spread_heads(pe, 0, hn_tok)

            temp.close()
            core_stack = ExitStack()
            core = [sb(core_stack, v, [P, 2, TT, P]) for v in
                    ("kbg", "k_end", "v_beta", "decay", "a_qk", "l_t", "inv_t")]
            for pair in range(PAIRS):
                gdn_pair(pair, h_hi, h_lo, g_, g_cum, beta, beta_eg, to_end, end_decay, state, v_new, sets, pre,
                         hn_tok, core)
            core_stack.close()
            st.close()

        def h_pair(name):
            st = ExitStack()
            return st, sb(st, "h_hi_" + name, [P, KD, SEQ], F32R), sb(st, "h_lo_" + name, [P, KD, SEQ], F32R)

        hs, h_hi, h_lo = h_pair("mlp0")
        mlp("mlp0", 0, N_FFN0, h_hi, h_lo, True)
        hs.close()
        ada_stack.close()

        hs, h_hi, h_lo = h_pair("gdn")
        gdn_o_stack = ExitStack()
        o_hi = sb(gdn_o_stack, "o_hi_gdn", [P, HEADS, SEQ], F32R, side="right")
        o_lo = sb(gdn_o_stack, "o_lo_gdn", [P, HEADS, SEQ], F32R, side="right")
        gdn(h_hi, h_lo)
        hs.close()
        out_projection("gdn_o", N_GWO, o_hi, o_lo, [[]] * 4, 2)
        gdn_o_stack.close()
        hs, h_hi, h_lo = h_pair("mlp1")
        mlp("mlp1", 1, N_FFN1, h_hi, h_lo, False)
        hs.close()
        with ExitStack() as st, nc.Block() as block:
            xr = [sb(st, f"xr{i}_last", [P, SEQ]) for i in range(2)]

            @block.tensor
            def _(pe):
                edge_pe(pe, 3, False)

            @block.scalar
            def _(act):
                edge_act(act, 3, False, None, None, None)

            @block.vector
            def _(dve):
                edge_dve(dve, 3, (1, 5), False, None, xr, None, None)

        with nc.Block() as block:
            o_tok = sb(root, "o_tok", [P, TT, D], side="right")
            back, back_copied, stored = sem("back"), sem("back_copied"), sem("stored")

            @block.tensor
            def _(pe):
                for i in range(2 * TT):
                    if i >= 4:
                        pe.wait_ge(back_copied, i - 3)
                    for k in range(4):
                        last = pe.transpose(bank[i % 4][:, P * k:P * k + P],
                                            x[:, 4 * (i % 2) + k, P * (i // 2):P * (i // 2) + P], ident)
                    last.then_inc(back, 1)

            @block.vector
            def _(dve):
                for i in range(2 * TT):
                    dve.wait_ge(back, i + 1)
                    dve.tensor_copy(o_tok[:, i // 2, 512 * (i % 2):512 * (i % 2) + 512], bank[i % 4][:]).then_inc(back_copied, 1)

            @block.sync
            def _(sp):
                for t in range(TT):
                    sp.wait_ge(back_copied, 2 * t + 2)
                    sp.dma_start(out[0, P * t:P * t + P, :], o_tok[:, t]).then_inc(stored, 16)
                sp.wait_ge(stored, 16 * TT)


_INS = ['x', 'c', 'positions', 'ada_w', 'ada_b', 'sandwich_g', 'mla_w_in', 'mla_q_norm_g', 'mla_kv_norm_g',
        'mla_w_uq', 'mla_w_ukv', 'mla_w_o', 'gdn_w_in', 'gdn_conv_w', 'gdn_a_log', 'gdn_dt_bias',
        'gdn_out_norm_g', 'gdn_w_o', 'ffn_w1', 'ffn_w2']


def make(nc, inputs):
    arrays, aps = {}, {}
    for name in _INS + ["const"]:
        v = constants() if name == "const" else np.ascontiguousarray(inputs[name])
        arrays[f"in_{name}"] = v
        aps[name] = nc.dram_tensor(f"in_{name}", v.shape, mybir.dt.from_np(v.dtype), kind="ExternalInput").ap()
    out = nc.dram_tensor("out_x", (1, SEQ, D), F32, kind="ExternalOutput").ap()
    build(nc, aps, out)
    return arrays


def kernel(**inputs):
    import concourse.bacc as bacc
    from concourse.bass_utils import run_bass_kernel_spmd

    nc = bacc.Bacc("TRN2", target_bir_lowering=False, num_devices=1)
    arrays = make(nc, inputs)
    r = run_bass_kernel_spmd(nc, [arrays], core_ids=[0])
    return r.results[0]["out_x"]
```

```python
from contextlib import ExitStack

import numpy as np

import concourse.bass as bass
from concourse import mybir

F32 = mybir.dt.float32
F32R = mybir.dt.float32r
I32 = mybir.dt.int32
ALU = mybir.AluOpType
ACT = mybir.ActivationFunctionType
AX = mybir.AxisListType

P = 128
D = 1024
SEQ = 512
KD = D // P
TT = SEQ // P
HEADS = 8
CHUNK = 64
Q_LORA = 384
KV_LORA = 256
ROPE = 64
NOPE = 128
KQ = Q_LORA // P
KKV = KV_LORA // P
FF = 4096
CONV = 4
EPS = 1e-6
ROPE_THETA = 10000.0
QKV_W = 3 * D
LEVELS = 6
ATT_SCALE = float((NOPE + ROPE) ** -0.5)
MASKED = -1e30

V_ADAB, V_C, V_QN, V_KVN, V_ON = 0, 96, 104, 107, 109
N_V1 = 110
V_SW = N_V1
V_CONV = V_SW + 64
N_VEC = V_CONV + 96

C_ID, C_TRI, C_SAME, C_LEVEL = 0, P, 2 * P, 3 * P
C_HALF = C_LEVEL + LEVELS * P
C_FREQ, C_SIGN, C_EARLY, C_LATE = C_HALF + 2, C_HALF + 3, C_HALF + 4, C_HALF + 4 + P
N_CONST = C_LATE + P


def constants():
    out = np.zeros((P, N_CONST), np.float32)
    j, c = np.arange(P)[:, None], np.arange(P)[None, :]
    same = j // CHUNK == c // CHUNK
    out[:, C_ID:C_ID + P] = j == c
    out[:, C_TRI:C_TRI + P] = same & (j <= c)
    out[:, C_SAME:C_SAME + P] = same
    for l in range(LEVELS):
        m = 1 << l
        out[:, C_LEVEL + l * P:C_LEVEL + (l + 1) * P] = (j // (2 * m) == c // (2 * m)) & (j // m < c // m)
    out[:, C_HALF] = np.arange(P) < CHUNK
    out[:, C_HALF + 1] = np.arange(P) >= CHUNK
    half = ROPE // 2
    freq = ROPE_THETA ** (-np.arange(half) / half)
    out[:, C_FREQ] = freq[np.arange(P) % half]
    out[:, C_SIGN] = np.where(np.arange(P) % ROPE < half, -1.0, 1.0)
    out[0, C_EARLY:C_EARLY + P] = np.arange(P) < CHUNK
    out[0, C_LATE:C_LATE + P] = MASKED * (np.arange(P) >= CHUNK)
    return out


def chunk_plan():
    size = [2048] * 3 + [1152] * 4 + [2048] * 2 + [2048] * 4 + [2048] * 32 + [2048] * 20 + [2048] * 32
    tiles = [2] * 3 + [3] * 4 + [8] * 2 + [2] * 4 + [2] * 32 + [2] * 20 + [2] * 32
    parts = [1] * 2 + [3] + [4] * 4 + [1] * (len(size) - 7)
    return size, tiles, parts


def build(nc, a, out):
    size, tiles, parts = chunk_plan()
    tiles_to = [sum(tiles[:n]) for n in range(len(tiles) + 1)]
    N_IN, N_UQ, N_UKV, N_WO, N_FFN0 = 0, 3, 7, 9, 13
    N_GDN, N_GWO, N_FFN1, N_END = 45, 61, 65, 97

    root = ExitStack()
    with root:
        sems = {}

        def sem(name):
            if name not in sems:
                sems[name] = root.enter_context(nc.semaphore(name))
            return sems[name]

        def sb(stack, name, shape, dt=F32, side="left"):
            return stack.enter_context(nc.sbuf_tensor(name, shape, dt, side=side))

        bank = [root.enter_context(nc.psum_tensor(f"bank{i}", [P, 512], F32)) for i in range(8)]
        sum_bank, mod_bank = bank[6], bank[7]

        x = sb(root, "x", [P, KD, SEQ])
        y = sb(root, "y", [P, KD, SEQ])
        w_raw = [sb(root, f"w_raw{i}", [P, 2048]) for i in range(2)]
        w_hi = [sb(root, f"w_hi{i}", [P, 2048], F32R) for i in range(2)]
        w_lo = [sb(root, f"w_lo{i}", [P, 2048], F32R) for i in range(2)]
        const = sb(root, "const", [P, N_CONST])
        vec = sb(root, "vec", [P, N_VEC])
        ones = sb(root, "ones", [P, P])
        coef = sb(root, "coef", [P, 2, 6 * KD])
        sq = [sb(root, f"sq{i}", [P, SEQ]) for i in range(2)]
        rms_tok = sb(root, "rms_tok", [P, 2 * TT])
        bias_t = sb(root, "bias_t", [P, 2])
        ident = const[:, C_ID:C_ID + P]

        w_loaded = [sem("w_loaded0"), sem("w_loaded1")]
        w_hi_ready, w_lo_ready, tile_done = sem("w_hi_ready"), sem("w_lo_ready"), sem("tile_done")

        def load_weights(sp, n, src, g=0):
            if n >= 2:
                sp.wait_ge(w_lo_ready, n - 1 + 8 * g)
            at = 0
            for part in src if isinstance(src, list) else [src]:
                k, cols = part.shape[1:]
                dst = w_raw[n % 2][:, 0:size[n]].rearrange("p (k n) -> p k n", k=k)[:, :, at:at + cols]
                sp.dma_start(dst, part).then_inc(w_loaded[n % 2], 16)
                at += cols

        def round_weights(act, n, g=0):
            act.wait_ge(w_loaded[n % 2], 16 * sum(parts[n % 2:n + 1:2]) + 64 * g)
            if n >= 2:
                act.wait_ge(tile_done, tiles_to[n - 1] + 16 * g)
            act.activation(w_hi[n % 2][:, 0:size[n]], w_raw[n % 2][:, 0:size[n]], ACT.Copy).then_inc(w_hi_ready, 1)

        def rest_weights(dve, n, g=0):
            dve.wait_ge(w_hi_ready, n + 1 + 8 * g)
            dve.tensor_tensor(w_lo[n % 2][:, 0:size[n]], w_raw[n % 2][:, 0:size[n]],
                              w_hi[n % 2][:, 0:size[n]].bitcast(F32), ALU.subtract).then_inc(w_lo_ready, 1)

        def product(pe, ps, s_hi, s_lo, m_hi, m_lo, first, last):
            pe.matmul(ps, s_lo, m_hi, start=first, stop=False)
            pe.matmul(ps, s_hi, m_lo, start=False, stop=False)
            return pe.matmul(ps, s_hi, m_hi, start=False, stop=last)

        def w_views(n, k):
            return (w_hi[n % 2][:, 0:size[n]].rearrange("p (k n) -> p k n", k=k),
                    w_lo[n % 2][:, 0:size[n]].rearrange("p (k n) -> p k n", k=k))

        def rows(w, k):
            return w.rearrange("(k p) n -> p k n", p=P)

        def src_of(n):
            if n == N_UQ - 1:
                w, at = rows(a["mla_w_in"][0], KD), 256 * n
                return [w[:, :, at:at + P]] + [w[:, :, at + P:at + P + ROPE]] * 2
            if n < N_UQ:
                return rows(a["mla_w_in"][0], KD)[:, :, 256 * n:min(256 * n + 256, Q_LORA + KV_LORA + ROPE)]
            if n < N_UKV:
                w, at = rows(a["mla_w_uq"][0], KQ), 2 * (NOPE + ROPE) * (n - N_UQ)
                heads = (at, at + NOPE + ROPE)
                return [w[:, :, c:c + NOPE] for c in heads] + [w[:, :, c + NOPE:c + NOPE + ROPE] for c in heads]
            if n < N_WO:
                return rows(a["mla_w_ukv"][0], KKV)[:, :, 1024 * (n - N_UKV):1024 * (n - N_UKV + 1)]
            if n < N_FFN0:
                return rows(a["mla_w_o"][0], KD)[:, :, 256 * (n - N_WO):256 * (n - N_WO + 1)]
            if n < N_GDN:
                return ffn_src(0, (n - N_FFN0) % 8, (n - N_FFN0) // 8)
            if n < N_GWO:
                pair, kind = (n - N_GDN) // 4, (n - N_GDN) % 4
                at = 256 * pair + (D * kind if kind < 3 else QKV_W + 2 * HEADS)
                return rows(a["gdn_w_in"][0], KD)[:, :, at:at + 256]
            if n < N_FFN1:
                return rows(a["gdn_w_o"][0], KD)[:, :, 256 * (n - N_GWO):256 * (n - N_GWO + 1)]
            return ffn_src(1, (n - N_FFN1) % 8, (n - N_FFN1) // 8)

        def ffn_src(l, j, g):
            if j < 4:
                return rows(a["ffn_w1"][l], KD)[:, :, bass.ds(1024 * g + 256 * j, 256)]
            return a["ffn_w2"][l][bass.ds(1024 * g, 1024), :].rearrange("(k p) n -> p k n", p=P)[
                :, :, 256 * (j - 4):256 * (j - 3)]

        ADA_FIRST = 8
        ADA_DIRECT, ADA_SHARED = (2, 5), (0, 1, 3, 4, 6, 7)
        N_DIRECT = len(ADA_DIRECT)
        ADA_UP = {3: 11, 5: 12, 7: 13, 8: 14}
        ADA_OUT = [[15], [16], [17, 18], [19]]
        ADA_MLP = 20
        ada_stack = root.enter_context(ExitStack())
        ada_raw = [sb(ada_stack, f"ada_raw{i}", [P, KD, 256]) for i in range(2)]
        ada_acc = [sb(ada_stack, f"ada_acc{i}", [P, 256]) for i in range(2)]
        c_act = sb(ada_stack, "c_act", [P, KD])
        ada_loaded = [sem(f"ada_loaded{i}") for i in range(6)]
        ada_step, ada_reduced, ada_done = sem("ada_step"), sem("ada_reduced"), sem("ada_done")
        ada_direct_done = sem("ada_direct_done")

        def load_ada(sp, m, g=0):
            if isinstance(g, int):
                m, g = m + 8 * g, 0
            layer = m // 24 if isinstance(g, int) else 1
            slot = ada_slot(m)
            if m >= 6:
                sp.wait_ge(ada_step, KD * (m - 1 - N_DIRECT if m >= ADA_FIRST else m - 5) + KD * 8 * g)
            elif m >= 4:
                sp.wait_ge(x_turned, KD)
            src = a["ada_w"][layer].rearrange("(k p) n -> p k n", p=P)[
                :, :, bass.ds(256 * (m - 24 * layer) + 2048 * g, 256)]
            sp.dma_start(ada_slots[slot], src).then_inc(ada_loaded[slot], 16)

        def ada_slot(m):
            return m if m < 6 else m % 2

        def ada_direct(pe, m):
            pe.wait_ge(ada_loaded[m], 16)
            for i in range(2):
                for k in range(KD):
                    last = pe.matmul(mod_bank[:, 2 * m + i:2 * m + i + 1], ada_slots[ada_slot(m)][:, k, P * i:P * i + P],
                                     c_act[:, k:k + 1], start=k == 0, stop=k == KD - 1)
            last.then_inc(ada_direct_done, 1)

        def first_multiply(dve, d):
            m, acc = ADA_SHARED[d], first_acc[d]
            dve.wait_ge(ada_loaded[ada_slot(m)], 16 if m < 6 else 32)
            dve.tensor_scalar(acc, ada_slots[ada_slot(m)][:, 0], c_act[:, 0:1], None, ALU.mult).then_inc(ada_step, 1)
            for k in range(1, KD):
                dve.wait_ge(ada_step, KD * d + k)
                dve.scalar_tensor_tensor(acc, ada_slots[ada_slot(m)][:, k], c_act[:, k:k + 1], acc,
                                         ALU.mult, ALU.add).then_inc(ada_step, 1)

        def first_reduce(pe, d):
            m = ADA_SHARED[d]
            pe.wait_ge(ada_step, KD * (d + 1))
            for i in range(2):
                last = pe.matmul(mod_bank[:, 2 * m + i:2 * m + i + 1], first_acc[d][:, P * i:P * i + P], ones[:, 0:1],
                                 start=True, stop=True)
            last.then_inc(ada_reduced, 1)

        def ada_first_finish(dve):
            dve.wait_ge(ada_reduced, len(ADA_SHARED))
            dve.wait_ge(ada_direct_done, N_DIRECT)
            dve.tensor_tensor(coef[:, 0, 0:2 * ADA_FIRST], mod_bank[:, 0:2 * ADA_FIRST],
                              vec[:, V_ADAB:V_ADAB + 2 * ADA_FIRST], ALU.add).then_inc(ada_done, ADA_FIRST)

        def ada_multiply(dve, m, g=0):
            dve.wait_ge(ada_loaded[m % 2], 16 * (m // 2 - 1) + 64 * g)
            dve.wait_ge(ada_reduced, m - 1 - N_DIRECT + 8 * g)
            acc = ada_acc[m % 2][:]
            dve.tensor_scalar(acc, ada_raw[m % 2][:, 0], c_act[:, 0:1], None, ALU.mult).then_inc(ada_step, 1)
            for k in range(1, KD):
                dve.wait_ge(ada_step, KD * (m - N_DIRECT) + k + KD * 8 * g)
                dve.scalar_tensor_tensor(acc, ada_raw[m % 2][:, k], c_act[:, k:k + 1], acc,
                                         ALU.mult, ALU.add).then_inc(ada_step, 1)

        def ada_reduce(pe, m, g=0):
            pe.wait_ge(ada_step, KD * (m + 1 - N_DIRECT) + KD * 8 * g)
            pe.wait_ge(ada_done, m + 8 * g)
            for i in range(2):
                last = pe.matmul(mod_bank[:, i:i + 1], ada_acc[m % 2][:, P * i:P * i + P], ones[:, 0:1],
                                 start=True, stop=True)
            last.then_inc(ada_reduced, 1)

        def ada_finish(dve, m, g=0):
            dve.wait_ge(ada_reduced, m + 1 - N_DIRECT + 8 * g)
            dve.tensor_tensor(coef[:].rearrange("p l c -> p (l c)")[:, bass.ds(2 * m + 16 * g, 2)], mod_bank[:, 0:2],
                              vec[:, bass.ds(V_ADAB + 2 * m + 16 * g, 2)], ALU.add).then_inc(ada_done, 1)

        def gain(l, s):
            return vec[:, V_SW + 8 * (4 * l + s):V_SW + 8 * (4 * l + s) + 8]

        def section(l, s):
            return coef[:, l, 8 * s:8 * s + 8]

        def square_tiles(act, src, n, name, b=0):
            for k in range(n):
                if k >= 2:
                    act.wait_ge(sem(name + "_summed"), n * b + k - 1)
                act.activation(sq[k % 2][:], src[:, k], ACT.Square).then_inc(sem(name + "_squared"), 1)

        def sum_tiles(pe, n, name, b=0, ps=None):
            for k in range(n):
                sum_tile(pe, k, n, name, b, ps or sum_bank)

        def sum_tile(pe, k, n, name, b, ps):
            pe.wait_ge(sem(name + "_squared"), n * b + k + 1)
            for t in range(TT):
                last = pe.matmul(ps[:, t:t + 1], sq[k % 2][:, P * t:P * t + P], ones[:, 0:1],
                                 start=k == 0 and t == 0, stop=k == n - 1, skip_group_check=True)
            last.then_inc(sem(name + "_summed"), 1)

        def root_of_mean(act, n, name, scale, b=0, ps=None):
            ps = ps or sum_bank
            act.wait_ge(sem(name + "_summed"), n * (b + 1))
            act.activation(rms_tok[:, 0:TT], ps[:, 0:TT], ACT.Sqrt, bias=bias_t[:, 0:1], scale=scale).then_inc(sem(name + "_root"), 1)

        def inverse_of_root(dve, name, b=0):
            dve.wait_ge(sem(name + "_root"), b + 1)
            dve.reciprocal(rms_tok[:, TT:2 * TT], rms_tok[:, 0:TT]).then_inc(sem(name + "_inv"), 1)

        def spread(pe, name, b=0, ps=None):
            ps = ps or sum_bank
            pe.wait_ge(sem(name + "_inv"), b + 1)
            for t in range(TT):
                last = pe.matmul(ps[:, P * t:P * t + P], rms_tok[:, TT + t:TT + t + 1].to_broadcast([P, P]), ident,
                                 start=True, stop=True)
            last.then_inc(sem(name + "_spread"), 1)

        xr_ready, hf_ready, h_hi_ready, h_lo_ready = sem("xr_ready"), sem("hf_ready"), sem("h_hi_ready"), sem("h_lo_ready")

        def scale_h(dve, b, inv_rms, hf, xr, h_hi, h_lo):
            for k in range(KD):
                if k >= 2:
                    dve.wait_ge(hf_ready, KD * b + k - 1)
                dve.tensor_tensor(xr[k % 2][:], x[:, k], inv_rms[:], ALU.mult).then_inc(xr_ready, 1)
                if k >= 1:
                    rest_h(dve, b, k - 1, hf, h_hi, h_lo)
            rest_h(dve, b, KD - 1, hf, h_hi, h_lo)

        def rest_h(dve, b, k, hf, h_hi, h_lo):
            dve.wait_ge(h_hi_ready, KD * b + k + 1)
            dve.tensor_tensor(h_lo[:, k], hf[k % 2][:], h_hi[:, k].bitcast(F32), ALU.subtract).then_inc(h_lo_ready, 1)

        def modulate_h(act, b, l, s, hf, xr, h_hi):
            fac, shift = section(l, s + 1), section(l, s)
            for k in range(KD):
                act.wait_ge(xr_ready, KD * b + k + 1)
                if k >= 2:
                    act.wait_ge(h_lo_ready, KD * b + k - 1)
                act.activation(hf[k % 2][:], xr[k % 2][:], ACT.Identity, bias=shift[:, k:k + 1],
                               scale=fac[:, k:k + 1]).then_inc(hf_ready, 1)
                act.wait_ge(hf_ready, KD * b + k + 1)
                act.activation(h_hi[:, k], hf[k % 2][:], ACT.Copy).then_inc(h_hi_ready, 1)

        yr_ready, x_new, factors_ready = sem("yr_ready"), sem("x_new"), sem("factors_ready")

        ADDS = KD - 2

        def square_y(act, b, t, src):
            if t >= 2:
                act.wait_ge(sem("edge_y_added"), ADDS * b + t - 1)
            act.activation(sq[min(t, 1)][:], src, ACT.Square).then_inc(sem("edge_y_squared"), 1)

        def add_squares(pool, name, b, slots):
            for k in range(1, KD - 1):
                pool.wait_ge(sem(name + "_squared"), KD * b + k + 1)
                if k >= 2:
                    pool.wait_ge(sem(name + "_added"), ADDS * b + k - 1)
                pool.tensor_tensor(sq[0][:], sq[0][:], slots[(k - 1) % len(slots)][:], ALU.add).then_inc(sem(name + "_added"), 1)

        def sum_added(pe, name, b, ps):
            for part in range(2):
                if part == 0:
                    pe.wait_ge(sem(name + "_added"), ADDS * (b + 1))
                else:
                    pe.wait_ge(sem(name + "_squared"), KD * (b + 1))
                for t in range(TT):
                    last = pe.matmul(ps[:, t:t + 1], sq[part][:, P * t:P * t + P], ones[:, 0:1],
                                     start=part == 0 and t == 0, stop=part == 1, skip_group_check=True)
            last.then_inc(sem(name + "_summed"), 1)

        def edge_pe(pe, b, nxt):
            sum_added(pe, "edge_y", b, sum_bank)
            spread(pe, "edge_y", b)
            if nxt:
                sum_added(pe, "edge_x", b, mod_bank)
                spread(pe, "edge_x", b, mod_bank)

        def edge_pool(pool, b, hf):
            add_squares(pool, "edge_x", b, (sq[1], hf[0]))

        def edge_act(act, b, nxt, hf, xr, h_hi, n_round=None, beside=None):
            root_of_mean(act, 1, "edge_y", 1 / D, b)
            if nxt:
                round_weights(act, n_round)
                if beside:
                    beside()
                for k in range(KD):
                    act.wait_ge(x_new, KD * b + k + 1)
                    if k >= 3:
                        act.wait_ge(sem("edge_x_added"), ADDS * b + k - 2)
                    slot = sq[0] if k == 0 else (sq[1], hf[0])[(k - 1) % 2]
                    act.activation(slot[:], x[:, k], ACT.Square).then_inc(sem("edge_x_squared"), 1)
                root_of_mean(act, 1, "edge_x", 1 / D, b, mod_bank)
                modulate_h(act, b + 1, *nxt, hf, xr, h_hi)

        def edge_dve(dve, b, gate, nxt, hf, xr, h_hi, h_lo, n_round=None, beside=None):
            l, s = gate
            g_fac = section(l, s)
            dve.tensor_tensor(g_fac, g_fac, gain(l, 1 if s == 2 else 3), ALU.mult).then_inc(factors_ready, 1)
            if nxt:
                nl, ns = nxt
                dve.scalar_tensor_tensor(section(nl, ns + 1), section(nl, ns + 1), 1.0,
                                         gain(nl, 0 if ns == 0 else 2), ALU.add, ALU.mult).then_inc(factors_ready, 1)
            dve.wait_ge(factors_ready, 1 + 2 * b + (2 if nxt else 1))
            inverse_of_root(dve, "edge_y", b)
            dve.wait_ge(sem("edge_y_spread"), b + 1)
            for k in range(KD + 1):
                if k < KD:
                    if k >= 2:
                        dve.wait_ge(x_new, KD * b + k - 1)
                    dve.scalar_tensor_tensor(xr[k % 2][:], y[:, k], g_fac[:, k:k + 1], sum_bank[:],
                                             ALU.mult, ALU.mult).then_inc(yr_ready, 1)
                if k:
                    dve.wait_ge(yr_ready, KD * b + k)
                    dve.tensor_tensor(x[:, k - 1], x[:, k - 1], xr[(k - 1) % 2][:], ALU.add).then_inc(x_new, 1)
            dve.wait_ge(x_new, KD * (b + 1))
            if nxt:
                if beside:
                    beside()
                rest_weights(dve, n_round)
                inverse_of_root(dve, "edge_x", b)
                dve.wait_ge(sem("edge_x_spread"), b + 1)
                scale_h(dve, b + 1, mod_bank, hf, xr, h_hi, h_lo)

        mla_tables = root.enter_context(ExitStack())
        low_stack = ExitStack()
        cos_t = sb(mla_tables, "cos_t", [P, SEQ], side="right")
        sin_t = sb(mla_tables, "sin_t", [P, SEQ], side="right")
        mla_keep = ExitStack()
        v_tok = sb(mla_keep, "v_tok", [P, TT, HEADS * P])
        k_rope = sb(mla_keep, "k_rope", [P, SEQ])
        low_hi = sb(low_stack, "low_hi", [P, KQ + KKV, SEQ], F32R, side="right")
        low_lo = sb(low_stack, "low_lo", [P, KQ + KKV, SEQ], F32R, side="right")
        rope_t = [sb(low_stack, f"rope_t{i}", [P, SEQ], side="right") for i in range(2)]
        h_stack = ExitStack()
        h_hi = sb(h_stack, "h_hi_mla", [P, KD, SEQ], F32R)
        h_lo = sb(h_stack, "h_lo_mla", [P, KD, SEQ], F32R)
        low_f = ExitStack()
        low = sb(low_f, "low", [P, KQ + KKV, SEQ])
        low_copied, krope_step = sem("low_copied"), sem("krope_step")
        ada_slots = [v[:] for v in ada_raw] + [
            v_tok[:, 2 * i:2 * i + 2].rearrange("p t (k n) -> p (t k) n", n=256) for i in range(2)] + [
            y[:, 4 * i:4 * i + 4].rearrange("p t (k n) -> p (t k) n", n=256) for i in (1, 0)]
        first_acc = [v[:] for v in ada_acc] + [rope_t[0][:, 0:256], rope_t[0][:, 256:512], rope_t[1][:, 0:256], rope_t[1][:, 256:512]]
        pos_i, ang, turns, wrap = low[:, 0].bitcast(I32), low[:, 1], low[:, 2], low[:, 3]
        v1, v2, v3 = low[0:N_V1, 4, 0:P], low[0:64, 4, P:2 * P], low[0:96, 4, 2 * P:3 * P]
        x_tok = y[:].rearrange("p k t -> p (k t)").rearrange("p (t d) -> p t d", t=TT)
        hf = [y[:, i] for i in range(2)]
        xr = [y[:, 2 + i] for i in range(2)]
        const_in, vec_in, x_in, pos_in = sem("const_in"), sem("vec_in"), sem("x_in"), sem("pos_in")
        v_turned, x_turned, x_copied, vec_copied = sem("v_turned"), sem("x_turned"), sem("x_copied"), sem("vec_copied")
        ones_set, angle_step, sin_done = sem("ones_set"), sem("angle_step"), sem("sin_done")

        def rope_dve(dve, ps, dst, base, done):
            t0, t1 = rope_t[0][:], rope_t[1][:]
            for b in range(4):
                lo, hi = 32 * b, 32 * (b ^ 1)
                dve.tensor_copy(t1[lo:lo + 32, :], ps[hi:hi + 32, :]).then_inc(done, 1)
            dve.tensor_tensor(t0, ps, cos_t[:], ALU.mult).then_inc(done, 1)
            dve.wait_ge(done, base + 5)
            dve.tensor_tensor(t1, t1, sin_t[:], ALU.mult).then_inc(done, 1)
            dve.wait_ge(done, base + 6)
            dve.tensor_tensor(dst, t0, t1, ALU.add).then_inc(done, 1)
            dve.wait_ge(done, base + 7)

        with nc.Block() as block:
            @block.sync
            def _(sp):
                sp.dma_start(const[:], a["const"]).then_inc(const_in, 16)
                for dst, src in ((v1[0:96, :], a["ada_b"].rearrange("l (k p) -> (l k) p", p=P)),
                                 (v1[96:104, :], a["c"].rearrange("b (k p) -> (b k) p", p=P)),
                                 (v1[104:107, :], a["mla_q_norm_g"].rearrange("b (k p) -> (b k) p", p=P)),
                                 (v1[107:109, :], a["mla_kv_norm_g"].rearrange("b (k p) -> (b k) p", p=P)),
                                 (v1[109:110, :], a["gdn_out_norm_g"]),
                                 (v2, a["sandwich_g"].rearrange("l s (k p) -> (l s k) p", p=P)),
                                 (v3, a["gdn_conv_w"].rearrange("b j (k p) -> (b j k) p", p=P))):
                    sp.dma_start(dst, src).then_inc(vec_in, 16)
                sp.dma_start(x_tok, a["x"][0].rearrange("(t p) d -> p t d", p=P)).then_inc(x_in, 16)
                sp.dma_start(pos_i, a["positions"].to_broadcast([P, SEQ])).then_inc(pos_in, 16)
                for m in range(ADA_FIRST - 1):
                    load_ada(sp, m)
                load_weights(sp, 0, src_of(0))
                load_ada(sp, ADA_FIRST - 1)
                load_weights(sp, 1, src_of(1))
                load_ada(sp, ADA_FIRST)
                load_ada(sp, ADA_FIRST + 1)
                for n in range(N_IN, N_UQ):
                    load_weights(sp, n + 2, src_of(n + 2))
                    load_ada(sp, n + 10)

            @block.gpsimd
            def _(pool):
                pool.memset(ones[:], 1.0).then_inc(ones_set, 1)

            @block.tensor
            def _(pe):
                pe.wait_ge(const_in, 16)
                pe.wait_ge(vec_in, 7 * 16)
                for v, n, at in ((v1, N_V1, 0), (v2, 64, V_SW), (v3, 96, V_CONV)):
                    last = pe.transpose(bank[5][:, at:at + n], v, ident[0:n, 0:n])
                last.then_inc(v_turned, 1)
                pe.wait_ge(x_in, 16)
                pe.wait_ge(ones_set, 1)
                for k in range(KD + 2):
                    if k < KD:
                        if k >= 4:
                            pe.wait_ge(x_copied, k - 3)
                        for t in range(TT):
                            last = pe.transpose(bank[k % 4][:, P * t:P * t + P], x_tok[:, t, P * k:P * k + P], ident)
                        last.then_inc(x_turned, 1)
                    if k >= 2:
                        sum_tile(pe, k - 2, KD, "first_x", 0, sum_bank)
                pe.wait_ge(vec_copied, 2)
                first_reduce(pe, 0)
                first_reduce(pe, 1)
                ada_direct(pe, ADA_DIRECT[0])
                spread(pe, "first_x")
                ada_direct(pe, ADA_DIRECT[1])
                for d in range(2, len(ADA_SHARED)):
                    first_reduce(pe, d)
                pe.wait_ge(w_lo_ready, 1)
                hi, lo = w_views(0, KD)
                for k in range(KD):
                    pe.wait_ge(h_lo_ready, k + 1)
                    for i in range(2):
                        last = product(pe, bank[i][:], hi[:, k, P * i:P * i + P], lo[:, k, P * i:P * i + P],
                                       h_hi[:, k], h_lo[:, k], k == 0, k == KD - 1)
                        if k == KD - 1:
                            last.then_inc(tile_done, 1)
                for n in range(N_IN + 1, N_UQ):
                    pe.wait_ge(w_lo_ready, n + 1)
                    hi, lo = w_views(n, KD)
                    for i in range(2):
                        t = 2 * n + i
                        cols = [v[:, :, P * i:P * i + P] for v in (hi, lo)]
                        if t >= 4:
                            pe.wait_ge(low_copied, t - 3)
                        ps = bank[t % 4 if t < KQ + KKV else 4]
                        for k in range(KD):
                            last = product(pe, ps[:], cols[0][:, k], cols[1][:, k], h_hi[:, k], h_lo[:, k],
                                           k == 0, k == KD - 1)
                        last.then_inc(tile_done, 1)
                        for v in (0, 1) if t == 2 else (t - 1,):
                            if v < KQ:
                                sum_tile(pe, v, KQ, "cq", 0, sum_bank)
                            else:
                                sum_tile(pe, v - KQ, KKV, "ckv", 0, bank[5])
                        if i == 0:
                            ada_reduce(pe, n + 7)
                ada_reduce(pe, N_UQ + 7)
                spread(pe, "cq")
                spread(pe, "ckv", 0, bank[5])

            @block.scalar
            def _(act):
                act.wait_ge(v_turned, 1)
                act.activation(vec[:], bank[5][:, 0:N_VEC], ACT.Copy).then_inc(vec_copied, 1)
                act.wait_ge(vec_copied, 1)
                act.activation(c_act[:], vec[:, V_C:V_C + KD], ACT.Silu).then_inc(vec_copied, 1)
                for k in range(KD):
                    act.wait_ge(x_turned, k + 1)
                    act.activation(x[:, k], bank[k % 4][:], ACT.Copy).then_inc(x_copied, 1)
                    act.wait_ge(x_copied, k + 1)
                    if k >= 2:
                        act.wait_ge(sem("first_x_summed"), k - 1)
                    act.activation(sq[k % 2][:], x[:, k], ACT.Square).then_inc(sem("first_x_squared"), 1)
                act.wait_ge(sem("eps_set"), 2)
                root_of_mean(act, KD, "first_x", 1 / D)
                act.wait_ge(angle_step, 16)
                act.activation(sin_t[:], ang, ACT.Sin, scale=const[:, C_SIGN:C_SIGN + 1]).then_inc(sin_done, 1)
                act.activation(cos_t[:], wrap, ACT.Sin).then_inc(sin_done, 1)
                round_weights(act, 0)
                act.wait_ge(factors_ready, 1)
                modulate_h(act, 0, 0, 0, hf, xr, h_hi)
                round_weights(act, 1)
                act.wait_ge(sin_done, 2)
                for n in range(N_IN, N_UQ):
                    for t in range(2 * n, min(2 * n + 2, KQ + KKV)):
                        act.wait_ge(tile_done, t + 1)
                        if t >= 2:
                            act.wait_ge(sem("cq_summed"), min(t, KQ) if t == KQ else t - 1)
                        slot = sq[t % 2 if t < KQ else (t - KQ) % 2]
                        act.activation(slot[:], bank[t % 4][:], ACT.Square).then_inc(
                            sem("cq_squared" if t < KQ else "ckv_squared"), 1)
                        act.activation(low[:, t], bank[t % 4][:], ACT.Copy).then_inc(low_copied, 1)
                    if n + 2 <= N_UQ:
                        round_weights(act, n + 2)
                root_of_mean(act, KQ, "cq", 1 / Q_LORA)
                act.wait_ge(sem("cq_inv"), 1)
                root_of_mean(act, KKV, "ckv", 1 / KV_LORA, 0, bank[5])
                for k in range(KQ + KKV):
                    act.wait_ge(sem("low_scaled"), k + 1)
                    act.activation(low_hi[:, k], low[:, k], ACT.Copy).then_inc(sem("low_hi_ready"), 1)

            @block.vector
            def _(dve):
                dve.memset(bias_t[:, 0:1], EPS).then_inc(sem("eps_set"), 1)
                dve.memset(bias_t[:, 1:2], P * EPS).then_inc(sem("eps_set"), 1)
                def step(ins, n):
                    ins.then_inc(angle_step, 1)
                    dve.wait_ge(angle_step, n)
                two_pi = 2 * np.pi
                p1 = 6.28125
                p2 = float(np.float32(int((two_pi - p1) * 2 ** 19) / 2 ** 19))
                p3 = float(two_pi - p1 - p2)
                limit = 3.1415925
                dve.wait_ge(pos_in, 16)
                dve.wait_ge(const_in, 16)
                step(dve.tensor_copy(ang, pos_i), 1)
                step(dve.tensor_scalar(ang, ang, const[:, C_FREQ:C_FREQ + 1], None, ALU.mult), 2)
                step(dve.tensor_scalar(turns, ang, 1 / two_pi, 12582912.0, ALU.mult, ALU.add), 3)
                step(dve.tensor_scalar(turns, turns, -12582912.0, None, ALU.add), 4)
                for n, part in ((5, p1), (6, p2)):
                    step(dve.scalar_tensor_tensor(ang, turns, -part, ang, ALU.mult, ALU.add), n)
                step(dve.scalar_tensor_tensor(ang, turns, -p3, ang, ALU.mult, ALU.add), 7)
                step(dve.tensor_scalar(wrap, ang, np.pi / 2, None, ALU.add), 8)
                for n, r in ((9, ang), (13, wrap)):
                    step(dve.tensor_scalar(turns, r, 1 / two_pi, 12582912.0, ALU.mult, ALU.add), n)
                    step(dve.tensor_scalar(turns, turns, -12582912.0, None, ALU.add), n + 1)
                    step(dve.scalar_tensor_tensor(r, turns, -two_pi, r, ALU.mult, ALU.add), n + 2)
                    step(dve.tensor_scalar(r, r, limit, -limit, ALU.min, ALU.max), n + 3)
                dve.wait_ge(vec_copied, 2)
                for d in range(2):
                    first_multiply(dve, d)
                inverse_of_root(dve, "first_x")
                for d in range(2, len(ADA_SHARED) - 1):
                    first_multiply(dve, d)
                rest_weights(dve, 0)
                first_multiply(dve, len(ADA_SHARED) - 1)
                ada_first_finish(dve)
                dve.wait_ge(ada_done, ADA_FIRST)
                dve.scalar_tensor_tensor(section(0, 1), section(0, 1), 1.0, gain(0, 0), ALU.add,
                                         ALU.mult).then_inc(factors_ready, 1)
                dve.wait_ge(sem("first_x_spread"), 1)
                scale_h(dve, 0, sum_bank, hf, xr, h_hi, h_lo)
                rest_weights(dve, 1)
                for n in range(N_IN, N_UQ):
                    ada_multiply(dve, n + 8)
                    if n + 2 <= N_UQ:
                        rest_weights(dve, n + 2)
                    if n + 1 < N_UQ:
                        ada_finish(dve, n + 8)
                for name, at, n in (("cq", 0, KQ), ("ckv", KQ, KKV)):
                    if at:
                        dve.wait_ge(sem("cq_spread"), 1)
                    inverse_of_root(dve, name)
                    if not at:
                        ada_finish(dve, N_UQ + 7)
                        dve.wait_ge(low_copied, KQ + KKV)
                    dve.wait_ge(sem(name + "_spread"), 1)
                    for k in range(at, at + n):
                        g = vec[:, V_QN + k:V_QN + k + 1]
                        inv_rms = sum_bank if name == "cq" else bank[5]
                        dve.scalar_tensor_tensor(low[:, k], low[:, k], g, inv_rms[:], ALU.mult,
                                                 ALU.mult).then_inc(sem("low_scaled"), 1)
                for k in range(KQ + KKV):
                    dve.wait_ge(sem("low_hi_ready"), k + 1)
                    dve.tensor_tensor(low_lo[:, k], low[:, k], low_hi[:, k].bitcast(F32), ALU.subtract)
        low_f.close()
        h_stack.close()

        q_stack = ExitStack()
        q_nope = sb(q_stack, "q_nope", [P, HEADS, SEQ])
        q_rope = sb(q_stack, "q_rope", [P, HEADS // 2, SEQ])
        k_nope = y
        up_copied, qrope_step = sem("up_copied"), sem("qrope_step")
        with nc.Block() as block:
            def copies_before(n, i):
                return 2 * (n - N_UQ) + i if n < N_UKV else 8 + 8 * (n - N_UKV) + i

            def up_bank(n, i):
                return bank[4 + (n - N_UQ) % 2] if n < N_UKV and i == 2 else bank[copies_before(n, i) % 4]

            @block.sync
            def _(sp):
                for n in range(N_UQ, N_WO):
                    load_weights(sp, n + 2, src_of(n + 2))
                    if n in ADA_UP:
                        load_ada(sp, ADA_UP[n] + 2)

            @block.tensor
            def _(pe):
                for n in range(N_UQ, N_WO):
                    pe.wait_ge(w_lo_ready, n + 1)
                    if n < N_UKV:
                        hi, lo = w_views(n, KQ)
                        for i in range(3):
                            if i < 2:
                                if copies_before(n, i) >= 4:
                                    pe.wait_ge(up_copied, copies_before(n, i) - 3)
                            else:
                                if n == N_UQ:
                                    pe.wait_ge(krope_step, 7)
                                elif n - N_UQ >= 2:
                                    pe.wait_ge(qrope_step, 7 * (n - N_UQ - 1))
                            cols = [v[:, :, P * i:P * i + P] for v in (hi, lo)]
                            for k in range(KQ):
                                last = product(pe, up_bank(n, i)[:], cols[0][:, k], cols[1][:, k], low_hi[:, k],
                                               low_lo[:, k], k == 0, k == KQ - 1)
                            last.then_inc(tile_done, 1)
                    else:
                        hi, lo = (v.rearrange("p k (h c) -> p k h c", h=4) for v in w_views(n, KKV))
                        for i in range(8):
                            pe.wait_ge(up_copied, copies_before(n, i) - 3)
                            for k in range(KKV):
                                ps = up_bank(n, i)[:]
                                kv = KQ + k
                                if i < 4:
                                    last = product(pe, ps, hi[:, k, i, 0:NOPE], lo[:, k, i, 0:NOPE], low_hi[:, kv],
                                                   low_lo[:, kv], k == 0, k == KKV - 1)
                                else:
                                    tok = slice(P * (i - 4), P * (i - 3))
                                    last = product(pe, ps, low_hi[:, kv, tok], low_lo[:, kv, tok], hi[:, k, :, NOPE:],
                                                   lo[:, k, :, NOPE:], k == 0, k == KKV - 1)
                            last.then_inc(tile_done, 1)
                    if n in ADA_UP:
                        ada_reduce(pe, ADA_UP[n])

            @block.scalar
            def _(act):
                for n in range(N_UQ, N_WO):
                    round_weights(act, n + 1)
                    for i in range(2 if n < N_UKV else 8):
                        act.wait_ge(tile_done, tiles_to[n] + i + 1)
                        if n < N_UKV:
                            dst = q_nope[:, 2 * (n - N_UQ) + i]
                        elif i < 4:
                            dst = k_nope[:, 4 * (n - N_UKV) + i]
                        else:
                            dst = v_tok[:, i - 4, 512 * (n - N_UKV):512 * (n - N_UKV + 1)]
                        act.activation(dst, up_bank(n, i)[:], ACT.Copy).then_inc(up_copied, 1)

            @block.vector
            def _(dve):
                rope_dve(dve, bank[4][:], k_rope[:], 0, krope_step)
                for n in range(N_UQ, N_WO):
                    rest_weights(dve, n + 1)
                    if n in ADA_UP:
                        ada_multiply(dve, ADA_UP[n])
                    if n < N_UKV:
                        dve.wait_ge(tile_done, tiles_to[n] + 3)
                        rope_dve(dve, up_bank(n, 2)[:], q_rope[:, n - N_UQ], 7 * (n - N_UQ), qrope_step)
                    if n in ADA_UP:
                        ada_finish(dve, ADA_UP[n])
        low_stack.close()
        mla_tables.close()

        o_stack = ExitStack()
        o_hi = sb(o_stack, "o_hi_mla", [P, HEADS, SEQ], F32R, side="right")
        o_lo = sb(o_stack, "o_lo_mla", [P, HEADS, SEQ], F32R, side="right")
        with ExitStack() as st, nc.Block() as block:
            prob = [sb(st, f"prob{i}", [P, SEQ]) for i in range(3)]
            prob_t = [sb(st, f"prob_t{i}", [P, SEQ]) for i in range(3)]
            stat = [sb(st, f"stat{i}", [P, 4]) for i in range(4)]
            scores_ready, peak, bias_ready, exp_done = sem("scores_ready"), sem("peak"), sem("bias_ready"), sem("exp_done")
            inv_ready, prob_ready, turned, turned_copied = sem("inv_ready"), sem("prob_ready"), sem("turned"), sem("turned_copied")
            valued, o_rounded, o_rest = sem("valued"), sem("o_rounded"), sem("o_rest")
            items = [(h, b) for h in range(HEADS) for b in range(TT)]
            N = len(items)
            score_bank = (bank[0], bank[1], bank[6])
            TURN_LAG, COPY_LAG, VALUE_LAG = 2, 3, 4

            @block.tensor
            def _(pe):
                def scores(i):
                    h, b = items[i]
                    if i >= 3:
                        pe.wait_ge(exp_done, i - 2)
                    into = score_bank[i % 3]
                    ps, keys, qs = into[:, 0:P * (b + 1)], slice(0, P * (b + 1)), slice(P * b, P * b + P)
                    r = ROPE * (h % 2)
                    pe.matmul(ps, q_nope[:, h, qs], k_nope[:, h, keys], start=True, stop=False)
                    pe.matmul(ps, q_rope[r:r + ROPE, h // 2, qs], k_rope[r:r + ROPE, keys], start=False, stop=True)
                    pe.matmul(into[:, P * b:P * b + P], const[0:1, C_EARLY:C_EARLY + P],
                              const[0:1, C_LATE:C_LATE + P], start=False, stop=True,
                              skip_group_check=True).then_inc(scores_ready, 1)

                def turn(i):
                    b = items[i][1]
                    pe.wait_ge(prob_ready, i + 1)
                    if i >= 2:
                        pe.wait_ge(turned_copied, i - 1)
                    for j in range(b + 1):
                        last = pe.transpose(bank[2 + i % 2][:, P * j:P * j + P], prob[i % 3][:, P * j:P * j + P], ident)
                    last.then_inc(turned, 1)

                def values(i):
                    h, b = items[i]
                    pe.wait_ge(turned_copied, i + 1)
                    if h >= 2 and b == 0:
                        pe.wait_ge(o_rest, h - 1)
                    for j in range(b + 1):
                        last = pe.matmul(bank[4 + h % 2][:, P * b:P * b + P], v_tok[:, j, P * h:P * h + P],
                                         prob_t[i % 3][:, P * j:P * j + P], start=j == 0, stop=j == b)
                    last.then_inc(valued, 1)

                for i in range(N + VALUE_LAG):
                    if i < N:
                        scores(i)
                    if TURN_LAG <= i < N + TURN_LAG:
                        turn(i - TURN_LAG)
                    if i >= VALUE_LAG:
                        values(i - VALUE_LAG)

            @block.vector
            def _(dve):
                def row_peak(i):
                    s, b = stat[i % 4], items[i][1]
                    dve.wait_ge(scores_ready, i + 1)
                    dve.reduce_max(s[:, 0:1], score_bank[i % 3][:, 0:P * (b + 1)], AX.X).then_inc(peak, 1)
                    dve.wait_ge(peak, i + 1)
                    dve.tensor_scalar(s[:, 1:2], s[:, 0:1], -ATT_SCALE, None, ALU.mult).then_inc(bias_ready, 1)

                def divide(i):
                    s, p = stat[i % 4], prob[i % 3][:, 0:P * (items[i][1] + 1)]
                    dve.wait_ge(exp_done, i + 1)
                    dve.reciprocal(s[:, 3:4], s[:, 2:3]).then_inc(inv_ready, 1)
                    dve.wait_ge(inv_ready, i + 1)
                    dve.tensor_scalar(p, p, s[:, 3:4], None, ALU.mult).then_inc(prob_ready, 1)

                def copy_turned(i):
                    cols = slice(0, P * (items[i][1] + 1))
                    dve.wait_ge(turned, i + 1)
                    if i >= 3:
                        dve.wait_ge(valued, i - 2)
                    dve.tensor_copy(prob_t[i % 3][:, cols], bank[2 + i % 2][:, cols]).then_inc(turned_copied, 1)

                def rest_of_head(h):
                    dve.wait_ge(o_rounded, h + 1)
                    dve.tensor_tensor(o_lo[:, h], bank[4 + h % 2][:], o_hi[:, h].bitcast(F32),
                                      ALU.subtract).then_inc(o_rest, 1)

                for i in range(N + COPY_LAG):
                    if i < N:
                        row_peak(i)
                    if 1 <= i <= N:
                        divide(i - 1)
                    if i >= COPY_LAG:
                        copy_turned(i - COPY_LAG)
                    if i >= 10 and i % TT == 2:
                        rest_of_head((i - 10) // TT)
                for h in range((N + COPY_LAG - 11) // TT + 1, HEADS):
                    rest_of_head(h)

            @block.scalar
            def _(act):
                def round_head(h):
                    act.wait_ge(valued, TT * (h + 1))
                    act.activation(o_hi[:, h], bank[4 + h % 2][:], ACT.Copy).then_inc(o_rounded, 1)

                for i in range(N):
                    s, b = stat[i % 4], items[i][1]
                    act.wait_ge(bias_ready, i + 1)
                    if i >= 3:
                        act.wait_ge(turned, i - 2)
                    act.activation(prob[i % 3][:, 0:P * (b + 1)], score_bank[i % 3][:, 0:P * (b + 1)], ACT.Exp,
                                   bias=s[:, 1:2], scale=ATT_SCALE, accum_out=s[:, 2:3]).then_inc(exp_done, 1)
                    if i >= 9 and i % TT == 1:
                        round_head((i - 9) // TT)
                for h in range((N - 10) // TT + 1, HEADS):
                    round_head(h)
        q_stack.close()
        mla_keep.close()

        def out_projection(name, n0, s_hi, s_lo, ada_at, edge, early=0):
            copied = sem(name + "_copied")
            with nc.Block() as block:
                @block.sync
                def _(sp):
                    for n in range(n0, n0 + 4):
                        if not (early and n == n0):
                            load_weights(sp, n + 2, src_of(n + 2))
                        for m in ada_at[n - n0]:
                            if m + 2 < 48:
                                load_ada(sp, m + 2)

                @block.tensor
                def _(pe):
                    for n in range(n0, n0 + 4):
                        pe.wait_ge(w_lo_ready, n + 1)
                        hi, lo = w_views(n, KD)
                        for i in range(2):
                            t = 2 * (n - n0) + i
                            if t >= 4:
                                pe.wait_ge(copied, t - 3)
                            first = early if t < 4 else 0
                            for k in range(first, KD):
                                last = product(pe, bank[t % 4][:], hi[:, k, P * i:P * i + P], lo[:, k, P * i:P * i + P],
                                               s_hi[:, k], s_lo[:, k], k == first, k == KD - 1)
                            last.then_inc(tile_done, 1)
                            for m in ada_at[n - n0 - 1] if i == 0 and n > n0 else ():
                                ada_reduce(pe, m)
                    for m in ada_at[3]:
                        ada_reduce(pe, m)

                @block.gpsimd
                def _(pool):
                    add_squares(pool, "edge_y", edge, (sq[1],))

                @block.scalar
                def _(act):
                    for n in range(n0, n0 + 4):
                        if not (early and n == n0):
                            round_weights(act, n + 1)
                        for i in range(2):
                            t = 2 * (n - n0) + i
                            act.wait_ge(tile_done, tiles_to[n0] + t + 1)
                            if early and t < 4:
                                act.wait_ge(copied, t + 1)
                                square_y(act, edge, t, y[:, t])
                            else:
                                square_y(act, edge, t, bank[t % 4][:])
                                act.activation(y[:, t], bank[t % 4][:], ACT.Copy).then_inc(copied, 1)

                @block.vector
                def _(dve):
                    for n in range(n0, n0 + 4):
                        for t in (2 * (n - n0), 2 * (n - n0) + 1) if early and n < n0 + 2 else ():
                            dve.wait_ge(tile_done, tiles_to[n0] + t + 1)
                            dve.tensor_tensor(y[:, t], y[:, t], bank[t % 4][:], ALU.add).then_inc(copied, 1)
                        if not (early and n == n0):
                            rest_weights(dve, n + 1)
                        for m in ada_at[n - n0]:
                            ada_multiply(dve, m)
                        for m in ada_at[n - n0]:
                            ada_finish(dve, m)

        out_projection("mla_o", N_WO, o_hi, o_lo, ADA_OUT, 0)
        o_stack.close()

        def mlp(name, l, n0, f_hi, f_lo, with_ada):
            edge = 2 * l
            u_stack = ExitStack()
            u_hi = sb(u_stack, name + "_u_hi", [P, 8, SEQ], F32R, side="right")
            u_lo = sb(u_stack, name + "_u_lo", [P, 8, SEQ], F32R, side="right")
            relu = [sb(u_stack, f"{name}_relu{i}", [P, SEQ], side="right") for i in range(2)]
            usq = [sb(u_stack, f"{name}_usq{i}", [P, SEQ], side="right") for i in range(2)]
            relu_done, u_rounded, u_squared = sem("relu_done"), sem("u_rounded"), sem("u_squared")
            u_rest, y_added = sem("u_rest"), sem("y_added")
            u0, y0 = 32 * l, 34 * l
            t0 = tiles_to[n0]

            def groups(eng, body):
                body(0, False)
                with eng.Fori(1, 3) as g:
                    body(g, False)
                body(3, True)

            def has_ada(j, final):
                return with_ada and (j < 4 or not final)

            with nc.Block() as block:
                @block.sync
                def _(sp):
                    def body(g, final):
                        for j in range(8):
                            if not final:
                                jj = (j + 2) % 8
                                load_weights(sp, n0 + j + 2, ffn_src(l, jj, g + (j + 2) // 8), g)
                            elif n0 + 24 + j + 2 < N_END:
                                load_weights(sp, n0 + 24 + j + 2, src_of(n0 + 24 + j + 2))
                            if has_ada(j + 2 if final else j, final):
                                load_ada(sp, ADA_MLP + j + 2, g)
                    groups(sp, body)

                @block.tensor
                def _(pe):
                    edge_pe(pe, edge, True)

                    def body(g, final):
                        for j in range(8):
                            n = n0 + j
                            pe.wait_ge(w_lo_ready, n + 1 + 8 * g)
                            hi, lo = w_views(n, KD)
                            if j == 0:
                                for k in range(KD):
                                    pe.wait_ge(h_lo_ready, KD * (edge + 1) + k + 1)
                                    for i in range(2):
                                        last = product(pe, bank[i][:], hi[:, k, P * i:P * i + P],
                                                       lo[:, k, P * i:P * i + P], f_hi[:, k], f_lo[:, k],
                                                       k == 0, k == KD - 1)
                                        if k == KD - 1:
                                            last.then_inc(tile_done, 1)
                            for i in range(2 if j else 0):
                                t = 2 * j + i
                                if j < 4:
                                    if t >= 4:
                                        pe.wait_ge(relu_done, u0 + t - 3 + 8 * g)
                                    ps, m_hi, m_lo = bank[t % 4][:], f_hi, f_lo
                                else:
                                    pe.wait_ge(y_added, y0 + t - 7 + 8 * g)
                                    ps, m_hi, m_lo = bank[4 + t % 2][:], u_hi, u_lo
                                for k in range(KD):
                                    if t == 8:
                                        pe.wait_ge(u_rest, u0 + k + 1 + 8 * g)
                                    last = product(pe, ps, hi[:, k, P * i:P * i + P], lo[:, k, P * i:P * i + P],
                                                   m_hi[:, k], m_lo[:, k], k == 0, k == KD - 1)
                                last.then_inc(tile_done, 1)
                                if i == 0 and has_ada(j - 1, final):
                                    ada_reduce(pe, ADA_MLP + j - 1, g)
                            if j == 7 and has_ada(7, final):
                                ada_reduce(pe, ADA_MLP + 7, g)
                    groups(pe, body)

                @block.gpsimd
                def _(pool):
                    edge_pool(pool, edge, usq)
                    for i in range(2):
                        pool.memset(y[:, 4 * i:4 * i + 4], 0.0).then_inc(y_added, 1)
                    add_squares(pool, "edge_y", edge + 1, (sq[1],))

                @block.scalar
                def _(act):
                    edge_act(act, edge, (l, 3), usq, relu, f_hi, n0 + 1)

                    def body(g, final):
                        for j in range(8):
                            for i in range(2 if j < 4 else 0):
                                t = 2 * j + i
                                act.wait_ge(tile_done, t0 + t + 1 + 16 * g)
                                if t >= 2:
                                    act.wait_ge(u_rest, u0 + t - 1 + 8 * g)
                                act.activation(relu[t % 2][:], bank[t % 4][:], ACT.Relu).then_inc(relu_done, 1)
                                act.wait_ge(relu_done, u0 + t + 1 + 8 * g)
                                act.activation(u_hi[:, t], relu[t % 2][:], ACT.Square).then_inc(u_rounded, 1)
                            for t in range(2 * j - 8, 2 * j - 6) if final and j >= 4 else ():
                                act.wait_ge(y_added, y0 + 2 + 24 + t + 1)
                                square_y(act, edge + 1, t, y[:, t])
                            if not final or (j < 7 and n0 + 24 + j + 2 < N_END):
                                round_weights(act, n0 + j + 2, g)
                    groups(act, body)

                @block.vector
                def _(dve):
                    edge_dve(dve, edge, (l, 2), (l, 3), usq, relu, f_hi, f_lo, n0 + 1)

                    def body(g, final):
                        for j in range(8):
                            if has_ada(j, final):
                                ada_multiply(dve, ADA_MLP + j, g)
                            if j < 4:
                                for i in range(2):
                                    t = 2 * j + i
                                    dve.wait_ge(relu_done, u0 + t + 1 + 8 * g)
                                    dve.tensor_tensor(usq[t % 2][:], relu[t % 2][:], relu[t % 2][:],
                                                      ALU.mult).then_inc(u_squared, 1)
                                    dve.wait_ge(u_squared, u0 + t + 1 + 8 * g)
                                    dve.wait_ge(u_rounded, u0 + t + 1 + 8 * g)
                                    dve.tensor_tensor(u_lo[:, t], usq[t % 2][:], u_hi[:, t].bitcast(F32),
                                                      ALU.subtract).then_inc(u_rest, 1)
                                    if j and i == 0 and has_ada(j - 1, final):
                                        ada_finish(dve, ADA_MLP + j - 1, g)
                            else:
                                for i in range(2):
                                    t = 2 * j + i
                                    dve.wait_ge(tile_done, t0 + t + 1 + 16 * g)
                                    dve.wait_ge(y_added, y0 + t - 6 + 8 * g)
                                    dve.tensor_tensor(y[:, t - 8], y[:, t - 8], bank[4 + t % 2][:],
                                                      ALU.add).then_inc(y_added, 1)
                                    if i == 0 and has_ada(j - 1, final):
                                        ada_finish(dve, ADA_MLP + j - 1, g)
                            if j == 7 and has_ada(7, final):
                                ada_finish(dve, ADA_MLP + 7, g)
                            if not final or (j < 7 and n0 + 24 + j + 2 < N_END):
                                rest_weights(dve, n0 + j + 2, g)
                    groups(dve, body)
            u_stack.close()

        PAIRS = HEADS // 2
        EARLY_HEADS = HEADS - 2
        pre_copied, z_done, conv_step, conv_silu = sem("pre_copied"), sem("z_done"), sem("conv_step"), sem("conv_silu")
        hn_squared, hn_summed, hn_root, hn_inv, hn_spread, hn_scaled = (
            sem("hn_" + v) for v in ("squared", "summed", "root", "inv", "spread", "scaled"))
        names = ("gram", "turned", "kv_used", "diff", "grow_exp", "decay_exp", "core_dve", "off", "w_ready",
                 "w_copied", "step_ready", "stepped", "uw_ready", "uw_copied")
        (gram, turned_kv, kv_used, diff, grow_exp, decay_exp, core_dve, off, w_ready, w_copied, step_ready,
         stepped, uw_ready, uw_copied) = (sem("core_" + v) for v in names)
        scan_ws, scan_new, scan_kv, scan_state = (sem("scan_" + v) for v in ("ws", "new", "kv", "state"))
        on_squared, on_summed, on_root, on_inv, on_spread, on_step, on_hi = (
            sem("on_" + v) for v in ("squared", "summed", "root", "inv", "spread", "step", "hi"))
        N_CH = SEQ // CHUNK
        part_done, part_copied = sem("part_done"), sem("part_copied")
        FILL_FRONT = ((0, 5), (5, 9), (9, 13), (13, 17))
        FILL_W = ((17, 19), (20, 23), (26, 29), (31, 34), (36, 39), (42, 45))
        FILL_STEP = ((19, 20), (23, 26), (29, 31), (34, 36), (39, 42), (45, 48))

        def flat(v):
            return v.rearrange("p t c -> p (t c)")

        def over_tiles(v):
            return v.unsqueeze(1).to_broadcast([P, TT, P])

        def token_scalar(v, h):
            return v[:, :, h:h + 1].to_broadcast([P, TT, P])

        def tiles4(v):
            return v.rearrange("p (t c) -> p t c", t=TT)

        def halves(v, l, which):
            m = 1 << l
            return v.rearrange("p (b two m) -> p b two m", two=2, m=m)[:, :, which, :]

        def packed(v, l):
            return v.rearrange("p (b m) -> p b m", m=1 << l)

        def first_chunk(q):
            return N_GDN + 4 * q

        def proj_bank(q, t):
            return bank[t % 4] if q == 0 else bank[7 - t % 2]

        def stat_bank(q, j):
            return bank[4 + j] if q == 0 else bank[j]

        def hn_sum_cols(q):
            return bank[4][:, 0:4 * TT] if q == 0 else bank[6][:, 0:4 * TT]

        def project(pe, q, steps, h_hi, h_lo):
            for s in steps:
                t, k = s // KD, s % KD
                if k == 0:
                    pe.wait_ge(w_lo_ready, first_chunk(q) + t // 2 + 1)
                    ahead = 4 if q == 0 else 2
                    if q and t == 7:
                        pe.wait_ge(hn_root, 2 * q + 2)
                    if t >= ahead:
                        pe.wait_ge(pre_copied, 6 * q + t - ahead + 1)
                    elif q and t == 1:
                        pe.wait_ge(core_dve, 8 * (q - 1) + 3)
                hi, lo = w_views(first_chunk(q) + t // 2, KD)
                cols = slice(P * (t % 2), P * (t % 2) + P)
                last = product(pe, proj_bank(q, t)[:], hi[:, k, cols], lo[:, k, cols], h_hi[:, k], h_lo[:, k],
                               k == 0, k == KD - 1)
                if k == KD - 1:
                    last.then_inc(tile_done, 1)

        def copy_pre(act, q, t, pre):
            act.wait_ge(tile_done, tiles_to[first_chunk(q)] + t + 1)
            act.wait_ge(conv_step, 2 + 24 * q + (4 * (t - 1) if t >= 2 else 0))
            act.activation(pre[t % 2][:, CONV - 1:], proj_bank(q, t)[:], ACT.Copy).then_inc(pre_copied, 1)

        def silu_conv(act, q, t, dst):
            act.wait_ge(conv_step, 2 + 24 * q + 4 * t + 4)
            act.activation(dst[t], dst[t], ACT.Silu).then_inc(conv_silu, 1)

        def silu_z(act, q, i, z_t):
            act.wait_ge(tile_done, tiles_to[first_chunk(q)] + 6 + i + 1)
            act.activation(z_t[:, i], proj_bank(q, 6 + i)[:], ACT.Silu).then_inc(z_done, 1)

        def convolve(dve, q, t, pre, dst):
            dve.wait_ge(pre_copied, 6 * q + t + 1)
            for j in range(CONV):
                at = V_CONV + 24 * j + 8 * (t // 2) + 2 * q + t % 2
                tap, w = pre[t % 2][:, j:j + SEQ], vec[:, at:at + 1]
                if j == 0:
                    dve.tensor_scalar(dst[t], tap, w, None, ALU.mult).then_inc(conv_step, 1)
                else:
                    dve.wait_ge(conv_step, 2 + 24 * q + 4 * t + j)
                    dve.scalar_tensor_tensor(dst[t], tap, w, dst[t], ALU.mult, ALU.add).then_inc(conv_step, 1)

        def square_head(act, q, j, dst):
            act.wait_ge(conv_silu, 6 * q + 6)
            if j >= 2:
                act.wait_ge(hn_summed, 4 * q + j - 1)
            act.activation(sq[j % 2][:], dst[j], ACT.Square).then_inc(hn_squared, 1)

        def sum_head(pe, q, j):
            pe.wait_ge(hn_squared, 4 * q + j + 1)
            for t in range(TT):
                last = pe.matmul(hn_sum_cols(q)[:, TT * j + t:TT * j + t + 1], sq[j % 2][:, P * t:P * t + P],
                                 ones[:, 0:1], start=True, stop=True)
            last.then_inc(hn_summed, 1)

        def root_heads(act, q, hn_tok):
            act.wait_ge(hn_summed, 4 * q + 4)
            sums = hn_sum_cols(q)
            act.activation(hn_tok[:, 0:2 * TT], sums[:, 0:2 * TT], ACT.Sqrt, bias=bias_t[:, 1:2],
                           scale=float(P)).then_inc(hn_root, 1)
            act.activation(hn_tok[:, 2 * TT:], sums[:, 2 * TT:], ACT.Sqrt, bias=bias_t[:, 0:1]).then_inc(hn_root, 1)

        def invert_heads(dve, q, hn_tok):
            dve.wait_ge(hn_root, 2 * q + 2)
            dve.reciprocal(hn_tok[:], hn_tok[:]).then_inc(hn_inv, 1)

        def spread_heads(pe, q, hn_tok):
            pe.wait_ge(hn_inv, q + 1)
            for j in range(4):
                for t in range(TT):
                    last = pe.matmul(stat_bank(q, j)[:, P * t:P * t + P],
                                     hn_tok[:, TT * j + t:TT * j + t + 1].to_broadcast([P, P]), ident,
                                     start=True, stop=True)
                last.then_inc(hn_spread, 1)

        def scale_heads(dve, q, dst):
            for j in range(4):
                dve.wait_ge(hn_spread, 4 * q + j + 1)
                dve.tensor_tensor(dst[j], dst[j], stat_bank(q, j)[:], ALU.mult)

        def project_out_part(pe, steps):
            for s in steps:
                t, k = s // EARLY_HEADS, s % EARLY_HEADS
                if k == 0:
                    pe.wait_ge(w_lo_ready, N_GWO + t // 2 + 1)
                    if t >= 2:
                        pe.wait_ge(part_copied, t - 1)
                    elif t == 1:
                        pe.wait_ge(core_dve, 8 * (PAIRS - 1) + 3)
                hi, lo = w_views(N_GWO + t // 2, KD)
                cols = slice(P * (t % 2), P * (t % 2) + P)
                last = product(pe, bank[7 - t % 2][:], hi[:, k, cols], lo[:, k, cols], o_hi[:, k], o_lo[:, k],
                               k == 0, k == EARLY_HEADS - 1)
                if k == EARLY_HEADS - 1:
                    last.then_inc(part_done, 1)

        def copy_out_part(act, t):
            act.wait_ge(part_done, t + 1)
            act.activation(y[:, t], bank[7 - t % 2][:], ACT.Copy).then_inc(part_copied, 1)

        def gdn_pair(pair, h_hi, h_lo, g_, g_cum, beta, beta_eg, to_end, end_decay, state, v_new, sets, pre, hn_tok, core):
            q = pair + 1
            more = q < PAIRS
            n_next = first_chunk(q)
            mine = sets[pair % 2]
            q_t, k_t, v_t, z_t = (mine[:, 2 * i:2 * i + 2] for i in range(4))
            other = sets[q % 2]
            dst = [other[:, i] for i in range(6)]
            z_next = other[:, 6:8]
            heads = (2 * pair, 2 * pair + 1)
            kbg, k_end, v_beta, decay, a_qk, l_t, inv_t = core
            w_t, u_tok, l_off = kbg, v_beta, decay
            prod, inv = (v.rearrange("p i (t c) -> p i t c", t=TT) for v in (k_t, v_t))
            grow = inv_t

            with nc.Block() as block:
                @block.sync
                def _(sp):
                    for n in range(n_next, n_next + 3) if more else (N_GWO,):
                        load_weights(sp, n + 2, src_of(n + 2))

                @block.tensor
                def _(pe):
                    def rows_of(i, ps, col):
                        for t in range(TT):
                            last = pe.matmul(ps[:, P * t:P * t + P], col[:, t, heads[i]:heads[i] + 1].to_broadcast([P, P]),
                                             ident, start=True, stop=True)
                        return last

                    def turn(ps, src):
                        for t in range(TT):
                            last = pe.transpose(ps[:, P * t:P * t + P], src[:, P * t:P * t + P], ident)
                        last.then_inc(turned_kv, 1)

                    def fill(a, b):
                        if more:
                            project(pe, q, range(a, b), h_hi, h_lo)
                        else:
                            project_out_part(pe, range(3 * a // 8, 3 * b // 8))

                    for i, h in enumerate(heads):
                        for t in range(TT):
                            tok, cols = slice(P * t, P * t + P), slice(P * t, P * t + P)
                            pe.matmul(bank[4 + i][:, cols], g_[:, t, h:h + 1].to_broadcast([P, P]),
                                      const[:, C_TRI:C_TRI + P], start=True, stop=True)
                            pe.matmul(bank[i][:, cols], k_t[:, i, tok], k_t[:, i, tok], start=True, stop=True)
                            last = pe.matmul(bank[2 + i][:, cols], k_t[:, i, tok], q_t[:, i, tok], start=True, stop=True)
                        last.then_inc(gram, 1)
                        if i == 0:
                            rows_of(0, bank[6], beta).then_inc(gram, 1)
                    fill(*FILL_FRONT[0])
                    pe.wait_ge(diff, 8 * pair + 4)
                    pe.wait_ge(grow_exp, 2 * pair + 1)
                    rows_of(1, bank[4], beta).then_inc(gram, 1)
                    pe.wait_ge(diff, 8 * pair + 8)
                    pe.wait_ge(grow_exp, 2 * pair + 2)
                    turn(bank[5], k_t[:, 0])
                    fill(*FILL_FRONT[1])
                    pe.wait_ge(core_dve, 8 * pair + 4)
                    turn(bank[2], v_t[:, 0])
                    fill(*FILL_FRONT[2])
                    pe.wait_ge(core_dve, 8 * pair + 7)
                    turn(bank[4], k_t[:, 1])
                    pe.wait_ge(core_dve, 8 * pair + 8)
                    turn(bank[3], v_t[:, 1])
                    fill(*FILL_FRONT[3])
                    for l in range(LEVELS):
                        for i in range(2):
                            pe.wait_ge(off, 12 * pair + 2 * l + i + 1)
                            if l:
                                pe.wait_ge(stepped, 22 * pair + 4 * (l - 1) + 2 * i + 2)
                            for t in range(TT):
                                last = pe.matmul(bank[i][:, P * t:P * t + P], l_off[:, i, t], inv[:, i, t] if l else ident,
                                                 start=True, stop=True)
                            last.then_inc(w_ready, 1)
                        fill(*FILL_W[l])
                        for i in range(2 if l else 0):
                            pe.wait_ge(w_copied, 10 * pair + 2 * (l - 1) + i + 1)
                            for t in range(TT):
                                cols = slice(P // 2 * t, P // 2 * t + P // 2)
                                if l < LEVELS - 1:
                                    pe.matmul(packed(bank[2 + i][:, cols], l), inv_t[:, i, t],
                                              halves(prod[:, i, t], l, 0), start=True, stop=True)
                                last = pe.matmul(packed(bank[4 + i][:, cols], l), prod[:, i, t],
                                                 halves(inv_t[:, i, t], l, 1), start=True, stop=True)
                            last.then_inc(step_ready, 1)
                        fill(*FILL_STEP[l])
                    for i in range(2):
                        pe.wait_ge(stepped, 22 * pair + 20 + i + 1)
                        for t in range(TT):
                            cols = slice(P * t, P * t + P)
                            pe.matmul(bank[i][:, cols], inv_t[:, i, t], v_beta[:, i, t], start=True, stop=True)
                            last = pe.matmul(bank[2 + i][:, cols], kbg[:, i, t], inv_t[:, i, t], start=True, stop=True)
                        last.then_inc(uw_ready, 1)

                @block.gpsimd
                def _(pool):
                    for l in range(LEVELS):
                        for i in range(2):
                            if l:
                                pool.wait_ge(w_ready, 12 * pair + 2 * (l - 1) + i + 1)
                                if l == 1:
                                    pool.wait_ge(stepped, 22 * pair + 2 * i + 2)
                            else:
                                pool.wait_ge(core_dve, 8 * pair + 4 * i + 4)
                            mask = const[:, C_LEVEL + P * l:C_LEVEL + P * l + P]
                            pool.tensor_tensor(l_off[:, i], l_t[:, i], over_tiles(mask), ALU.mult).then_inc(off, 1)

                @block.scalar
                def _(act):
                    def copy_w(l):
                        for i in range(2):
                            act.wait_ge(w_ready, 12 * pair + 2 * l + i + 1)
                            act.activation(flat(prod[:, i]), bank[i][:], ACT.Copy).then_inc(w_copied, 1)

                    round_weights(act, n_next + 1)
                    for i in range(2):
                        act.wait_ge(diff, 8 * pair + 4 * i + 4)
                        act.activation(flat(decay[:, i]), flat(decay[:, i]), ACT.Exp).then_inc(decay_exp, 1)
                        act.activation(flat(grow[:, i]), bank[4 + i][:], ACT.Exp).then_inc(grow_exp, 1)
                    after = {0: (("pre", 0), ("pre", 1), ("round", 2)), 1: (("silu", 0), ("pre", 2)),
                             2: (("silu", 1), ("pre", 3)), 3: (("silu", 2), ("round", 3)),
                             4: (("silu", 3), ("pre", 4)), 5: (("silu", 4), ("pre", 5))}
                    for l in range(LEVELS):
                        if l:
                            copy_w(l)
                        for what, v in after[l] if more else ():
                            if what == "pre":
                                copy_pre(act, q, v, pre)
                            elif what == "silu":
                                silu_conv(act, q, v, dst)
                            else:
                                round_weights(act, n_next + v)
                        if not more and l in (0, 3, 5):
                            copy_out_part(act, (0, 3, 5).index(l))
                    for i in range(2):
                        act.wait_ge(uw_ready, 2 * pair + i + 1)
                        act.activation(flat(u_tok[:, i]), bank[i][:], ACT.Copy).then_inc(uw_copied, 1)
                        act.activation(flat(w_t[:, i]), bank[2 + i][:], ACT.Copy).then_inc(uw_copied, 1)
                    if more:
                        silu_conv(act, q, 5, dst)

                @block.vector
                def _(dve):
                    for i, h in enumerate(heads):
                        dve.wait_ge(gram, 4 * pair + (1, 3)[i])
                        for t in range(TT):
                            dve.tensor_scalar(decay[:, i, t], bank[4 + i][:, P * t:P * t + P], g_cum[:, t, h:h + 1], 0.0,
                                              ALU.subtract, ALU.min).then_inc(diff, 1)
                    for i in range(2):
                        at = 8 * pair + 4 * i
                        dve.wait_ge(decay_exp, 2 * pair + i + 1)
                        dve.tensor_tensor(decay[:, i], decay[:, i], over_tiles(const[:, C_TRI:C_TRI + P]),
                                          ALU.mult).then_inc(core_dve, 1)
                        dve.wait_ge(core_dve, at + 1)
                        dve.tensor_tensor(flat(l_t[:, i]), flat(decay[:, i]), bank[i][:], ALU.mult).then_inc(core_dve, 1)
                        dve.wait_ge(core_dve, at + 2)
                        dve.wait_ge(gram, 4 * pair + (2, 4)[i])
                        beta_row = bank[(6, 4)[i]]
                        dve.tensor_tensor(flat(l_t[:, i]), flat(l_t[:, i]), beta_row[:], ALU.mult).then_inc(core_dve, 1)
                        dve.tensor_tensor(flat(a_qk[:, i]), flat(decay[:, i]), bank[2 + i][:], ALU.mult).then_inc(core_dve, 1)
                    for i, h in enumerate(heads):
                        dve.tensor_tensor(q_t[:, i], flat(grow[:, i]), q_t[:, i], ALU.mult).then_inc(kv_used, 1)
                        dve.wait_ge(turned_kv, 4 * pair + 2 * i + 1)
                        for dst_, f in ((kbg, beta_eg), (k_end, to_end)):
                            dve.tensor_tensor(dst_[:, i], tiles4(bank[5 - i][:]), token_scalar(f, h), ALU.mult).then_inc(kv_used, 1)
                        dve.wait_ge(turned_kv, 4 * pair + 2 * i + 2)
                        dve.tensor_tensor(v_beta[:, i], tiles4(bank[2 + i][:]), token_scalar(beta, h), ALU.mult).then_inc(kv_used, 1)
                    rest_weights(dve, n_next + 1)
                    dve.wait_ge(kv_used, 8 * pair + 8)
                    after = {0: (("conv", 0), ("rest", 2)), 1: (("conv", 1),), 2: (("conv", 2),), 3: (("conv", 3), ("rest", 3)),
                             4: (("conv", 4),), 5: (("conv", 5),)}
                    for l in range(LEVELS):
                        for i in range(2):
                            if l == 0:
                                dve.wait_ge(w_ready, 12 * pair + i + 1)
                                dve.tensor_tensor(inv[:, i], over_tiles(ident), tiles4(bank[i][:]), ALU.subtract).then_inc(stepped, 1)
                                dve.tensor_tensor(inv_t[:, i], over_tiles(ident), l_off[:, i], ALU.subtract).then_inc(stepped, 1)
                            else:
                                dve.wait_ge(step_ready, 10 * pair + 2 * (l - 1) + i + 1)
                                if l < LEVELS - 1:
                                    part = halves(flat(inv[:, i]), l, 0)
                                    dve.tensor_tensor(part, part, packed(bank[2 + i][:, 0:SEQ // 2], l), ALU.subtract).then_inc(stepped, 1)
                                part = halves(flat(inv_t[:, i]), l, 1)
                                dve.tensor_tensor(part, part, packed(bank[4 + i][:, 0:SEQ // 2], l), ALU.subtract).then_inc(stepped, 1)
                        for what, v in after[l] if more else ():
                            if what == "conv":
                                convolve(dve, q, v, pre, dst)
                            else:
                                rest_weights(dve, n_next + v)

            o_n, o_f = (inv, inv_t)
            on_sums = bank[0][:, 0:2 * TT]
            with nc.Block() as block:
                @block.sync
                def _(sp):
                    if more:
                        load_weights(sp, n_next + 5, src_of(n_next + 5))

                @block.tensor
                def _(pe):
                    def fill(a, b):
                        if more:
                            project(pe, q, range(a, b), h_hi, h_lo)

                    for n in range(N_CH):
                        t, r = n // 2, CHUNK * (n % 2)
                        cols = slice(CHUNK * n, CHUNK * n + CHUNK)
                        for i in range(2):
                            pe.wait_ge(scan_state, (2 * N_CH + 1) * pair + (2 * n + i if n else 1))
                            pe.matmul(bank[i][r:r + CHUNK, 0:P], flat(w_t[:, i])[:, cols], state[:, i], start=True,
                                      stop=True).then_inc(scan_ws, 1)
                            pe.matmul(bank[4 + i][:, cols], state[:, i], q_t[:, i, cols], start=True, stop=False)
                        fill(48 + 3 * n // 2, 48 + 3 * (n + 1) // 2)
                        for i in range(2):
                            pe.wait_ge(scan_new, 2 * (N_CH * pair + n) + i + 1)
                            vn = v_new[r:r + CHUNK, i]
                            pe.matmul(bank[4 + i][:, cols], vn, a_qk[r:r + CHUNK, i, t, r:r + CHUNK], start=False, stop=True)
                            pe.matmul(bank[2 + i][:, 0:P], k_end[r:r + CHUNK, i, t], vn, start=True,
                                      stop=True).then_inc(scan_kv, 1)
                        if more and n < 4:
                            sum_head(pe, q, n)
                        if not more and n < EARLY_HEADS:
                            project_out_part(pe, (3 * EARLY_HEADS + n,))
                    fill(60, 62)
                    for i in range(2):
                        pe.wait_ge(on_squared, 2 * pair + i + 1)
                        for t in range(TT):
                            last = pe.matmul(on_sums[:, TT * i + t:TT * i + t + 1], sq[i][:, P * t:P * t + P], ones[:, 0:1],
                                             start=True, stop=True)
                    last.then_inc(on_summed, 1)
                    fill(62, 64)
                    pe.wait_ge(on_inv, pair + 1)
                    if more:
                        pe.wait_ge(scan_state, (2 * N_CH + 1) * (pair + 1))
                        spread_heads(pe, q, hn_tok)
                        pe.wait_ge(z_done, 2 * q + 2)
                    for i in range(2):
                        for t in range(TT):
                            last = pe.matmul(bank[6 + i][:, P * t:P * t + P],
                                             rms_tok[:, TT * i + t:TT * i + t + 1].to_broadcast([P, P]), ident,
                                             start=True, stop=True)
                        last.then_inc(on_spread, 1)

                @block.vector
                def _(dve):
                    dve.memset(state[:], 0.0).then_inc(scan_state, 1)
                    for n in range(N_CH):
                        t, r = n // 2, CHUNK * (n % 2)
                        for i in range(2):
                            dve.wait_ge(scan_ws, 2 * (N_CH * pair + n) + i + 1)
                            dve.tensor_tensor(v_new[r:r + CHUNK, i], u_tok[r:r + CHUNK, i, t], bank[i][r:r + CHUNK, 0:P],
                                              ALU.subtract).then_inc(scan_new, 1)
                        for i, h in enumerate(heads):
                            dve.wait_ge(scan_kv, 2 * (N_CH * pair + n) + i + 1)
                            dve.scalar_tensor_tensor(state[:, i], state[:, i], end_decay[:, n % 2, t, h:h + 1],
                                                     bank[2 + i][:, 0:P], ALU.mult, ALU.add).then_inc(scan_state, 1)
                    if more:
                        invert_heads(dve, q, hn_tok)
                    for i in range(2):
                        dve.wait_ge(on_squared, 2 * pair + i + 1)
                        dve.scalar_tensor_tensor(flat(o_n[:, i]), bank[4 + i][:], vec[:, V_ON:V_ON + 1], z_t[:, i],
                                                 ALU.mult, ALU.mult).then_inc(on_step, 1)
                    dve.wait_ge(on_root, pair + 1)
                    dve.reciprocal(rms_tok[:], rms_tok[:]).then_inc(on_inv, 1)
                    if more:
                        rest_weights(dve, n_next + 4)
                        scale_heads(dve, q, dst)
                    dve.wait_ge(on_step, 4 * pair + 2)
                    for i in range(2):
                        dve.wait_ge(on_spread, 2 * pair + i + 1)
                        dve.tensor_tensor(flat(o_f[:, i]), flat(o_n[:, i]), bank[6 + i][:], ALU.mult).then_inc(on_step, 1)
                    for i, h in enumerate(heads):
                        dve.wait_ge(on_hi, 2 * pair + i + 1)
                        dve.tensor_tensor(o_lo[:, h], flat(o_f[:, i]), o_hi[:, h].bitcast(F32), ALU.subtract)

                @block.scalar
                def _(act):
                    if more:
                        for j in range(4):
                            square_head(act, q, j, dst)
                        root_heads(act, q, hn_tok)
                        round_weights(act, n_next + 4)
                        silu_z(act, q, 0, z_next)
                    else:
                        copy_out_part(act, 3)
                    for i in range(2):
                        act.wait_ge(scan_kv, 2 * N_CH * (pair + 1) - 1 + i)
                        act.activation(sq[i][:], bank[4 + i][:], ACT.Square).then_inc(on_squared, 1)
                    act.wait_ge(on_summed, pair + 1)
                    act.activation(rms_tok[:], on_sums, ACT.Sqrt, bias=bias_t[:, 0:1], scale=1 / P).then_inc(on_root, 1)
                    if more:
                        silu_z(act, q, 1, z_next)
                    for i, h in enumerate(heads):
                        act.wait_ge(on_step, 4 * pair + 3 + i)
                        act.activation(o_hi[:, h], flat(o_f[:, i]), ACT.Copy).then_inc(on_hi, 1)

        def gdn(h_hi, h_lo):
            st = ExitStack()
            g_, beta, g_cum = (sb(st, v, [P, TT, HEADS]) for v in ("g_", "beta", "g_cum"))
            beta_eg = sb(st, "beta_eg", [P, TT, HEADS])
            to_end = sb(st, "to_end", [P, TT, HEADS])
            end_decay = sb(st, "end_decay", [P, 2, TT, HEADS])
            state = sb(st, "state", [P, 2, P])
            v_new = sb(st, "v_new", [P, 2, P])
            hn_tok = sb(st, "hn_tok", [P, 4 * TT])
            sets = (y, sb(st, "qkvz_odd", [P, KD, SEQ]))
            pre = [sb(st, f"pre{i}", [P, CONV - 1 + SEQ]) for i in range(2)]
            temp = ExitStack()
            hf, xr = ([sb(temp, f"{v}{i}_gdn", [P, SEQ]) for i in range(2)] for v in ("hf", "xr"))
            t_, abs_, e_, u_, ln_ = (sb(temp, f"gate_temp{i}", [P, TT, HEADS]) for i in range(5))
            ba = sb(temp, "ba", [P, TT, 2 * HEADS])
            ba_f = sb(temp, "ba_f", [2 * HEADS, SEQ])
            w_ba = sb(temp, "w_ba", [P, KD, 2 * HEADS])
            w_ba_hi = sb(temp, "w_ba_hi", [P, KD, 2 * HEADS], F32R)
            w_ba_lo = sb(temp, "w_ba_lo", [P, KD, 2 * HEADS], F32R)
            head_in = sb(temp, "head_in", [P, 2, HEADS])

            def per_token(v):
                return v.rearrange("p t h -> p (t h)")

            dst, z_first, n0 = [y[:, i] for i in range(6)], y[:, 6:8], first_chunk(0)
            gate_in, gate_step, gate_act, gate_pe = sem("gate_in"), sem("gate_step"), sem("gate_act"), sem("gate_pe")
            with nc.Block() as block:
                @block.sync
                def _(sp):
                    sp.dma_start(w_ba[:], rows(a["gdn_w_in"][0], KD)[:, :, QKV_W:QKV_W + 2 * HEADS]).then_inc(gate_in, 16)
                    for i, name in enumerate(("gdn_a_log", "gdn_dt_bias")):
                        sp.dma_start(head_in[:, i], a[name].to_broadcast([P, HEADS])).then_inc(gate_in, 16)
                    for n in range(n0, n0 + 4):
                        load_weights(sp, n + 2, src_of(n + 2))

                @block.scalar
                def _(act):
                    def round_ba():
                        act.wait_ge(gate_in, 48)
                        act.activation(w_ba_hi[:], w_ba[:], ACT.Copy).then_inc(gate_act, 1)
                    edge_act(act, 1, (1, 0), hf, xr, h_hi, n0 + 1, round_ba)
                    act.wait_ge(gate_pe, 1)
                    act.activation(ba_f[:], bank[4][0:2 * HEADS, :], ACT.Copy).then_inc(gate_act, 1)
                    copy_pre(act, 0, 0, pre)
                    copy_pre(act, 0, 1, pre)
                    act.wait_ge(gate_pe, 2)
                    act.activation(ba[:], bank[5][:, 0:TT * 2 * HEADS], ACT.Copy).then_inc(gate_act, 1)
                    round_weights(act, n0 + 2)
                    silu_conv(act, 0, 0, dst)
                    copy_pre(act, 0, 2, pre)
                    act.wait_ge(gate_step, 4)
                    act.activation(e_[:], abs_[:], ACT.Exp, scale=-1.0).then_inc(gate_act, 1)
                    act.activation(head_in[:, 0], head_in[:, 0], ACT.Exp).then_inc(gate_act, 1)
                    silu_conv(act, 0, 1, dst)
                    copy_pre(act, 0, 3, pre)
                    act.wait_ge(gate_step, 5)
                    act.activation(ln_[:], u_[:], ACT.Ln).then_inc(gate_act, 1)
                    act.activation(beta[:], ba[:, :, 0:HEADS], ACT.Sigmoid).then_inc(gate_act, 1)
                    round_weights(act, n0 + 3)
                    silu_conv(act, 0, 2, dst)
                    copy_pre(act, 0, 4, pre)
                    silu_conv(act, 0, 3, dst)
                    copy_pre(act, 0, 5, pre)
                    silu_conv(act, 0, 4, dst)
                    round_weights(act, n0 + 4)
                    silu_z(act, 0, 0, z_first)
                    silu_conv(act, 0, 5, dst)
                    act.wait_ge(gate_step, 15)
                    act.activation(per_token(beta_eg[:]), per_token(g_cum[:]), ACT.Exp).then_inc(gate_act, 1)
                    act.activation(to_end[:], to_end[:], ACT.Exp).then_inc(gate_act, 1)
                    act.activation(end_decay[:].rearrange("p i t h -> p (i t h)"), bank[5][:, 0:64],
                                   ACT.Exp).then_inc(gate_act, 1)
                    for j in range(4):
                        square_head(act, 0, j, dst)
                    silu_z(act, 0, 1, z_first)
                    root_heads(act, 0, hn_tok)

                @block.vector
                def _(dve):
                    def step(ins, n):
                        ins.then_inc(gate_step, 1)
                        dve.wait_ge(gate_step, n)
                    for i in range(2):
                        dve.memset(pre[i][:, 0:CONV - 1], 0.0).then_inc(conv_step, 1)

                    def rest_ba():
                        dve.wait_ge(gate_act, 1)
                        step(dve.tensor_tensor(w_ba_lo[:], w_ba[:], w_ba_hi[:].bitcast(F32), ALU.subtract), 1)
                    edge_dve(dve, 1, (0, 5), (1, 0), hf, xr, h_hi, h_lo, n0 + 1, rest_ba)
                    convolve(dve, 0, 0, pre, dst)
                    dve.wait_ge(gate_act, 3)
                    bias = head_in[:, 1:2].to_broadcast([P, TT, HEADS])
                    step(dve.tensor_tensor(t_[:], ba[:, :, HEADS:], bias, ALU.add), 2)
                    step(dve.scalar_tensor_tensor(abs_[:], t_[:], -1.0, t_[:], ALU.mult, ALU.max), 3)
                    step(dve.tensor_scalar(t_[:], t_[:], 0.0, None, ALU.max), 4)
                    convolve(dve, 0, 1, pre, dst)
                    rest_weights(dve, n0 + 2)
                    dve.wait_ge(gate_act, 4)
                    step(dve.tensor_scalar(u_[:], e_[:], 1.0, None, ALU.add), 5)
                    step(dve.scalar_tensor_tensor(e_[:], u_[:], -1.0, e_[:], ALU.add, ALU.subtract), 6)
                    convolve(dve, 0, 2, pre, dst)
                    dve.wait_ge(gate_act, 6)
                    step(dve.reciprocal(u_[:], u_[:]), 7)
                    step(dve.tensor_tensor(e_[:], e_[:], u_[:], ALU.mult), 8)
                    step(dve.tensor_tensor(ln_[:], ln_[:], e_[:], ALU.subtract), 9)
                    step(dve.tensor_tensor(t_[:], t_[:], ln_[:], ALU.add), 10)
                    step(dve.tensor_scalar(t_[:], t_[:], -1.0, None, ALU.mult), 11)
                    step(dve.tensor_tensor(g_[:], t_[:], head_in[:, 0:1].to_broadcast([P, TT, HEADS]), ALU.mult), 12)
                    convolve(dve, 0, 3, pre, dst)
                    rest_weights(dve, n0 + 3)
                    convolve(dve, 0, 4, pre, dst)
                    convolve(dve, 0, 5, pre, dst)
                    dve.wait_ge(gate_pe, 3)
                    step(dve.tensor_copy(per_token(g_cum[:]), bank[4][:, 0:32]), 13)
                    step(dve.tensor_copy(per_token(to_end[:]), bank[4][:, 32:64]), 14)
                    step(dve.tensor_tensor(to_end[:], to_end[:], g_cum[:], ALU.subtract), 15)
                    dve.wait_ge(gate_act, 8)
                    dve.tensor_tensor(beta_eg[:], beta_eg[:], beta[:], ALU.mult)
                    rest_weights(dve, n0 + 4)
                    invert_heads(dve, 0, hn_tok)
                    scale_heads(dve, 0, dst)

                @block.gpsimd
                def _(pool):
                    edge_pool(pool, 1, hf)

                @block.tensor
                def _(pe):
                    edge_pe(pe, 1, True)
                    pe.wait_ge(gate_step, 1)
                    for k in range(KD):
                        pe.wait_ge(h_lo_ready, 2 * KD + k + 1)
                        last = product(pe, bank[4][0:2 * HEADS, :], w_ba_hi[:, k], w_ba_lo[:, k], h_hi[:, k],
                                       h_lo[:, k], k == 0, k == KD - 1)
                        if k == KD - 1:
                            last.then_inc(gate_pe, 1)
                        project(pe, 0, (k, KD + k), h_hi, h_lo)
                    project(pe, 0, range(2 * KD, 3 * KD), h_hi, h_lo)
                    pe.wait_ge(gate_act, 2)
                    for t in range(TT):
                        last = pe.transpose(bank[5][:, 16 * t:16 * t + 16], ba_f[0:2 * HEADS, P * t:P * t + P],
                                            ident[0:2 * HEADS, 0:2 * HEADS])
                    last.then_inc(gate_pe, 1)
                    project(pe, 0, range(3 * KD, 6 * KD), h_hi, h_lo)
                    pe.wait_ge(gate_step, 12)
                    gf = per_token(g_[:])
                    pe.matmul(bank[4][:, 0:32], const[:, C_TRI:C_TRI + P], gf, start=True, stop=True)
                    pe.matmul(bank[4][:, 32:64], const[:, C_SAME:C_SAME + P], gf, start=True, stop=True)
                    for i in range(2):
                        last = pe.matmul(bank[5][:, 32 * i:32 * i + 32],
                                         const[:, C_HALF + i:C_HALF + i + 1].to_broadcast([P, P]), gf,
                                         start=True, stop=True)
                    last.then_inc(gate_pe, 1)
                    project(pe, 0, range(6 * KD, 8 * KD), h_hi, h_lo)
                    pe.wait_ge(gate_step, 14)
                    for j in range(4):
                        sum_head(pe, 0, j)
                    pe.wait_ge(gate_act, 10)
                    spread_heads(pe, 0, hn_tok)

            temp.close()
            core_stack = ExitStack()
            core = [sb(core_stack, v, [P, 2, TT, P]) for v in
                    ("kbg", "k_end", "v_beta", "decay", "a_qk", "l_t", "inv_t")]
            for pair in range(PAIRS):
                gdn_pair(pair, h_hi, h_lo, g_, g_cum, beta, beta_eg, to_end, end_decay, state, v_new, sets, pre,
                         hn_tok, core)
            core_stack.close()
            st.close()

        def h_pair(name):
            st = ExitStack()
            return st, sb(st, "h_hi_" + name, [P, KD, SEQ], F32R), sb(st, "h_lo_" + name, [P, KD, SEQ], F32R)

        hs, h_hi, h_lo = h_pair("mlp0")
        mlp("mlp0", 0, N_FFN0, h_hi, h_lo, True)
        hs.close()
        ada_stack.close()

        hs, h_hi, h_lo = h_pair("gdn")
        gdn_o_stack = ExitStack()
        o_hi = sb(gdn_o_stack, "o_hi_gdn", [P, HEADS, SEQ], F32R, side="right")
        o_lo = sb(gdn_o_stack, "o_lo_gdn", [P, HEADS, SEQ], F32R, side="right")
        gdn(h_hi, h_lo)
        hs.close()
        out_projection("gdn_o", N_GWO, o_hi, o_lo, [[]] * 4, 2, EARLY_HEADS)
        gdn_o_stack.close()
        hs, h_hi, h_lo = h_pair("mlp1")
        mlp("mlp1", 1, N_FFN1, h_hi, h_lo, False)
        hs.close()
        with ExitStack() as st, nc.Block() as block:
            xr = [sb(st, f"xr{i}_last", [P, SEQ]) for i in range(2)]
            o_tok = sb(st, "o_tok", [P, TT, D])
            back, back_copied, stored = sem("back"), sem("back_copied"), sem("stored")
            out_bank = [bank[0], bank[1], bank[2], bank[3], bank[4], bank[5], bank[7], bank[0]]

            @block.tensor
            def _(pe):
                edge_pe(pe, 3, False)
                for k in range(KD):
                    pe.wait_ge(x_new, KD * 3 + k + 1)
                    for t in range(TT):
                        i = TT * (k // 4) + t
                        if i == 7 and k == 4:
                            pe.wait_ge(back_copied, 1)
                        last = pe.transpose(out_bank[i][:, P * (k % 4):P * (k % 4) + P], x[:, k, P * t:P * t + P], ident)
                        if k % 4 == 3:
                            last.then_inc(back, 1)

            @block.scalar
            def _(act):
                edge_act(act, 3, False, None, None, None)
                for i in range(2 * TT):
                    act.wait_ge(back, i + 1)
                    act.activation(o_tok[:, i % TT, 512 * (i // TT):512 * (i // TT) + 512], out_bank[i][:],
                                   ACT.Copy).then_inc(back_copied, 1)

            @block.vector
            def _(dve):
                edge_dve(dve, 3, (1, 5), False, None, xr, None, None)

            @block.sync
            def _(sp):
                for i in range(2 * TT):
                    t, cols = i % TT, slice(512 * (i // TT), 512 * (i // TT) + 512)
                    sp.wait_ge(back_copied, i + 1)
                    sp.dma_start(out[0, P * t:P * t + P, cols], o_tok[:, t, cols]).then_inc(stored, 16)
                sp.wait_ge(stored, 16 * 2 * TT)


_INS = ['x', 'c', 'positions', 'ada_w', 'ada_b', 'sandwich_g', 'mla_w_in', 'mla_q_norm_g', 'mla_kv_norm_g',
        'mla_w_uq', 'mla_w_ukv', 'mla_w_o', 'gdn_w_in', 'gdn_conv_w', 'gdn_a_log', 'gdn_dt_bias',
        'gdn_out_norm_g', 'gdn_w_o', 'ffn_w1', 'ffn_w2']


def make(nc, inputs):
    arrays, aps = {}, {}
    for name in _INS + ["const"]:
        v = constants() if name == "const" else np.ascontiguousarray(inputs[name])
        arrays[f"in_{name}"] = v
        aps[name] = nc.dram_tensor(f"in_{name}", v.shape, mybir.dt.from_np(v.dtype), kind="ExternalInput").ap()
    out = nc.dram_tensor("out_x", (1, SEQ, D), F32, kind="ExternalOutput").ap()
    build(nc, aps, out)
    return arrays


def kernel(**inputs):
    import concourse.bacc as bacc
    from concourse.bass_utils import run_bass_kernel_spmd

    nc = bacc.Bacc("TRN2", target_bir_lowering=False, num_devices=1)
    arrays = make(nc, inputs)
    r = run_bass_kernel_spmd(nc, [arrays], core_ids=[0])
    return r.results[0]["out_x"]
```
